# Optimizing a Trainium2 kernel written in Bass

```python
import math
import jax, jax.numpy as jnp
from jax import lax
import numpy as np

D_MODEL = 1024
BATCH = 1
SEQ = 256
DEPTH = 1
DEC_BATCH = 8
DEC_SEQ = 4
PAST_LEN = 256
PAGE_SIZE = 128

HEAD_DIM = 64
DSA_GROUPS = ((128, 1), (512, 4), (2048, 16))
DSA_HEADS = 4
DSA_BLOCK = 128
MOBA_HEADS = 4
MOBA_BLOCK = 256
MOBA_TOPK = 3
MOBA_Q_CHUNK = 64
ROT_DIM = HEAD_DIM // 4
ROPE_THETA = 500000.0
D_FF = -(-8 * D_MODEL // (3 * 256)) * 256
N_DSA_GROUPS = len(DSA_GROUPS)
DSA_WIDTH = N_DSA_GROUPS * DSA_HEADS * HEAD_DIM
DSA_OUT = DSA_HEADS * HEAD_DIM
MOBA_WIDTH = MOBA_HEADS * HEAD_DIM
W_IN_SPLITS = [DSA_WIDTH, 2 * DSA_WIDTH, 3 * DSA_WIDTH, 3 * DSA_WIDTH + MOBA_WIDTH,
               3 * DSA_WIDTH + 2 * MOBA_WIDTH, 3 * DSA_WIDTH + 3 * MOBA_WIDTH,
               3 * DSA_WIDTH + 3 * MOBA_WIDTH + D_MODEL]
W_IN_COLS = 3 * DSA_WIDTH + 3 * MOBA_WIDTH + 2 * D_MODEL
LN_EPS = 1e-5
ALPHA = (2 * DEPTH) ** 0.25
BETA = (8 * DEPTH) ** -0.25

kernel_name = "dilated_moba_gated_deepnorm_decoder_step"

def _rope(x, pos):
    inv = jnp.exp(-math.log(ROPE_THETA) * jnp.arange(0, ROT_DIM, 2, dtype=jnp.float32) / ROT_DIM)
    ang = pos.astype(jnp.float32)[:, None] * inv[None, :]
    cos, sin = jnp.cos(ang)[:, None, :], jnp.sin(ang)[:, None, :]
    xr = x[..., :ROT_DIM].astype(jnp.float32)
    x1, x2 = xr[..., :ROT_DIM // 2], xr[..., ROT_DIM // 2:]
    rot = jnp.concatenate([x1 * cos - x2 * sin, x2 * cos + x1 * sin], axis=-1).astype(x.dtype)
    return jnp.concatenate([rot, x[..., ROT_DIM:]], axis=-1)

def _layer_norm(x, g, b):
    xf = x.astype(jnp.float32)
    mu = xf.mean(-1, keepdims=True)
    var = jnp.square(xf - mu).mean(-1, keepdims=True)
    return ((xf - mu) * lax.rsqrt(var + LN_EPS)).astype(x.dtype) * g + b

def _softmax_lse(s):
    m = s.max(-1, keepdims=True)
    p = jnp.exp(s - m)
    den = p.sum(-1, keepdims=True)
    return p / den, (m + jnp.log(den))[..., 0]

def _dilated_prompt(q, k, v, dil, n_off):
    B, S, H, E = q.shape
    L = S // dil
    Lp = -(-L // DSA_BLOCK) * DSA_BLOCK
    nb = Lp // DSA_BLOCK

    def strided(x):
        x = x.reshape(B, L, dil, H, E).transpose(0, 2, 3, 1, 4)
        x = jnp.pad(x, ((0, 0), (0, 0), (0, 0), (0, Lp - L), (0, 0)))
        return x.reshape(B, dil, H, nb, DSA_BLOCK, E)

    def with_prev(x):
        prev = jnp.pad(x, ((0, 0), (0, 0), (0, 0), (1, 0), (0, 0), (0, 0)))[:, :, :, :-1]
        return jnp.concatenate([prev, x], axis=4)

    qb = strided(q)
    kk, vv = with_prev(strided(k)), with_prev(strided(v))
    s = jnp.einsum('bghnqe,bghnke->bghnqk', qb, kk).astype(jnp.float32) * (E ** -0.5)
    qi = jnp.arange(DSA_BLOCK)[:, None]
    kj = jnp.arange(2 * DSA_BLOCK)[None, :]
    off = DSA_BLOCK + qi - kj
    blk = jnp.arange(nb)[:, None, None]
    valid = (off >= 0) & (off <= n_off) & (blk * DSA_BLOCK + kj - DSA_BLOCK >= 0)
    p, lse = _softmax_lse(jnp.where(valid, s, -jnp.inf))
    o = jnp.einsum('bghnqk,bghnke->bghnqe', p.astype(v.dtype), vv)
    o = o.reshape(B, dil, H, Lp, E)[:, :, :, :L].transpose(0, 3, 1, 2, 4).reshape(B, S, H, E)
    lse = lse.reshape(B, dil, H, Lp)[:, :, :, :L].transpose(0, 3, 1, 2).reshape(B, S, H)
    return o, lse

def _dilated_sample(q, k, v, buf, dil, n_off):
    B, T, H, E = q.shape
    Lw = buf.shape[1]
    kv = jnp.concatenate([buf, jnp.stack([k, v], axis=2)], axis=1)
    idx = Lw + jnp.arange(T)[:, None] - dil * jnp.arange(n_off + 1)[None, :]
    ok = idx >= 0
    g = kv[:, jnp.maximum(idx, 0)]
    s = jnp.einsum('bthe,btjhe->bthj', q, g[:, :, :, 0]).astype(jnp.float32) * (E ** -0.5)
    p, lse = _softmax_lse(jnp.where(ok[None, :, None, :], s, -jnp.inf))
    o = jnp.einsum('bthj,btjhe->bthe', p.astype(v.dtype), g[:, :, :, 1])
    return o, lse, kv[:, T:]

def _merge_groups(outs, lses):
    w = jax.nn.softmax(jnp.stack(lses, axis=0), axis=0)
    o = jnp.einsum('gbsh,gbshe->bshe', w, jnp.stack(outs, axis=0).astype(jnp.float32))
    return o.astype(outs[0].dtype)

def _moba_blocks(k, v):
    B, L, H, E = k.shape
    Lp = -(-L // MOBA_BLOCK) * MOBA_BLOCK
    pad = ((0, 0), (0, Lp - L), (0, 0), (0, 0))
    to_blocks = lambda x: jnp.pad(x, pad).reshape(B, Lp // MOBA_BLOCK, MOBA_BLOCK, H, E).transpose(0, 3, 1, 2, 4)
    kblk, vblk = to_blocks(k), to_blocks(v)
    kmean = kblk.astype(jnp.float32).mean(axis=3).astype(k.dtype)
    return kblk, vblk, kmean

def _moba_core(q, q_pos, kblk, vblk, kmean):
    B, Q, H, E = q.shape
    NB = kblk.shape[2]
    topk = min(MOBA_TOPK, NB)
    scale = E ** -0.5
    qh = q.transpose(0, 2, 1, 3)
    own = q_pos // MOBA_BLOCK
    gate = jnp.einsum('bhqe,bhne->bhqn', qh, kmean).astype(jnp.float32)
    past = jnp.arange(NB)[None, :] < own[:, None]
    top_s, top_i = lax.top_k(jnp.where(past, gate, -jnp.inf), topk)
    sel_ok = jnp.isfinite(top_s)
    pick = jax.vmap(jax.vmap(lambda blocks, ix: blocks[ix]))
    k_sel, v_sel = pick(kblk, top_i), pick(vblk, top_i)
    k_own, v_own = jnp.take(kblk, own, axis=2), jnp.take(vblk, own, axis=2)
    s_sel = jnp.einsum('bhqe,bhqkle->bhqkl', qh, k_sel).astype(jnp.float32) * scale
    s_sel = jnp.where(sel_ok[..., None], s_sel, -jnp.inf).reshape(B, H, Q, topk * MOBA_BLOCK)
    key_pos = own[:, None] * MOBA_BLOCK + jnp.arange(MOBA_BLOCK)[None, :]
    s_own = jnp.einsum('bhqe,bhqle->bhql', qh, k_own).astype(jnp.float32) * scale
    s_own = jnp.where(key_pos <= q_pos[:, None], s_own, -jnp.inf)
    p = jax.nn.softmax(jnp.concatenate([s_sel, s_own], axis=-1), axis=-1).astype(vblk.dtype)
    p_sel = p[..., :topk * MOBA_BLOCK].reshape(B, H, Q, topk, MOBA_BLOCK)
    p_own = p[..., topk * MOBA_BLOCK:]
    o = (jnp.einsum('bhqkl,bhqkle->bhqe', p_sel, v_sel)
         + jnp.einsum('bhql,bhqle->bhqe', p_own, v_own))
    return o.transpose(0, 2, 1, 3)

def _moba_prompt(q, k, v, pos):
    B, S, H, E = q.shape
    kblk, vblk, kmean = _moba_blocks(k, v)
    n = S // MOBA_Q_CHUNK
    qc = q.reshape(B, n, MOBA_Q_CHUNK, H, E).transpose(1, 0, 2, 3, 4)
    pc = pos.reshape(n, MOBA_Q_CHUNK)
    o = lax.map(lambda a: _moba_core(a[0], a[1], kblk, vblk, kmean), (qc, pc))
    return o.transpose(1, 0, 2, 3, 4).reshape(B, S, H, E)

def _moba_sample(q, k, v, pool, page_table, pos):
    B, T, H, E = q.shape
    past = pool[page_table].reshape(B, page_table.shape[1] * pool.shape[1], 2, H, E)
    kv = jnp.concatenate([past, jnp.stack([k, v], axis=2)], axis=1)
    kblk, vblk, kmean = _moba_blocks(kv[:, :, 0], kv[:, :, 1])
    return _moba_core(q, pos, kblk, vblk, kmean)

def _prompt_mixer(qa, ka, va, qb, kb, vb, pos):
    S = qa.shape[1]
    outs, lses, new_state = [], [], []
    for g, (win, dil) in enumerate(DSA_GROUPS):
        hs = slice(g * DSA_HEADS, (g + 1) * DSA_HEADS)
        o, l = _dilated_prompt(qa[:, :, hs], ka[:, :, hs], va[:, :, hs], dil, win // dil)
        outs.append(o)
        lses.append(l)
        new_state.append(jnp.stack([ka[:, :, hs], va[:, :, hs]], axis=2)[:, S - min(win, S):])
    ob = _moba_prompt(qb, kb, vb, pos)
    new_state.append(jnp.stack([kb, vb], axis=2))
    return _merge_groups(outs, lses), ob, new_state

def _sample_mixer(qa, ka, va, qb, kb, vb, pos, bufs, pool, page_table):
    outs, lses, new_state = [], [], []
    for g, (win, dil) in enumerate(DSA_GROUPS):
        hs = slice(g * DSA_HEADS, (g + 1) * DSA_HEADS)
        o, l, nbuf = _dilated_sample(qa[:, :, hs], ka[:, :, hs], va[:, :, hs], bufs[g], dil, win // dil)
        outs.append(o)
        lses.append(l)
        new_state.append(nbuf)
    ob = _moba_sample(qb, kb, vb, pool, page_table, pos)
    new_state.append(jnp.stack([kb, vb], axis=2))
    return _merge_groups(outs, lses), ob, new_state

def _trunk_layer(x, c, pos, mixer, w_ada, b_ada, w_in, w_pa, w_pb, w_o,
                 ln1_g, ln1_b, w_up, w_down, ln2_g, ln2_b):
    B, S, _ = x.shape
    mod = (jax.nn.silu(c) @ w_ada + b_ada).reshape(B, 6, 1, D_MODEL)
    sh1, sc1, g1, sh2, sc2, g2 = [mod[:, i] for i in range(6)]
    h = x * (1 + sc1) + sh1
    qa, ka, va, qb, kb, vb, ga, gb = jnp.split(h @ w_in, W_IN_SPLITS, axis=-1)
    heads = lambda t: t.reshape(B, S, -1, HEAD_DIM)
    qa, ka, va = _rope(heads(qa), pos), _rope(heads(ka), pos), heads(va)
    qb, kb, vb = _rope(heads(qb), pos), _rope(heads(kb), pos), heads(vb)
    oa, ob, new_state = mixer(qa, ka, va, qb, kb, vb, pos)
    merged = (jax.nn.sigmoid(ga) * (oa.reshape(B, S, DSA_OUT) @ w_pa)
              + jax.nn.sigmoid(gb) * (ob.reshape(B, S, MOBA_WIDTH) @ w_pb))
    x = _layer_norm(ALPHA * x + g1 * (merged @ w_o), ln1_g, ln1_b)
    h2 = x * (1 + sc2) + sh2
    up, gt = jnp.split(h2 @ w_up, 2, axis=-1)
    f = (jax.nn.silu(gt) * up) @ w_down
    x = _layer_norm(ALPHA * x + g2 * f, ln2_g, ln2_b)
    return x, new_state

def setup_inputs(seed: int = 0) -> dict:
    key = jax.random.key(seed)
    ks = jax.random.split(key, 24)
    f32 = jnp.float32
    nrm = lambda k, shape, s: jax.random.normal(k, shape, f32) * s
    n_pages = PAST_LEN // PAGE_SIZE
    n_used = DEC_BATCH * n_pages
    n_phys = n_used + max(1, n_used // 4)
    page_table = jax.random.permutation(ks[0], n_phys)[:n_used].reshape(DEC_BATCH, n_pages).astype(jnp.int32)
    lw = [min(w, PAST_LEN) for w, _ in DSA_GROUPS]
    return {
        'x_prompt': nrm(ks[1], (BATCH, SEQ, D_MODEL), 1.0),
        'x_sample': nrm(ks[2], (DEC_BATCH, DEC_SEQ, D_MODEL), 1.0),
        'cache_kv_a0': nrm(ks[3], (DEPTH, DEC_BATCH, lw[0], 2, DSA_HEADS, HEAD_DIM), 1.0),
        'cache_kv_a1': nrm(ks[4], (DEPTH, DEC_BATCH, lw[1], 2, DSA_HEADS, HEAD_DIM), 1.0),
        'cache_kv_a2': nrm(ks[5], (DEPTH, DEC_BATCH, lw[2], 2, DSA_HEADS, HEAD_DIM), 1.0),
        'cache_kv_b': nrm(ks[6], (DEPTH, n_phys, PAGE_SIZE, 2, MOBA_HEADS, HEAD_DIM), 1.0),
        'page_table': page_table,
        'c_prompt': nrm(ks[7], (BATCH, D_MODEL), 1.0),
        'c_sample': nrm(ks[8], (DEC_BATCH, D_MODEL), 1.0),
        'w_ada': nrm(ks[9], (DEPTH, D_MODEL, 6 * D_MODEL), 0.5 * D_MODEL ** -0.5),
        'b_ada': nrm(ks[10], (DEPTH, 6 * D_MODEL), 0.02),
        'w_in': nrm(ks[11], (DEPTH, D_MODEL, W_IN_COLS), D_MODEL ** -0.5),
        'w_pa': nrm(ks[12], (DEPTH, DSA_OUT, D_MODEL), DSA_OUT ** -0.5),
        'w_pb': nrm(ks[13], (DEPTH, MOBA_WIDTH, D_MODEL), MOBA_WIDTH ** -0.5),
        'w_o': nrm(ks[14], (DEPTH, D_MODEL, D_MODEL), BETA * D_MODEL ** -0.5),
        'ln1_g': 1.0 + nrm(ks[15], (DEPTH, D_MODEL), 0.02),
        'ln1_b': nrm(ks[16], (DEPTH, D_MODEL), 0.02),
        'w_up': nrm(ks[17], (DEPTH, D_MODEL, 2 * D_FF), D_MODEL ** -0.5),
        'w_down': nrm(ks[18], (DEPTH, D_FF, D_MODEL), BETA * D_FF ** -0.5),
        'ln2_g': 1.0 + nrm(ks[19], (DEPTH, D_MODEL), 0.02),
        'ln2_b': nrm(ks[20], (DEPTH, D_MODEL), 0.02),
    }

def reference(x_prompt, x_sample, cache_kv_a0, cache_kv_a1, cache_kv_a2, cache_kv_b, page_table,
              c_prompt, c_sample, w_ada, b_ada, w_in, w_pa, w_pb, w_o, ln1_g, ln1_b,
              w_up, w_down, ln2_g, ln2_b):
    past_len = page_table.shape[1] * cache_kv_b.shape[2]
    pos_p = jnp.arange(x_prompt.shape[1], dtype=jnp.int32)
    pos_s = past_len + jnp.arange(x_sample.shape[1], dtype=jnp.int32)
    yp, ys = x_prompt, x_sample
    states_p, states_s = [], []
    for layer in range(DEPTH):
        lw = (w_ada[layer], b_ada[layer], w_in[layer], w_pa[layer], w_pb[layer], w_o[layer],
              ln1_g[layer], ln1_b[layer], w_up[layer], w_down[layer], ln2_g[layer], ln2_b[layer])
        yp, st_p = _trunk_layer(yp, c_prompt, pos_p, _prompt_mixer, *lw)
        bufs = (cache_kv_a0[layer], cache_kv_a1[layer], cache_kv_a2[layer])
        pool = cache_kv_b[layer]
        ys, st_s = _trunk_layer(
            ys, c_sample, pos_s,
            lambda qa, ka, va, qb, kb, vb, pos: _sample_mixer(qa, ka, va, qb, kb, vb, pos, bufs, pool, page_table),
            *lw)
        states_p.append(st_p)
        states_s.append(st_s)
    kv_a0_p, kv_a1_p, kv_a2_p, kv_b_p = [jnp.stack(s, axis=0) for s in zip(*states_p)]
    kv_a0_s, kv_a1_s, kv_a2_s, kv_b_s = [jnp.stack(s, axis=0) for s in zip(*states_s)]
    return (yp, ys, kv_a0_p, kv_a1_p, kv_a2_p, kv_b_p, kv_a0_s, kv_a1_s, kv_a2_s, kv_b_s)


_drawn_inputs = setup_inputs


def setup_inputs(seed=0):
    import zlib

    import numpy as np

    out = dict(_drawn_inputs(seed))
    spreads = {}
    factors = {'cache_kv_b': 6.395, 'ln1_g': 7.707, 'ln1_b': 7.771, 'ln2_g': 8.014, 'ln2_b': 8.339}
    for name, (base, spread) in spreads.items():
        noise = np.random.default_rng([zlib.crc32(name.encode()), seed]).standard_normal(out[name].shape)
        drawn = base * np.exp(spread * noise) if base else spread * noise
        out[name] = __import__('jax').numpy.asarray(drawn.astype(out[name].dtype))
    for name, factor in factors.items():
        out[name] = (out[name] * factor).astype(out[name].dtype)
    return out
```

```python
import math
from contextlib import ExitStack

import concourse.bass as bass
from concourse import mybir
from concourse.alu_op_type import AluOpType as ALU

F32 = mybir.dt.float32
F32R = mybir.dt.float32r
ACT = mybir.ActivationFunctionType

D = 1024
KT = D // 128
PROMPT = 256
DEC_B, DEC_T = 8, 4
SAMPLE = DEC_B * DEC_T
TOK = PROMPT + SAMPLE
PAST = 256
PAGE = 128
N_PAGES = PAST // PAGE
E = 64
ROT = E // 4
THETA = 500000.0
D_FF = -(-8 * D // (3 * 256)) * 256
FT = D_FF // 128
WIN = (128, 512, 2048)
DIL = (1, 4, 16)
BUF = tuple(min(w, PAST) for w in WIN)
ALPHA = 2.0 ** 0.25
EPS = 1e-5
SCALE = E ** -0.5
NEG = -1.0e30

RAW = 3
SPLIT = 4
N_ADA0 = 8
MIX0 = N_ADA0
GATE0 = MIX0 + 24
PAB0 = GATE0 + 8
WO0 = PAB0 + 2
ADA2 = WO0 + 4
UP0 = ADA2 + 4
DOWN0 = UP0 + 22
PAIRS = D_FF // 256


def ropetables():
    import numpy as np
    inv = np.exp(np.float32(-math.log(THETA)) * np.arange(0, ROT, 2, dtype=np.float32) / np.float32(ROT)).astype(np.float32)
    pos = np.concatenate([np.arange(PROMPT), np.tile(PAST + np.arange(DEC_T), DEC_B)]).astype(np.float32)
    ang = (pos[:, None] * inv[None, :]).astype(np.float32)
    cos, sin = np.cos(ang).astype(np.float32), np.sin(ang).astype(np.float32)
    c, s = np.ones((128, TOK), np.float32), np.zeros((128, TOK), np.float32)
    for base in (0, E):
        for j in range(ROT // 2):
            c[base + j] = c[base + j + ROT // 2] = cos[:, j]
            s[base + j] = -sin[:, j]
            s[base + j + ROT // 2] = sin[:, j]
    return c, s


def prompt_mask(tile, group):
    import numpy as np
    q = tile * 128 + np.arange(128)[:, None]
    k = np.arange((tile + 1) * 128)[None, :]
    off = q - k
    ok = off >= 0
    if group < 3:
        ok = ok & (off <= WIN[group]) & (off % DIL[group] == 0)
    return np.where(ok, 0.0, NEG).astype(np.float32)


def sample_mask():
    import numpy as np
    r = np.arange(128)
    b, t = r // 16, r % 4
    m = np.full((128, 832), NEG, np.float32)
    new_b, new_t = np.arange(SAMPLE) // DEC_T, np.arange(SAMPLE) % DEC_T

    def put(at, ok):
        m[:, at:at + ok.shape[1]] = np.where(ok, 0.0, NEG)
    put(0, np.arange(128)[None, :] >= t[:, None])
    put(160, np.arange(256)[None, :] % 4 == t[:, None])
    put(448, np.arange(64)[None, :] % 4 == t[:, None])
    put(544, np.ones((128, 256), bool))
    own = new_b[None, :] == b[:, None]
    put(128, own & (new_t[None, :] <= t[:, None]))
    put(416, own & (new_t[None, :] == t[:, None]))
    put(512, own & (new_t[None, :] == t[:, None]))
    put(800, own & (new_t[None, :] <= t[:, None]))
    return m


C_ID, C_ONE, C_COS, C_SIN = 0, 128, 256, 256 + TOK
C_MS = 256 + 2 * TOK
C_MA1 = C_MS + 832
C_MA0 = C_MA1 + 768
C_MB1 = C_MA0 + 384
C_MB0 = C_MB1 + 256
C_EPS = C_MB0 + 128
C_END = C_EPS + 1


def constants():
    import numpy as np
    c = np.zeros((128, C_END), np.float32)
    c[:, C_ID:C_ID + 128] = np.eye(128)
    c[:, C_ONE:C_ONE + 128] = 1.0 / D
    c[:, C_COS:C_COS + TOK], c[:, C_SIN:C_SIN + TOK] = ropetables()
    c[:, C_MS:C_MS + 832] = sample_mask()
    for g in range(3):
        c[:, C_MA1 + 256 * g:C_MA1 + 256 * (g + 1)] = prompt_mask(1, g)
        c[:, C_MA0 + 128 * g:C_MA0 + 128 * (g + 1)] = prompt_mask(0, g)
    c[:, C_MB1:C_MB1 + 256] = prompt_mask(1, 3)
    c[:, C_MB0:C_MB0 + 128] = prompt_mask(0, 3)
    c[:, C_EPS] = EPS
    return c


S_PIECES = [(0, 128), (160, 128), (288, 128), (448, 64), (544, 128), (672, 128), (128, 32), (416, 32), (512, 32), (800, 32)]
NEW_COL = [128, 416, 512, 800]
SWAP = [(i + ROT // 2) % ROT if i < ROT else i for i in range(32)]
KV_LOADS = 3 + N_PAGES
N_POOL_STORES = 3 + 16


def block_at(t, blk):
    if isinstance(blk, int):
        return t[:, blk, :]
    return t[:, bass.ds(blk, 1), :].rearrange("p a t -> p (a t)")


def o_sample_dst(t, h2):
    return t[E * h2:E * h2 + E, :, PROMPT:TOK].rearrange("p f (b t) -> p f b t", t=DEC_T)


def o_sample_src(psum, h2):
    v = psum[E * h2:E * h2 + E, 7, 0:256].rearrange("p (f b s t) -> p f b s t", f=4, s=2, t=DEC_T)
    return v[:, :, :, h2, :]


class Count:

    def __init__(self, sem):
        self.sem, self.n = sem, 0

    def up(self, ins):
        ins.then_inc(self.sem, 1)
        self.n = self.n + 1


def q_blk(g, hp):
    return 2 * g + hp if g < 3 else 18 + hp


def k_blk(g, hp):
    return 6 + 2 * g + hp if g < 3 else 20 + hp


def v_blk(g, hp):
    return 12 + 2 * g + hp if g < 3 else 22 + hp


def gate_slot(g):
    return 24 + g if g < 8 else ([12, 13, 14, 15, 16, 17, 22, 23])[g - 8]


UNITS = [(0, 1, h) for h in range(4)] + [(0, 0, h) for h in range(4)] + \
        [(1, 1, h) for h in range(4)] + [(1, 0, h) for h in range(4)]


def build(nc, x_prompt, x_sample, cache_a, cache_rows, cache_b, page_table, c_prompt, c_sample, w_ada, b_ada, w_in,
          w_pa, w_pb, w_o, ln1_g, ln1_b, w_up, w_down, ln2_g, ln2_b, const,
          y_prompt, y_sample, kv_prompt, kv_sample):
    ctx = ExitStack()
    base = nc.sbuf_base if isinstance(nc.sbuf_base, int) else 0
    at = [(base + 63) // 64 * 64]

    def sb(name, shape, dt=F32, offset=None):
        size = 4
        for n in shape[1:]:
            size *= n
        if offset is None:
            offset = at[0]
            at[0] += (size + 31) // 32 * 32
        return nc.alloc_sbuf_tensor_at(name, list(shape), dt, offset=offset), offset

    xT, _ = sb("xT", [128, KT, TOK])
    act_hi, _ = sb("act_hi", [128, KT, TOK], F32R)
    act_lo, _ = sb("act_lo", [128, KT, TOK], F32R)
    raw, _ = sb("raw", [128, RAW, 2048])
    w_hi, _ = sb("w_hi", [128, SPLIT, 1024], F32R)
    w_lo, _ = sb("w_lo", [128, SPLIT, 1024], F32R)
    cst, _ = sb("cst", [128, C_END])
    qkvg, o_qkvg = sb("qkvg", [128, 32, TOK])
    kvin, _ = sb("kvin", [128, 2, 6, 256])
    kT, o_kT = sb("kT", [128, 2, 832])
    qz, o_qz = sb("qz", [128, 4, 2, 4, 48])
    tok, o_tok = sb("tok", [128, 3, 2, 1024])
    tmp, o_tmp = sb("tmp", [128, 3840])
    o_tokens, _ = sb("o_tokens", [128, 2, 2, 256])
    mod, _ = sb("mod", [128, 48, 9])
    rowbuf, _ = sb("rowbuf", [18, 3, 256])
    c_hl, _ = sb("c_hl", [128, KT, 18], F32R)
    small, _ = sb("small", [128, 128])
    rows, _ = sb("rows", [64, 128])
    pages, _ = sb("pages", [1, DEC_B * N_PAGES], mybir.dt.int32)

    x_tok, _ = sb("x_tok", [128, 3, D], F32, o_tok)
    s_msk, _ = sb("s_msk", [128, 832], F32, o_tmp)
    s_prb, _ = sb("s_prb", [128, 832], F32, o_tmp + 832 * 4)
    s_prbT, _ = sb("s_prbT", [128, 10, 128], F32, o_qz)
    msk, _ = sb("msk", [128, 768], F32, o_tmp)
    prb, _ = sb("prb", [128, 2, 768], F32, o_tmp + 768 * 4)
    prbT, _ = sb("prbT", [128, 2, 768], F32, o_tmp + 3 * 768 * 4)
    oT_hi, _ = sb("oT_hi", [128, 4, TOK], F32R, o_kT)
    oT_lo, _ = sb("oT_lo", [128, 4, TOK], F32R, o_kT + 4 * TOK * 4)
    assert o_qz + 6144 >= o_kT + 8 * TOK * 4
    f_hi, _ = sb("f_hi", [128, FT, TOK], F32R, o_qkvg)
    f_lo, _ = sb("f_lo", [128, FT, TOK], F32R, o_qkvg + FT * TOK * 4)
    assert o_qkvg + 2 * FT * TOK * 4 <= o_tok
    ln_rows, _ = sb("ln_rows", [128, 2, D], F32, o_tok)
    y_tok, _ = sb("y_tok", [128, 3, D], F32, o_tok + 2 * D * 4)
    silu_t, _ = sb("silu_t", [128, 2, TOK], F32, o_tmp)
    f_t, _ = sb("f_t", [128, 2, TOK], F32, o_tmp + 2 * TOK * 4)
    rstd, _ = sb("rstd", [128, TOK], F32, o_tmp + 4 * TOK * 4)
    h_t, _ = sb("h_t", [128, 2, TOK], F32, o_tmp + 5 * TOK * 4)
    rope_t, _ = sb("rope_t", [128, 2, TOK], F32, o_tmp)
    ctok, _ = sb("ctok", [9, D], F32, o_tmp)
    c_t, _ = sb("c_t", [128, KT, 9], F32, o_tmp + 8 * TOK * 4)

    lnp, _ = sb("lnp", [128, 64])
    st6, _ = sb("st6", [128, 3, 2, 6])
    ident = cst[:, C_ID:C_ID + 128]
    ones = cst[:, C_ONE:C_ONE + 128]

    assert at[0] <= nc.sbuf_usable_end
    psum = nc.alloc_psum_tensor("psum", [128, 8, 512], F32)

    def sem(name):
        return nc.alloc_semaphore(name)

    const_in, x_in, c_in, rows_in, pages_in = sem("const_in"), sem("x_in"), sem("c_in"), sem("rows_in"), sem("pages_in")
    ln_rows_in = sem("ln_rows_in")
    raw_in = [sem(f"raw_in{i}") for i in range(RAW)]
    kv_in = [sem(f"kv_in{i}") for i in range(2)]
    stored, y_stored = sem("stored"), sem("y_stored")
    hi_ready, lo_ready, half_used = sem("hi_ready"), sem("lo_ready"), sem("half_used")
    acc_free = [sem("acc_free0"), sem("acc_free1")]
    turned_c, turned_rows, turned_x = sem("turned_c"), sem("turned_rows"), sem("turned_x")
    c_silu, c_hi, c_ready = sem("c_silu"), sem("c_hi"), sem("c_ready")
    x_ready_act, x_ready_dve = sem("x_ready_act"), sem("x_ready_dve")
    rows_ready = sem("rows_ready")
    ada_done, ada_row, ada_turned, ada_mod = sem("ada_done"), sem("ada_row"), sem("ada_turned"), sem("ada_mod")
    h_ready, h_hi, h_lo = sem("h_ready"), sem("h_hi"), sem("h_lo")
    evicted, cos_done, roped = sem("evicted"), sem("cos_done"), sem("roped")
    x_scaled = sem("x_scaled")
    qz_zero, qz_ready = sem("qz_zero"), sem("qz_ready")
    tok_turned, v_tok, k_tok = sem("tok_turned"), sem("v_tok"), sem("k_tok")
    kt_turned, kt_x, kt_y, scored_s = sem("kt_turned"), sem("kt_x"), sem("kt_y"), sem("scored_s")
    max_s, exp_s, prob_s = sem("max_s"), sem("exp_s"), sem("prob_s")
    probT_turned, probT_s, pv_s = sem("probT_turned"), sem("probT_s"), sem("pv_s")
    scored, maxed, exped, turned, prbT_a, prbT_b, pv_done, o_ready = (sem(n) for n in (
        "scored", "maxed", "exped", "turned", "prbT_a", "prbT_b", "pv_done", "o_ready"))
    oT_turned, oT_h, oT_l = sem("oT_turned"), sem("oT_h"), sem("oT_l")
    gates_in, sig_ready = sem("gates_in"), sem("sig_ready")
    pab_done, merged, merged_hi, merged_lo = sem("pab_done"), sem("merged"), sem("merged_hi"), sem("merged_lo")
    z_ready, mean_done, centred, squared, var_done, std_ready = (sem(n) for n in (
        "z_ready", "mean_done", "centred", "squared", "var_done", "std_ready"))
    normed, x1_ready, h2_ready, h2_hi, h2_lo, x1_scaled = (sem(n) for n in (
        "normed", "x1_ready", "h2_ready", "h2_hi", "h2_lo", "x1_scaled"))
    silu_ready, f_ready, f_hi_ready, f_lo_ready = sem("silu_ready"), sem("f_ready"), sem("f_hi_ready"), sem("f_lo_ready")
    down_done, z2_ready, z2_turned = sem("down_done"), sem("z2_ready"), sem("z2_turned")
    var2, std2, rs2, y_norm, y_done = sem("var2"), sem("std2"), sem("rs2"), sem("y_norm"), sem("y_done")
    dve_link = Count(sem("dve_link"))
    sp_past, pe_past, dve_past = sem("sp_past"), sem("pe_past"), sem("dve_past")

    def halves_of(n):
        if isinstance(n, int) and n >= DOWN0:
            c = n - DOWN0
            return 2 * DOWN0 + 11 * (c // 6) + 2 * (c % 6)
        return 2 * n

    def raw_need(n, slot):
        extra = sum(1 for m in (PAB0, PAB0 + 1) if m % RAW == slot and n >= m)
        return 16 * (n // RAW + 1 + extra)

    MIX_TRIPS = 4
    UP_PAIRS = 3
    UP_TRIPS = PAIRS // UP_PAIRS

    w_in_v = w_in.rearrange("(k p) n -> p k n", p=128)
    w_ada_v = w_ada.rearrange("(k p) n -> p k n", p=128)
    w_o_v = w_o.rearrange("(k p) n -> p k n", p=128)
    w_up_v = w_up.rearrange("(k p) n -> p k n", p=128)
    w_pa_v = w_pa.rearrange("(k p) n -> p k n", p=128)
    w_pb_v = w_pb.rearrange("(k p) n -> p k n", p=128)
    w_down_v = w_down.rearrange("(k p) n -> p k n", p=128)

    def raw8(slot):
        return raw[:, slot, :].rearrange("p (k n) -> p k n", k=8)

    def raw_half(n_static_slot, hh, by_rows):
        if by_rows:
            return raw[:, n_static_slot, 1024 * hh:1024 * hh + 1024]
        return raw8(n_static_slot)[:, :, 128 * hh:128 * hh + 128]

    def part(t, slot, by_rows):
        if by_rows:
            return t[:, slot, :]
        return t[:, slot, :].rearrange("p (k n) -> p k n", k=8)

    def split_hi(act, nb, slot4, rslot, hh, need, by_rows=False):
        act.wait_ge(raw_in[rslot], need)
        if not isinstance(nb, int) or nb >= SPLIT:
            act.wait_ge(half_used, nb - SPLIT + 1)
        nc.scalar.activation(part(w_hi, slot4, by_rows), raw_half(rslot, hh, by_rows), ACT.Copy).then_inc(hi_ready, 1)

    def split_lo(dve, nb, slot4, rslot, hh, by_rows=False):
        dve.wait_ge(hi_ready, nb + 1)
        nc.vector.tensor_tensor(part(w_lo, slot4, by_rows), raw_half(rslot, hh, by_rows),
                                part(w_hi, slot4, by_rows).bitcast(F32), ALU.subtract).then_inc(lo_ready, 1)

    def halves(first, last):
        out = []
        for n in range(first, last):
            by_rows = PAB0 <= n < WO0 or n >= DOWN0
            for hh in range(1 if n >= DOWN0 and (n - DOWN0) % 6 == 5 else 2):
                nb = halves_of(n) + hh
                out.append((nb, nb % SPLIT, n % RAW, hh, by_rows, raw_need(n, n % RAW)))
        return out

    ALL = {h[0]: h for h in halves(0, DOWN0 + 12)}
    LAST = max(ALL)

    def hi_static(act, nb):
        if nb in ALL:
            _, s, r, hh, by, need = ALL[nb]
            split_hi(act, nb, s, r, hh, need, by)

    def lo_static(dve, nb):
        if nb in ALL:
            _, s, r, hh, by, need = ALL[nb]
            split_lo(dve, nb, s, r, hh, by)

    AHEAD = SPLIT

    block = ctx.enter_context(nc.Block())

    @block.sync
    def _(sp):
        sp.dma_start(cst[:], const).then_inc(const_in, 16)
        sp.dma_start(ctok[0:1, :], c_prompt).then_inc(c_in, 16)
        sp.dma_start(ctok[1:9, :], c_sample).then_inc(c_in, 16)
        sp.dma_start(rows[0:48, :], b_ada.rearrange("a (j p) -> (a j) p", p=128)).then_inc(rows_in, 16)
        sp.dma_start(rows[48:56, :], ln1_g.rearrange("a (j p) -> (a j) p", p=128)).then_inc(rows_in, 16)
        sp.dma_start(rows[56:64, :], ln1_b.rearrange("a (j p) -> (a j) p", p=128)).then_inc(rows_in, 16)

        def load(n, slot, src, dst, first_use):
            if not first_use:
                sp.wait_ge(lo_ready, halves_of(n - RAW + 1))
            sp.dma_start(dst, src).then_inc(raw_in[slot], 16)

        for n in range(MIX0):
            load(n, n % RAW, w_ada_v[:, :, 256 * n:256 * n + 256], raw8(n % RAW), n < RAW)
            if n == 1:
                sp.dma_start(x_tok[:, 0:2, :], x_prompt.rearrange("a (t p) d -> p (a t) d", p=128)).then_inc(x_in, 16)
                sp.dma_start(x_tok[0:SAMPLE, 2, :], x_sample.rearrange("b t d -> (b t) d")).then_inc(x_in, 16)

        with sp.Fori(0, MIX_TRIPS) as i:
            for k in range(6):
                col = sp.snap((i * 3 + (k // 2 if k % 2 == 0 else N_ADA0 + k // 2)) * 256)
                sp.wait_ge(lo_ready, i * 12 + 2 * (MIX0 + k - RAW + 1))
                sp.sem_inc(sp_past, 1)
                src = (w_in_v if k % 2 == 0 else w_ada_v)[:, :, bass.ds(col, 256)]
                sp.dma_start(raw8((MIX0 + k) % RAW), src).then_inc(raw_in[(MIX0 + k) % RAW], 16)
        for n in range(GATE0, PAB0):
            col = 3072 + 256 * (n - GATE0)
            load(n, n % RAW, w_in_v[:, :, col:col + 256], raw8(n % RAW), False)
        for n in range(PAB0, WO0):
            j = n - PAB0
            dst = raw[:, n % RAW, :].rearrange("p (k n) -> p k n", k=4)
            load(n, n % RAW, w_pa_v[:, :, 512 * j:512 * j + 512], dst[:, 0:2, :], False)
            sp.dma_start(dst[:, 2:4, :], w_pb_v[:, :, 512 * j:512 * j + 512]).then_inc(raw_in[n % RAW], 16)
        for n in range(WO0, ADA2):
            j = n - WO0
            load(n, n % RAW, w_o_v[:, :, 256 * j:256 * j + 256], raw8(n % RAW), False)
        for n in range(ADA2, UP0):
            j = 20 + n - ADA2
            load(n, n % RAW, w_ada_v[:, :, 256 * j:256 * j + 256], raw8(n % RAW), False)
        with sp.Fori(0, UP_TRIPS) as i:
            for k in range(6):
                n = UP0 + k
                col = sp.snap((i * 3 + k // 2) * 256 + (D_FF if k % 2 == 0 else 0))
                sp.wait_ge(lo_ready, i * 12 + 2 * (n - RAW + 1))
                sp.sem_inc(sp_past, 1)
                sp.dma_start(raw8(n % RAW), w_up_v[:, :, bass.ds(col, 256)]).then_inc(raw_in[n % RAW], 16)
        for n in range(UP0 + 6 * UP_TRIPS, DOWN0):
            k = n - UP0
            col = (k // 2) * 256 + (D_FF if k % 2 == 0 else 0)
            load(n, n % RAW, w_up_v[:, :, col:col + 256], raw8(n % RAW), False)
        for n in range(DOWN0, DOWN0 + 12):
            c, hcol = (n - DOWN0) % 6, (n - DOWN0) // 6
            nk = min(4, FT - 4 * c)
            dst = raw[:, n % RAW, 0:512 * nk].rearrange("p (k n) -> p k n", k=nk)
            load(n, n % RAW, w_down_v[:, 4 * c:4 * c + nk, 512 * hcol:512 * hcol + 512], dst, False)
        for t in range(3):
            rows_n = 128 if t < 2 else SAMPLE
            sp.wait_ge(y_done, t + 1)
            dst = y_prompt[0, 128 * t:128 * t + 128, :] if t < 2 else y_sample.rearrange("b t d -> (b t) d")
            sp.dma_start(dst, y_tok[0:rows_n, t, :]).then_inc(y_stored, 16)
        sp.wait_ge(y_stored, 16 * 3)
        sp.wait_ge(stored, 16 * N_POOL_STORES)

    def mm3(out, hi_l, lo_l, hi_r, lo_r, start, stop):
        nc.tensor.matmul(out, hi_l, hi_r, start=start, stop=False, skip_group_check=True)
        nc.tensor.matmul(out, hi_l, lo_r, start=False, stop=False, skip_group_check=True)
        return nc.tensor.matmul(out, lo_l, hi_r, start=False, stop=stop, skip_group_check=True)

    def unit_mm(pe, nb, slot, bank, rhs_ready=None):
        pe.wait_ge(lo_ready, nb + 1)
        wh, wl = part(w_hi, slot, False), part(w_lo, slot, False)
        for k in range(KT):
            if rhs_ready is not None:
                pe.wait_ge(rhs_ready, k + 1)
            mm = mm3(psum[:, bank, 0:TOK], wh[:, k, :], wl[:, k, :], act_hi[:, k, :], act_lo[:, k, :], k == 0, k == KT - 1)
        mm.then_inc(half_used, 1)

    def ada_mm(pe, nb, slot, bank, hh):
        pe.wait_ge(lo_ready, nb + 1)
        wh, wl = part(w_hi, slot, False), part(w_lo, slot, False)
        out = psum[0:18, bank, 128 * hh:128 * hh + 128]
        for k in range(KT):
            nc.tensor.matmul(out, c_hl[:, k, :], wh[:, k, :], start=(k == 0), stop=False, skip_group_check=True)
            mm = nc.tensor.matmul(out, c_hl[:, k, :], wl[:, k, :], start=False, stop=(k == KT - 1), skip_group_check=True)
        mm.then_inc(half_used, 1)

    def ada_turn(pe, a, bank, slot):
        pe.wait_ge(ada_row, a + 1)
        pe.sem_inc(pe_past, 1)
        for hh in range(2):
            mm = nc.tensor.transpose(psum[:, bank, 256 + 18 * hh:256 + 18 * hh + 18],
                                     rowbuf[:, slot, 128 * hh:128 * hh + 128], cst[0:18, 0:18])
        mm.then_inc(ada_turned, 1)

    def kv_pieces():
        return [(0, 128, 0), (1, 128, 160), (2, 128, 288), (5, 64, 448), (3, 128, 544), (4, 128, 672)]

    @block.tensor
    def _(pe):
        pe.wait_ge(const_in, 16)
        pe.wait_ge(c_in, 32)
        for k in range(KT):
            mm = nc.tensor.transpose(psum[:, 0, 9 * k:9 * k + 9], ctok[:, 128 * k:128 * k + 128], cst[0:9, 0:9])
        mm.then_inc(turned_c, 1)
        pe.wait_ge(rows_in, 48)
        nc.tensor.transpose(psum[:, 1, 0:64], rows[:, :], cst[0:64, 0:64]).then_inc(turned_rows, 1)
        pe.wait_ge(x_in, 32)
        for t in range(2):
            for k in range(KT):
                mm = nc.tensor.transpose(psum[:, 2 + t if k < 4 else 4 + t, 128 * (k % 4):128 * (k % 4) + 128],
                                         x_tok[:, t, 128 * k:128 * k + 128], ident)
                if k % 4 == 3:
                    mm.then_inc(turned_x, 1)
        for k in range(KT):
            mm = nc.tensor.transpose(psum[:, 6, SAMPLE * k:SAMPLE * k + SAMPLE],
                                     x_tok[0:SAMPLE, 2, 128 * k:128 * k + 128], cst[0:SAMPLE, 0:SAMPLE])
        mm.then_inc(turned_x, 1)

        pe.wait_ge(c_ready, 1)
        pe.wait_ge(x_ready_act, 2)
        pe.wait_ge(x_ready_dve, 3)
        for a in range(N_ADA0):
            if a >= 3:
                pe.wait_ge(ada_mod, a - 2)
            for hh in range(2):
                ada_mm(pe, 2 * a + hh, (2 * a + hh) % SPLIT, 5 + a % 3, hh)
            if a >= 1:
                ada_turn(pe, a - 1, 5 + (a - 1) % 3, (a - 1) % 3)
        ada_turn(pe, N_ADA0 - 1, 5 + (N_ADA0 - 1) % 3, (N_ADA0 - 1) % 3)

        def mix(i, first=False):
            for k in range(6):
                nb0 = i * 12 + 2 * (MIX0 + k)
                for hh in range(2):
                    slot = (2 * k + hh) % SPLIT
                    if k % 2 == 0:
                        u = i * 6 + (k + hh)
                        if not (first and k == 0):
                            pe.wait_ge(acc_free[hh], i * 3 + k // 2)
                        unit_mm(pe, nb0 + hh, slot, hh, h_lo if first and k == 0 and hh == 0 else None)
                    else:
                        a = i * 3 + (N_ADA0 + k // 2)
                        bank = (N_ADA0 + k // 2) % 3
                        if hh == 0:
                            pe.wait_ge(ada_mod, a - 2)
                        ada_mm(pe, nb0 + hh, slot, 5 + bank, hh)
                if k % 2 == 0 and k >= 2:
                    ada_turn(pe, i * 3 + (N_ADA0 + k // 2 - 1), 5 + (N_ADA0 + k // 2 - 1) % 3, (N_ADA0 + k // 2 - 1) % 3)
            ada_turn(pe, i * 3 + (N_ADA0 + 2), 5 + (N_ADA0 + 2) % 3, (N_ADA0 + 2) % 3)

        mix(0, True)
        with pe.Fori(1, MIX_TRIPS) as i:
            mix(i)

        pe.wait_ge(ada_mod, N_ADA0 + 12)
        for j in range(8):
            g, hp = j // 2, j % 2
            for kind in range(2):
                bank = 2 + (j % 2) * 2 + kind
                if kind == 0:
                    pe.wait_ge(acc_free[hp], v_blk(g, hp) // 2 + 1)
                    if j >= 2:
                        pe.wait_ge(v_tok, j - 1)
                else:
                    pe.wait_ge(roped, k_blk(g, hp) + 1 if g < 3 else 15 + hp)
                    if j >= 2:
                        pe.wait_ge(k_tok, j - 1)
                blk = (v_blk if kind == 0 else k_blk)(g, hp)
                for t in range(2):
                    nc.tensor.transpose(psum[:, bank, 128 * t:128 * t + 128], qkvg[:, blk, 128 * t:128 * t + 128], ident)
                nc.tensor.transpose(psum[0:SAMPLE, bank, 256:384], qkvg[:, blk, PROMPT:TOK], ident).then_inc(tok_turned, 1)

        pe.wait_ge(v_tok, 8)
        pe.wait_ge(k_tok, 8)
        pe.wait_ge(qz_ready, 1)

        def keys_turn(idx):
            b, hp = idx // 2, idx % 2
            if hp == 0:
                pe.wait_ge(kv_in[b % 2], 16 * KV_LOADS * (b // 2 + 1))
            if idx >= 2:
                pe.wait_ge(kt_x, idx - 1)
                pe.wait_ge(kt_y, idx - 1)
            for n, (tile, nr, _) in enumerate(kv_pieces()):
                bank = 4 + 2 * hp + (n >= 3)
                col = 128 * n if n < 3 else (0, 64, 192)[n - 3]
                mm = nc.tensor.transpose(psum[:, bank, col:col + nr], kvin[0:nr, b % 2, tile, 128 * hp:128 * hp + 128],
                                         cst[0:nr, 0:nr])
            mm.then_inc(kt_turned, 1)

        def sample_scores(idx):
            b, hp = idx // 2, idx % 2
            pe.wait_ge(kt_x, idx + 1)
            pe.wait_ge(kt_y, idx + 1)
            r0 = 32 * (b // 2)
            for g, (c0, n, bank, o0) in enumerate(((0, 160, 2, 0), (160, 288, 2, 160), (448, 96, 3, 0), (544, 288, 3, 96))):
                w = qz[:, g, hp, b // 2, 16 * (b % 2):16 * (b % 2) + 32]
                mm = nc.tensor.matmul(psum[r0:r0 + 32, bank, o0:o0 + n], w, kT[:, hp, c0:c0 + n],
                                      start=(b % 2 == 0 and hp == 0 and g in (0, 2)), stop=(b % 2 == 1 and hp == 1),
                                      skip_group_check=True)
            mm.then_inc(scored_s, 1)

        for idx in range(2 * DEC_B + 1):
            if idx < 2 * DEC_B:
                keys_turn(idx)
            if idx >= 1:
                sample_scores(idx - 1)

        def sample_probs_turn():
            pe.wait_ge(prob_s, 2)
            for n, (c0, nc_) in enumerate(S_PIECES):
                mm = nc.tensor.transpose(psum[0:nc_, 4 + n // 4, 128 * (n % 4):128 * (n % 4) + 128],
                                         s_prb[:, c0:c0 + nc_], ident)
                if n in (3, 7, 9):
                    mm.then_inc(probT_turned, 1)

        def sample_values(b):
            if b == 0:
                pe.wait_ge(probT_s, 2)
                for g in range(4):
                    for hp in range(2):
                        rhs = s_prbT[0:SAMPLE, 6 + g, :].rearrange("p (b x) -> p b x", x=16)[:, :, 8 * hp:8 * hp + 8]
                        o0 = 128 * (g // 3) + 64 * hp
                        nc.tensor.matmul(psum[:, 7, o0:o0 + 64], tok[0:SAMPLE, 2, 1, 256 * g + 128 * hp:256 * g + 128 * hp + 128],
                                         rhs, start=(g == 0 and hp == 0), stop=False, skip_group_check=True)
            pe.wait_ge(kv_in[b % 2], 16 * KV_LOADS * (4 + b // 2 + 1))
            for hp in range(2):
                for n, (tile, nr, br) in enumerate(((0, 128, 0), (1, 128, 0), (2, 128, 0), (5, 64, 0), (3, 128, 1), (4, 128, 1))):
                    o0 = 128 * br + 64 * hp + 8 * b
                    mm = nc.tensor.matmul(psum[:, 7, o0:o0 + 8], kvin[0:nr, b % 2, tile, 128 * hp:128 * hp + 128],
                                          s_prbT[0:nr, n, 16 * b + 8 * hp:16 * b + 8 * hp + 8],
                                          start=False, stop=(b == DEC_B - 1), skip_group_check=True)
            mm.then_inc(pv_s, 1)

        def prompt_scores(u):
            br, t, h = UNITS[u]
            if u >= 1:
                pe.wait_ge(maxed, u)
            nk = 128 * (t + 1)
            p0 = E * (h % 2)
            for j, g in enumerate((0, 1, 2) if br == 0 else (3,)):
                c0 = j * nk
                mm = nc.tensor.matmul(psum[:, 2 + c0 // 512, c0 % 512:c0 % 512 + nk],
                                      qkvg[p0:p0 + E, q_blk(g, h // 2), 128 * t:128 * t + 128],
                                      qkvg[p0:p0 + E, k_blk(g, h // 2), 0:nk], start=True, stop=True,
                                      skip_group_check=True)
            mm.then_inc(scored, 1)

        def prompt_turn(u):
            br, t, h = UNITS[u]
            pe.wait_ge(exped, u + 1)
            if u == 0:
                pe.wait_ge(probT_s, 2)
            else:
                pe.wait_ge(prbT_a, u)
                pe.wait_ge(prbT_b, min(u, 4))
            nb_ = (3 if br == 0 else 1) * (t + 1)
            for n in range(nb_):
                mm = nc.tensor.transpose(psum[:, 4 + n // 4, 128 * (n % 4):128 * (n % 4) + 128],
                                         prb[:, u % 2, 128 * n:128 * n + 128], ident)
            mm.then_inc(turned, 1)

        def prompt_values(u):
            br, t, h = UNITS[u]
            pe.wait_ge(prbT_a, u + 1)
            pe.wait_ge(prbT_b, min(u + 1, 4))
            if u >= 1:
                pe.wait_ge(o_ready, u)
            nkb = t + 1
            steps = [(j, g, kb) for j, g in enumerate((0, 1, 2) if br == 0 else (3,)) for kb in range(nkb)]
            for n, (j, g, kb) in enumerate(steps):
                mm = nc.tensor.matmul(psum[:, 6, 0:E], prbT[:, u % 2, 128 * (j * nkb + kb):128 * (j * nkb + kb) + 128],
                                      tok[:, kb, 1, 256 * g + E * h:256 * g + E * h + E],
                                      start=(n == 0), stop=(n == len(steps) - 1))
            mm.then_inc(pv_done, 1)

        for s in range(20):
            if s < 16:
                u = 24 + s
                pe.wait_ge(acc_free[s % 2], u // 2)
                unit_mm(pe, 2 * GATE0 + s, s % SPLIT, s % 2)
            if s == 2:
                sample_probs_turn()
            if 2 <= s < 18:
                prompt_scores(s - 2)
            if 3 <= s < 19:
                prompt_turn(s - 3)
            if s >= 4:
                prompt_values(s - 4)
            if 6 <= s < 14:
                sample_values(s - 6)

        pe.wait_ge(o_ready, 16)
        for t in range(2):
            for f in range(4):
                mm = nc.tensor.transpose(psum[:, 2 + t, 128 * f:128 * f + 128],
                                         o_tokens[:, t, f // 2, 128 * (f % 2):128 * (f % 2) + 128], ident)
            mm.then_inc(oT_turned, 1)
        pe.wait_ge(oT_l, 4)

        for h in range(4):
            nb = 2 * PAB0 + h
            pe.wait_ge(lo_ready, nb + 1)
            wh, wl = w_hi[:, nb % SPLIT, :], w_lo[:, nb % SPLIT, :]
            for m in range(4):
                u = 40 + 4 * h + m
                pe.wait_ge(acc_free[u % 2], u // 2)
                for k in range(2):
                    c = 512 * k + 128 * m
                    mm = mm3(psum[:, u % 2, 0:TOK], wh[:, c:c + 128], wl[:, c:c + 128],
                             oT_hi[:, 2 * (h % 2) + k, :], oT_lo[:, 2 * (h % 2) + k, :], k == 0, k == 1)
                mm.then_inc(half_used if m == 3 else pab_done, 1)

        def mean(m):
            pe.wait_ge(z_ready, m + 1)
            mm = nc.tensor.matmul(psum[:, 2, 0:TOK], ones, xT[:, m, :], start=(m == 0), stop=(m == KT - 1))
            mm.then_inc(mean_done, 1)

        for m in range(KT):
            u = 56 + m
            if m < 2:
                pe.wait_ge(acc_free[u % 2], u // 2)
            else:
                pe.wait_ge(z_ready, m - 1)
            unit_mm(pe, 2 * WO0 + m, (2 * WO0 + m) % SPLIT, u % 2, merged_lo if m == 0 else None)
            if m >= 1:
                mean(m - 1)
        mean(KT - 1)
        for j in range(4):
            a = 20 + j
            for hh in range(2):
                nb = 2 * (ADA2 + j) + hh
                if hh == 0 and j == 3:
                    pe.wait_ge(ada_mod, a - 2)
                ada_mm(pe, nb, nb % SPLIT, 5 + a % 3, hh)
            if j >= 1:
                ada_turn(pe, a - 1, 5 + (a - 1) % 3, (a - 1) % 3)
            if j == 1:
                for m in range(KT):
                    if m % 4 == 0:
                        pe.wait_ge(squared, m // 4 + 1)
                    mm = nc.tensor.matmul(psum[:, 3, 0:TOK], ones, qkvg[:, 8 + m, :], start=(m == 0), stop=(m == KT - 1))
                mm.then_inc(var_done, 1)
        ada_turn(pe, 23, 5 + 23 % 3, 23 % 3)

        def up_pair(j, first=False):
            for q in range(4):
                nb = j * 4 + (2 * UP0 + q)
                if q < 2 and first:
                    pe.wait_ge(z_ready, KT)
                elif q < 2:
                    pe.wait_ge(f_ready, j * 2 + (q - 1))
                else:
                    pe.wait_ge(silu_ready, j * 2 + (q - 1))
                unit_mm(pe, nb, q, q % 2, h2_lo if first and q == 0 else None)

        up_pair(0, True)
        up_pair(1)
        up_pair(2)
        with pe.Fori(1, UP_TRIPS) as i:
            for k in range(UP_PAIRS):
                up_pair(i * 3 + k)
        for j in range(UP_PAIRS * UP_TRIPS, PAIRS):
            up_pair(j)

        def z2_turn(m):
            pe.wait_ge(z2_ready, 4 * (m // 4 + 1))
            for t in range(3):
                nt = 128 if t < 2 else SAMPLE
                mm = nc.tensor.transpose(psum[0:nt, t + 3 * (m // 4), 128 * (m % 4):128 * (m % 4) + 128],
                                         xT[:, m, 128 * t:128 * t + nt], ident)
            mm.then_inc(z2_turned, 1)

        for hcol in range(2):
            for kk in range(0, FT, 2):
                nb = 2 * DOWN0 + 11 * hcol + kk // 2
                pe.wait_ge(lo_ready, nb + 1)
                wh, wl = w_hi[:, nb % SPLIT, :], w_lo[:, nb % SPLIT, :]
                if hcol == 0:
                    pe.wait_ge(f_lo_ready, kk // 2 + 1)
                if hcol == 0 and kk == 0:
                    pe.wait_ge(f_ready, 2 * PAIRS)
                if hcol == 1 and kk == 0:
                    pe.wait_ge(ada_mod, 24)
                for m in range(4):
                    for k in range(2):
                        c = 512 * k + 128 * m
                        mm = mm3(psum[:, 4 * hcol + m, 0:TOK], wh[:, c:c + 128], wl[:, c:c + 128],
                                 f_hi[:, kk + k, :], f_lo[:, kk + k, :], kk + k == 0, kk + k == FT - 1)
                    if m == 3:
                        mm.then_inc(half_used, 1)
                    elif kk == FT - 2:
                        mm.then_inc(down_done, 1)
                if hcol == 1 and kk == 4:
                    for m in range(4):
                        z2_turn(m)
        for m in range(4, 8):
            z2_turn(m)

    @block.scalar
    def _(act):
        act.wait_ge(turned_c, 1)
        nc.scalar.activation(c_t[:], psum[:, 0, 0:72].rearrange("p (k c) -> p k c", c=9), ACT.Silu).then_inc(c_silu, 1)
        act.wait_ge(c_silu, 1)
        nc.scalar.activation(c_hl[:, :, 0:9], c_t[:], ACT.Copy).then_inc(c_hi, 1)
        for nb in range(AHEAD):
            hi_static(act, nb)
        for j in range(2):
            act.wait_ge(turned_x, j + 1)
            nc.scalar.activation(xT[:, 4 * j:4 * j + 4, 0:128], psum[:, 2 + 2 * j, :].rearrange("p (k c) -> p k c", c=128),
                                 ACT.Copy).then_inc(x_ready_act, 1)

        def ada_rows(a, bank, slot, used):
            act.wait_ge(half_used, used)
            nc.scalar.activation(rowbuf[:, slot, :], psum[0:18, bank, 0:256], ACT.Copy).then_inc(ada_row, 1)

        for a in range(N_ADA0):
            ada_rows(a, 5 + a % 3, a % 3, 2 * a + 2)
            hi_static(act, 2 * a + AHEAD)
            hi_static(act, 2 * a + 1 + AHEAD)
        for k in range(KT):
            act.wait_ge(h_ready, k + 1)
            nc.scalar.activation(act_hi[:, k, :], qkvg[:, k, :], ACT.Copy).then_inc(h_hi, 1)

        def mix(i, kinds):
            for k in range(6):
                nb0 = i * 12 + 2 * (MIX0 + k)
                for hh in range(2):
                    nb = nb0 + hh
                    if k % 2 == 0 and kinds[k // 2]:
                        act.wait_ge(half_used, nb + 1)
                        blk = i * 6 + (k + hh)
                        nc.scalar.activation(block_at(qkvg, blk), psum[:, hh, 0:TOK], ACT.Copy).then_inc(evicted, 1)
                    elif k % 2 == 1 and hh == 1:
                        a8 = N_ADA0 + k // 2
                        ada_rows(None, 5 + a8 % 3, a8 % 3, nb + 1)
                for hh in range(2):
                    kk = k + 2
                    rslot = (MIX0 + kk) % RAW
                    split_hi(act, nb0 + hh + AHEAD, (2 * k + hh) % SPLIT, rslot, hh,
                             (i * 2 + ((MIX0 + kk) // RAW + 1)) * 16)

        with act.Fori(0, 2) as i:
            mix(i, (True, True, True))
        mix(2, (False, False, False))
        mix(3, (True, True, False))

        for j in range(8):
            act.wait_ge(tok_turned, 2 * j + 1)
            bank = 2 + (j % 2) * 2
            nc.scalar.activation(tok[:, 0:2, 1, 128 * j:128 * j + 128],
                                 psum[:, bank, 0:256].rearrange("p (t c) -> p t c", t=2), ACT.Copy)
            nc.scalar.activation(tok[0:SAMPLE, 2, 1, 128 * j:128 * j + 128], psum[0:SAMPLE, bank, 256:384],
                                 ACT.Copy).then_inc(v_tok, 1)
        for idx in range(2 * DEC_B):
            b, hp = idx // 2, idx % 2
            act.wait_ge(kt_turned, idx + 1)
            if idx >= 2:
                act.wait_ge(scored_s, idx - 1)
            nc.scalar.activation(kT[:, hp, 0:128], psum[:, 4 + 2 * hp, 0:128], ACT.Copy)
            nc.scalar.activation(kT[:, hp, 160:416], psum[:, 4 + 2 * hp, 128:384], ACT.Copy).then_inc(kt_x, 1)
        for br, (c0, c1) in enumerate(((0, 544), (544, 832))):
            act.wait_ge(max_s, br + 1)
            nc.scalar.activation(s_prb[:, c0:c1], s_msk[:, c0:c1], ACT.Exp, bias=small[:, 4 + br:5 + br], scale=SCALE,
                                 accum_out=small[:, 6 + br:7 + br]).then_inc(exp_s, 1)

        def softmax_exp(u):
            br, t, h = UNITS[u]
            act.wait_ge(maxed, u + 1)
            if u >= 2:
                act.wait_ge(turned, u - 1)
            if u == 0:
                act.wait_ge(probT_turned, 3)
            n = (3 if br == 0 else 1) * 128 * (t + 1)
            nc.scalar.activation(prb[:, u % 2, 0:n], msk[:, 0:n], ACT.Exp, bias=small[:, 16 + u:17 + u], scale=SCALE,
                                 accum_out=small[:, 32 + u:33 + u]).then_inc(exped, 1)

        def prbT_copy(u):
            br, t, h = UNITS[u]
            act.wait_ge(turned, u + 1)
            if u >= 2:
                act.wait_ge(pv_done, u - 1)
            n = min(4, (3 if br == 0 else 1) * (t + 1)) * 128
            nc.scalar.activation(prbT[:, u % 2, 0:n], psum[:, 4, 0:n], ACT.Copy).then_inc(prbT_a, 1)

        for s in range(20):
            if s < 16:
                act.wait_ge(half_used, 2 * GATE0 + s + 1)
                if s == 8:
                    act.wait_ge(tok_turned, 16)
                nc.scalar.activation(qkvg[:, gate_slot(s), :], psum[:, s % 2, 0:TOK], ACT.Copy).then_inc(acc_free[s % 2], 1)
                hi_static(act, 2 * GATE0 + s + AHEAD)
            if s == 2:
                for n0, n1, rows_n, turned_n in ((0, 3, 128, 1), (3, 4, 64, 1), (4, 6, 128, 2), (6, 8, SAMPLE, 2), (8, 10, SAMPLE, 3)):
                    act.wait_ge(probT_turned, turned_n)
                    c0 = 128 * (n0 % 4)
                    src = psum[0:rows_n, 4 + n0 // 4, c0:c0 + 128 * (n1 - n0)].rearrange("p (k c) -> p k c", c=128)
                    ins = nc.scalar.activation(s_prbT[0:rows_n, n0:n1, :], src, ACT.Copy)
                    if n1 in (8, 10):
                        ins.then_inc(probT_s, 1)
            if 2 <= s < 18:
                softmax_exp(s - 2)
            if 3 <= s < 19:
                prbT_copy(s - 3)
        act.wait_ge(acc_free[1], 20)
        act.wait_ge(acc_free[0], 20)
        for c0, c1 in ((24, 32), (12, 18), (22, 24)):
            nc.scalar.activation(qkvg[:, c0:c1, :], qkvg[:, c0:c1, :], ACT.Sigmoid).then_inc(sig_ready, 1)
        for t in range(2):
            act.wait_ge(oT_turned, t + 1)
            if t == 0:
                act.wait_ge(pv_s, DEC_B)
            nc.scalar.activation(oT_hi[:, :, 128 * t:128 * t + 128], psum[:, 2 + t, :].rearrange("p (k c) -> p k c", c=128),
                                 ACT.Copy).then_inc(oT_h, 1)
        for h2 in range(2):
            nc.scalar.activation(o_sample_dst(oT_hi, h2), o_sample_src(psum, h2), ACT.Copy).then_inc(oT_h, 1)
        for h in range(4):
            hi_static(act, 2 * PAB0 + h + AHEAD)
            if h % 2 == 0:
                for m in range(2 * h, 2 * h + 4):
                    act.wait_ge(merged, m + 1)
                    nc.scalar.activation(act_hi[:, m, :], qkvg[:, m, :], ACT.Copy).then_inc(merged_hi, 1)
        for m in range(KT):
            hi_static(act, 2 * WO0 + m + AHEAD)
        for j in range(2):
            act.wait_ge(centred, j + 1)
            nc.scalar.activation(qkvg[:, 8 + 4 * j:12 + 4 * j, :], xT[:, 4 * j:4 * j + 4, :], ACT.Square).then_inc(squared, 1)
        ada_rows(20, 5 + 20 % 3, 20 % 3, 2 * ADA2 + 2)
        hi_static(act, 2 * ADA2 + AHEAD)
        hi_static(act, 2 * ADA2 + 1 + AHEAD)
        act.wait_ge(var_done, 1)
        nc.scalar.activation(rstd[:], psum[:, 3, 0:TOK], ACT.Sqrt, bias=cst[:, C_EPS:C_EPS + 1]).then_inc(std_ready, 1)
        for j in range(1, 3):
            ada_rows(20 + j, 5 + (20 + j) % 3, (20 + j) % 3, 2 * (ADA2 + j) + 2)
        for m in range(KT + 1):
            if m < KT:
                act.wait_ge(normed, m + 1)
                nc.scalar.activation(xT[:, m, :], xT[:, m, :], ACT.Identity, bias=lnp[:, 56 + m:57 + m],
                                     scale=lnp[:, 48 + m:49 + m]).then_inc(x1_ready, 1)
            if m < 6:
                hi_static(act, 2 * ADA2 + 2 + AHEAD + m)
            if m == 3:
                ada_rows(23, 5 + 23 % 3, 23 % 3, 2 * (ADA2 + 3) + 2)
            if m >= 1:
                act.wait_ge(h2_ready, m)
                nc.scalar.activation(act_hi[:, m - 1, :], h_t[:, (m - 1) % 2, :], ACT.Copy).then_inc(h2_hi, 1)

        def up_pair(j, k, i):
            for q in range(4):
                nb = j * 4 + (2 * UP0 + q)
                if q < 2:
                    act.wait_ge(half_used, nb + 1)
                    if not isinstance(j, int) or j >= 1:
                        act.wait_ge(f_ready, j * 2 + (q - 1))
                    nc.scalar.activation(silu_t[:, q, :], psum[:, q, 0:TOK], ACT.Silu).then_inc(silu_ready, 1)
                if isinstance(j, int):
                    hi_static(act, nb + AHEAD)
                else:
                    n2 = UP0 + 2 * k + 2 + q // 2
                    split_hi(act, nb + AHEAD, q, n2 % RAW, q % 2, (i * 2 + raw_need(n2, n2 % RAW) // 16) * 16)
                if q >= 2:
                    fi = j * 2 + (q - 2)
                    act.wait_ge(f_ready, fi + 1)
                    nc.scalar.activation(block_at(f_hi, fi), f_t[:, q - 2, :], ACT.Copy).then_inc(f_hi_ready, 1)

        for j in range(3):
            up_pair(j, j, 0)
        with act.Fori(1, UP_TRIPS) as i:
            for k in range(UP_PAIRS):
                up_pair(i * 3 + k, k, i)
        for j in range(UP_PAIRS * UP_TRIPS, PAIRS):
            up_pair(j, 0, 0)
        for nb in range(2 * DOWN0, LAST + 1):
            hi_static(act, nb + AHEAD)
        for t in range(3):
            nt = 128 if t < 2 else SAMPLE
            act.wait_ge(var2, t + 1)
            nc.scalar.activation(small[0:nt, 60 + t:61 + t], small[0:nt, 51 + 2 * t:52 + 2 * t], ACT.Sqrt,
                                 bias=cst[0:nt, C_EPS:C_EPS + 1]).then_inc(std2, 1)
        act.wait_ge(ln_rows_in, 32)
        for t in range(3):
            nt = 128 if t < 2 else SAMPLE
            act.wait_ge(rs2, t + 1)
            for hcol in range(2):
                nc.scalar.activation(y_tok[0:nt, t, 512 * hcol:512 * hcol + 512], psum[0:nt, t + 3 * hcol, :], ACT.Identity,
                                     bias=small[0:nt, 66 + t:67 + t], scale=small[0:nt, 63 + t:64 + t]).then_inc(y_norm, 1)

    @block.vector
    def _(dve):
        V = nc.vector

        def link(ins):
            dve_link.up(ins)
            dve.wait_ge(dve_link.sem, dve_link.n)

        dve.wait_ge(c_hi, 1)
        V.tensor_tensor(c_hl[:, :, 9:18], c_t[:], c_hl[:, :, 0:9].bitcast(F32), ALU.subtract).then_inc(c_ready, 1)
        dve.wait_ge(turned_rows, 1)
        V.tensor_copy(lnp[:, :], psum[:, 1, 0:64]).then_inc(rows_ready, 1)
        for nb in range(AHEAD):
            lo_static(dve, nb)
        for j in range(2):
            dve.wait_ge(turned_x, j + 3)
            V.tensor_copy(xT[:, 4 * j:4 * j + 4, 128:256],
                          psum[:, 3 + 2 * j, :].rearrange("p (k c) -> p k c", c=128)).then_inc(x_ready_dve, 1)
        dve.wait_ge(turned_x, 5)
        V.tensor_copy(xT[:, :, PROMPT:TOK], psum[:, 6, 0:256].rearrange("p (k c) -> p k c", c=SAMPLE)).then_inc(x_ready_dve, 1)
        dve.wait_ge(rows_ready, 1)

        def ada_add(a, bank):
            dve.wait_ge(ada_turned, a + 1)
            dst = mod[:, 2 * a:2 * a + 2, :] if isinstance(a, int) else mod[:, bass.ds(a * 2, 2), :]
            src = psum[:, bank, 256:292].rearrange("p (k h c) -> p k c h", k=2, h=2)
            V.tensor_reduce(dst, src, mybir.AxisListType.X, ALU.add).then_inc(ada_mod, 1)

        def add_bias(b0, b1, a_done):
            dve.wait_ge(ada_mod, a_done)
            link(V.tensor_tensor(mod[:, b0:b1, :], mod[:, b0:b1, :],
                                 lnp[:, b0:b1].unsqueeze(2).broadcast_to([128, b1 - b0, 9]), ALU.add))

        def modulated(dst, src, m, sh, sc, done):
            V.tensor_scalar(dst[:, 0:PROMPT], src[:, 0:PROMPT], mod[:, 8 * sc + m, 0:1], mod[:, 8 * sh + m, 0:1], ALU.mult, ALU.add)
            by_b = lambda i: mod[:, 8 * i + m, 1:9].unsqueeze(2).broadcast_to([128, DEC_B, DEC_T])
            d3 = dst[:, PROMPT:TOK].rearrange("p (b t) -> p b t", t=DEC_T)
            s3 = src[:, PROMPT:TOK].rearrange("p (b t) -> p b t", t=DEC_T)
            link(V.tensor_tensor(d3, s3, by_b(sc), ALU.mult))
            V.tensor_tensor(d3, d3, by_b(sh), ALU.add).then_inc(done, 1)

        for a in range(N_ADA0):
            ada_add(a, 5 + a % 3)
            lo_static(dve, 2 * a + AHEAD)
            lo_static(dve, 2 * a + 1 + AHEAD)
        add_bias(0, 16, 8)
        link(V.tensor_scalar_add(mod[:, 8:16, :], mod[:, 8:16, :], 1.0))
        dve.wait_ge(x_ready_act, 2)
        dve.wait_ge(x_ready_dve, 3)
        for k in range(KT):
            modulated(qkvg[:, k, :], xT[:, k, :], k, 0, 1, h_ready)
            if k >= 1:
                dve.wait_ge(h_hi, k)
                V.tensor_tensor(act_lo[:, k - 1, :], qkvg[:, k - 1, :], act_hi[:, k - 1, :].bitcast(F32), ALU.subtract).then_inc(h_lo, 1)
        dve.wait_ge(h_hi, KT)
        V.tensor_tensor(act_lo[:, KT - 1, :], qkvg[:, KT - 1, :], act_hi[:, KT - 1, :].bitcast(F32), ALU.subtract).then_inc(h_lo, 1)

        def rope(blk, ru, hh, turn):
            dve.wait_ge(evicted, ru + 1)
            dve.sem_inc(dve_past, 1)
            V.stream_shuffle(rope_t[:, hh, :], psum[:, hh, 0:TOK], SWAP).then_inc(acc_free[hh], 1)
            dve.wait_ge(acc_free[hh], turn + 1)
            link(V.tensor_tensor(rope_t[:, hh, :], rope_t[:, hh, :], cst[:, C_SIN:C_SIN + TOK], ALU.mult))
            dve.wait_ge(cos_done, ru + 1)
            V.tensor_tensor(block_at(qkvg, blk), block_at(qkvg, blk), rope_t[:, hh, :], ALU.add).then_inc(roped, 1)

        def mix(i, rope_base, kinds):
            for k in range(6):
                nb0 = i * 12 + 2 * (MIX0 + k)
                if k % 2 == 1:
                    a8 = N_ADA0 + k // 2
                    for hh in range(2):
                        split_lo(dve, nb0 + hh + AHEAD, (2 * k + hh) % SPLIT, (MIX0 + k + 2) % RAW, hh)
                    if k >= 3:
                        ada_add(i * 3 + (a8 - 1), 5 + (a8 - 1) % 3)
                else:
                    for hh in range(2):
                        blk = i * 6 + (k + hh)
                        if kinds[k // 2]:
                            rope(blk, rope_base + k + hh, hh, i * 3 + k // 2)
                        else:
                            dve.wait_ge(half_used, nb0 + hh + 1)
                            V.tensor_copy(block_at(qkvg, blk), psum[:, hh, 0:TOK]).then_inc(acc_free[hh], 1)
                        split_lo(dve, nb0 + hh + AHEAD, (2 * k + hh) % SPLIT, (MIX0 + k + 2) % RAW, hh)
            ada_add(i * 3 + (N_ADA0 + 2), 5 + (N_ADA0 + 2) % 3)

        before, links = dve_link.n, 6
        with dve.Fori(0, 2) as i:
            dve_link.n = i * links + before
            mix(i, i * 6, (True, True, True))
        dve_link.n = before + 2 * links
        mix(2, 0, (False, False, False))
        mix(3, 12, (True, True, False))
        add_bias(16, 40, N_ADA0 + 12)
        link(V.tensor_scalar_add(mod[:, 32:40, :], mod[:, 32:40, :], 1.0))

        dve.wait_ge(roped, 16)
        dve.wait_ge(qz_zero, 1)
        for g in range(4):
            for hp in range(2):
                for h2 in range(2):
                    dst = qz[E * h2:E * h2 + E, g, hp, :, :].rearrange("p q (s c) -> p q s c", c=16)
                    dst = dst[:, :, 0:3:2, 8 * hp + 4 * h2:8 * hp + 4 * h2 + 4]
                    src = qkvg[E * h2:E * h2 + E, q_blk(g, hp), PROMPT:TOK].rearrange("p (q s t) -> p q s t", s=2, t=4)
                    V.tensor_copy(dst, src)
                last = V.tensor_copy(kT[:, hp, NEW_COL[g]:NEW_COL[g] + SAMPLE], qkvg[:, k_blk(g, hp), PROMPT:TOK])
        last.then_inc(qz_ready, 1)
        for j in range(8):
            dve.wait_ge(tok_turned, 2 * j + 2)
            bank = 3 + (j % 2) * 2
            V.tensor_copy(tok[:, 0:2, 0, 128 * j:128 * j + 128], psum[:, bank, 0:256].rearrange("p (t c) -> p t c", t=2))
            V.tensor_copy(tok[0:SAMPLE, 2, 0, 128 * j:128 * j + 128], psum[0:SAMPLE, bank, 256:384]).then_inc(k_tok, 1)
        for idx in range(2 * DEC_B):
            b, hp = idx // 2, idx % 2
            dve.wait_ge(kt_turned, idx + 1)
            if idx >= 2:
                dve.wait_ge(scored_s, idx - 1)
            V.tensor_copy(kT[:, hp, 448:512], psum[:, 5 + 2 * hp, 0:64])
            V.tensor_copy(kT[:, hp, 544:800], psum[:, 5 + 2 * hp, 64:320]).then_inc(kt_y, 1)
        dve.wait_ge(scored_s, 2 * DEC_B)
        for j, (c0, c1, bank, o0) in enumerate(((0, 448, 2, 0), (448, 544, 3, 0), (544, 832, 3, 96))):
            ins = V.tensor_tensor_reduce(s_msk[:, c0:c1], psum[:, bank, o0:o0 + c1 - c0], cst[:, C_MS + c0:C_MS + c1],
                                         1.0, -3.0e38, ALU.add, ALU.max, small[:, j:j + 1])
            link(ins)
        link(V.tensor_tensor(small[:, 1:2], small[:, 0:1], small[:, 1:2], ALU.max))
        V.tensor_scalar(small[:, 4:5], small[:, 1:2], -SCALE, None, ALU.mult).then_inc(max_s, 1)
        V.tensor_scalar(small[:, 5:6], small[:, 2:3], -SCALE, None, ALU.mult).then_inc(max_s, 1)

        def softmax_max(u):
            br, t, h = UNITS[u]
            dve.wait_ge(scored, u + 1)
            if u == 0:
                dve.wait_ge(probT_turned, 3)
            else:
                dve.wait_ge(exped, u)
            n = (3 if br == 0 else 1) * 128 * (t + 1)
            m0 = ((C_MA0, C_MA1), (C_MB0, C_MB1))[br][t]
            src = psum[:, 2:4, :].rearrange("p b c -> p (b c)")[:, 0:n]
            link(V.tensor_tensor_reduce(msk[:, 0:n], src, cst[:, m0:m0 + n], 1.0, -3.0e38, ALU.add, ALU.max, small[:, 112 + u:113 + u]))
            V.tensor_scalar(small[:, 16 + u:17 + u], small[:, 112 + u:113 + u], -SCALE, None, ALU.mult).then_inc(maxed, 1)

        def prbT_copy(u):
            br, t, h = UNITS[u]
            dve.wait_ge(turned, u + 1)
            if u >= 2:
                dve.wait_ge(pv_done, u - 1)
            n = (3 if br == 0 else 1) * (t + 1) * 128
            if n > 512:
                V.tensor_copy(prbT[:, u % 2, 512:n], psum[:, 5, 0:n - 512]).then_inc(prbT_b, 1)

        def out_copy(u):
            br, t, h = UNITS[u]
            dve.wait_ge(exped, u + 1)
            link(V.reciprocal(small[:, 96 + u:97 + u], small[:, 32 + u:33 + u]))
            dve.wait_ge(pv_done, u + 1)
            V.tensor_scalar(o_tokens[:, t, br, E * h:E * h + E], psum[:, 6, 0:E], small[:, 96 + u:97 + u], None, ALU.mult).then_inc(o_ready, 1)

        for s in range(20):
            if s < 16:
                lo_static(dve, 2 * GATE0 + s + AHEAD)
            if s == 1:
                dve.wait_ge(exp_s, 2)
                link(V.reciprocal(small[:, 10:12], small[:, 6:8]))
                for br, (c0, c1) in enumerate(((0, 544), (544, 832))):
                    V.tensor_scalar(s_prb[:, c0:c1], s_prb[:, c0:c1], small[:, 10 + br:11 + br], None, ALU.mult).then_inc(prob_s, 1)
            if 2 <= s < 18:
                softmax_max(s - 2)
            if 3 <= s < 19:
                prbT_copy(s - 3)
            if s >= 4:
                out_copy(s - 4)
        for t in range(2):
            dve.wait_ge(oT_h, t + 1)
            V.tensor_tensor(oT_lo[:, :, 128 * t:128 * t + 128], psum[:, 2 + t, :].rearrange("p (k c) -> p k c", c=128),
                            oT_hi[:, :, 128 * t:128 * t + 128].bitcast(F32), ALU.subtract).then_inc(oT_l, 1)
        dve.wait_ge(oT_h, 4)
        for h2 in range(2):
            V.tensor_tensor(o_sample_dst(oT_lo, h2), o_sample_src(psum, h2), o_sample_dst(oT_hi, h2).bitcast(F32),
                            ALU.subtract).then_inc(oT_l, 1)
        dve.wait_ge(sig_ready, 3)

        def merged_rest(m):
            dve.wait_ge(merged_hi, m + 1)
            V.tensor_tensor(act_lo[:, m, :], qkvg[:, m, :], act_hi[:, m, :].bitcast(F32), ALU.subtract).then_inc(merged_lo, 1)

        for h in range(4):
            for m in range(4):
                u = 40 + 4 * h + m
                blk = 4 * (h // 2) + m
                if m < 3:
                    dve.wait_ge(pab_done, 3 * h + m + 1)
                else:
                    dve.wait_ge(half_used, 2 * PAB0 + h + 1)
                gate = qkvg[:, gate_slot(blk + 8 * (h % 2)), :]
                dst = h_t[:, m % 2, :] if h % 2 else qkvg[:, blk, :]
                V.tensor_tensor(dst, psum[:, u % 2, 0:TOK], gate, ALU.mult).then_inc(acc_free[u % 2], 1)
                if h % 2 == 1:
                    dve.wait_ge(acc_free[u % 2], u // 2 + 1)
                    V.tensor_tensor(qkvg[:, blk, :], qkvg[:, blk, :], h_t[:, m % 2, :], ALU.add).then_inc(merged, 1)
                    if m >= 1:
                        merged_rest(blk - 1)
            if h % 2 == 1:
                merged_rest(4 * (h // 2) + 3)
            lo_static(dve, 2 * PAB0 + h + AHEAD)

        def residual(m, bank, gi, done, free=None):
            g3 = mod[:, 8 * gi + m, 1:9].unsqueeze(2).broadcast_to([128, DEC_B, DEC_T])
            t3 = h_t[:, m % 2, 0:SAMPLE].rearrange("p (b t) -> p b t", t=DEC_T)
            p3 = psum[:, bank, PROMPT:TOK].rearrange("p (b t) -> p b t", t=DEC_T)
            link(V.tensor_tensor(t3, p3, g3, ALU.mult))
            link(V.tensor_tensor(xT[:, m, PROMPT:TOK], xT[:, m, PROMPT:TOK], h_t[:, m % 2, 0:SAMPLE], ALU.add))
            V.scalar_tensor_tensor(xT[:, m, 0:PROMPT], psum[:, bank, 0:PROMPT], mod[:, 8 * gi + m, 0:1], xT[:, m, 0:PROMPT],
                                   ALU.mult, ALU.add).then_inc(done, 1)

        dve.wait_ge(x_scaled, 1)
        for m in range(KT):
            dve.wait_ge(half_used, 2 * WO0 + m + 1)
            residual(m, m % 2, 2, z_ready)
            lo_static(dve, 2 * WO0 + m + AHEAD)
        dve.wait_ge(mean_done, KT)
        for j in range(2):
            V.tensor_tensor(xT[:, 4 * j:4 * j + 4, :], xT[:, 4 * j:4 * j + 4, :],
                            psum[:, 2, 0:TOK].unsqueeze(1).broadcast_to([128, 4, TOK]), ALU.subtract).then_inc(centred, 1)
        ada_add(20, 5 + 20 % 3)
        lo_static(dve, 2 * ADA2 + AHEAD)
        lo_static(dve, 2 * ADA2 + 1 + AHEAD)
        dve.wait_ge(std_ready, 1)
        link(V.reciprocal(rstd[:], rstd[:]))
        for m in range(KT + 2):
            if m < KT:
                V.tensor_tensor(xT[:, m, :], xT[:, m, :], rstd[:], ALU.mult).then_inc(normed, 1)
            if m < 6:
                lo_static(dve, 2 * ADA2 + 2 + AHEAD + m)
            if 1 <= m <= KT:
                dve.wait_ge(x1_ready, m)
                if m >= 3:
                    dve.wait_ge(h2_lo, m - 2)
                modulated(h_t[:, (m - 1) % 2, :], xT[:, m - 1, :], m - 1, 3, 4, h2_ready)
            if m >= 2:
                dve.wait_ge(h2_hi, m - 1)
                V.tensor_tensor(act_lo[:, m - 2, :], h_t[:, m % 2, :], act_hi[:, m - 2, :].bitcast(F32), ALU.subtract).then_inc(h2_lo, 1)
        for a in range(21, 24):
            ada_add(a, 5 + a % 3)
        add_bias(40, 48, 24)

        def up_pair(j, k):
            for q in range(4):
                nb = j * 4 + (2 * UP0 + q)
                fi = j * 2 + (q - 2)
                if q >= 2:
                    dve.wait_ge(half_used, nb + 1)
                    dve.wait_ge(silu_ready, fi + 1)
                    if not isinstance(j, int) or j >= 1:
                        dve.wait_ge(f_lo_ready, fi - 1)
                    V.tensor_tensor(f_t[:, q - 2, :], psum[:, q % 2, 0:TOK], silu_t[:, q - 2, :], ALU.mult).then_inc(f_ready, 1)
                if isinstance(j, int):
                    lo_static(dve, nb + AHEAD)
                else:
                    split_lo(dve, nb + AHEAD, q, (UP0 + 2 * k + 2 + q // 2) % RAW, q % 2)
                if q >= 2:
                    dve.wait_ge(f_hi_ready, fi + 1)
                    V.tensor_tensor(block_at(f_lo, fi), f_t[:, q - 2, :], block_at(f_hi, fi).bitcast(F32), ALU.subtract).then_inc(f_lo_ready, 1)

        for j in range(3):
            up_pair(j, j)
        with dve.Fori(1, UP_TRIPS) as i:
            for k in range(UP_PAIRS):
                up_pair(i * 3 + k, k)
        for j in range(UP_PAIRS * UP_TRIPS, PAIRS):
            up_pair(j, 0)

        dve.wait_ge(x1_scaled, 1)

        def second(hcol):
            for m in range(4):
                if m < 3:
                    dve.wait_ge(down_done, 3 * hcol + m + 1)
                else:
                    dve.wait_ge(half_used, 2 * DOWN0 + 11 * hcol + 11)
                residual(4 * hcol + m, 4 * hcol + m, 5, z2_ready)
        for nb in range(2 * DOWN0, 2 * DOWN0 + 11):
            lo_static(dve, nb + AHEAD)
        second(0)
        for nb in range(2 * DOWN0 + 11, LAST + 1):
            lo_static(dve, nb + AHEAD)
        second(1)
        dve.wait_ge(z2_turned, 8)
        for t in range(3):
            nt = 128 if t < 2 else SAMPLE
            for hcol in range(2):
                link(V.bn_stats(st6[0:nt, t, hcol, :], psum[0:nt, t + 3 * hcol, :]))
            V.bn_aggr(small[0:nt, 50 + 2 * t:52 + 2 * t], st6[0:nt, t, :, :].rearrange("p a b -> p (a b)")).then_inc(var2, 1)
        for t in range(3):
            nt = 128 if t < 2 else SAMPLE
            dve.wait_ge(std2, t + 1)
            link(V.reciprocal(small[0:nt, 63 + t:64 + t], small[0:nt, 60 + t:61 + t]))
            V.scalar_tensor_tensor(small[0:nt, 66 + t:67 + t], small[0:nt, 50 + 2 * t:51 + 2 * t], -1.0, small[0:nt, 63 + t:64 + t],
                                   ALU.mult, ALU.mult).then_inc(rs2, 1)
        dve.wait_ge(ln_rows_in, 32)
        for t in range(3):
            nt = 128 if t < 2 else SAMPLE
            dve.wait_ge(y_norm, 2 * t + 2)
            link(V.tensor_tensor(y_tok[0:nt, t, :], y_tok[0:nt, t, :], ln_rows[0:nt, 0, :], ALU.mult))
            V.tensor_tensor(y_tok[0:nt, t, :], y_tok[0:nt, t, :], ln_rows[0:nt, 1, :], ALU.add).then_inc(y_done, 1)

    @block.gpsimd
    def _(pool):
        pool.dma_start(pages[:], page_table.rearrange("b n -> (b n)").unsqueeze(0)).then_inc(pages_in, 16)
        nc.gpsimd.memset(qz[:], 0.0).then_inc(qz_zero, 1)
        pool.wait_ge(pages_in, 16)

        def load_kv(b, kind):
            slot, s = b % 2, kv_in[b % 2]
            pool.dma_start(kvin[:, slot, 0, :], cache_a[0][b, :, kind, :]).then_inc(s, 16)
            pool.dma_start(kvin[:, slot, 1:3, :], cache_a[1][b, :, kind, :].rearrange("(n p) c -> p n c", p=128)).then_inc(s, 16)
            src = cache_a[2][b, :, kind, :].rearrange("(g r) c -> g r c", r=16)[:, 0:4, :]
            pool.dma_start(kvin[0:64, slot, 5, :], src).then_inc(s, 16)
            for j in range(N_PAGES):
                page = pool.value_load(pages[0:1, N_PAGES * b + j:N_PAGES * b + j + 1], min_val=0, max_val=cache_b.shape[0] - 1)
                pool.dma_start(kvin[:, slot, 3 + j, :],
                               cache_b[bass.ds(page, 1), :, kind, :].rearrange("a p c -> (a p) c")).then_inc(s, 16)

        def cos_mult(blk, ru):
            pool.wait_ge(evicted, ru + 1)
            nc.gpsimd.tensor_tensor(block_at(qkvg, blk), block_at(qkvg, blk), cst[:, C_COS:C_COS + TOK], ALU.mult).then_inc(cos_done, 1)

        pool.wait_ge(const_in, 16)
        with pool.Fori(0, 12) as i:
            cos_mult(i, i)
        for b in range(2):
            load_kv(b, 0)
        for blk in range(18, 22):
            cos_mult(blk, blk - 6)
        nc.gpsimd.tensor_scalar(xT[:], xT[:], ALPHA, None, ALU.mult).then_inc(x_scaled, 1)
        for g in range(3):
            pool.dma_start(kv_sample[g][:, 0:BUF[g] - DEC_T, :], cache_rows[g][:, DEC_T:BUF[g], :]).then_inc(stored, 16)
        for b in range(2, DEC_B):
            pool.wait_ge(kt_turned, 2 * b - 2)
            load_kv(b, 0)
        pool.wait_ge(k_tok, 8)
        pool.wait_ge(v_tok, 8)
        for kind in range(2):
            for g in range(4):
                lo = PROMPT - (min(WIN[g], PROMPT) if g < 3 else PROMPT)
                cols = slice(256 * g, 256 * g + 256)
                dst = kv_prompt[g].rearrange("(t p) s c -> p t s c", p=128)
                pool.dma_start(dst[:, :, kind, :], tok[:, lo // 128:2, kind, cols]).then_inc(stored, 16)
        for kind in range(2):
            for g in range(4):
                dst = kv_sample[g][:, (BUF[g] - DEC_T if g < 3 else 0):, 256 * kind:256 * kind + 256]
                src = tok[0:SAMPLE, 2, kind, 256 * g:256 * g + 256]
                pool.dma_start(dst, src).then_inc(stored, 16)
        for b in range(DEC_B):
            if b < 2:
                pool.wait_ge(kt_turned, 2 * (DEC_B - 2 + b) + 2)
            else:
                pool.wait_ge(pv_s, b - 1)
            load_kv(b, 1)
        pool.wait_ge(half_used, 2 * WO0)
        pool.wait_ge(stored, 16 * N_POOL_STORES)
        pool.dma_start(ln_rows[:, 0, :], ln2_g.broadcast_to([128, D])).then_inc(ln_rows_in, 16)
        pool.dma_start(ln_rows[:, 1, :], ln2_b.broadcast_to([128, D])).then_inc(ln_rows_in, 16)
        pool.wait_ge(x1_ready, KT)
        pool.wait_ge(h2_ready, KT)
        nc.gpsimd.tensor_scalar(xT[:], xT[:], ALPHA, None, ALU.mult).then_inc(x1_scaled, 1)

    ctx.close()


_INS = ["x_prompt", "x_sample", "cache_kv_a0", "cache_kv_a1", "cache_kv_a2", "cache_kv_b", "page_table", "c_prompt", "c_sample",
        "w_ada", "b_ada", "w_in", "w_pa", "w_pb", "w_o", "ln1_g", "ln1_b", "w_up", "w_down", "ln2_g", "ln2_b"]
_OUTS = [(1, PROMPT, D), (DEC_B, DEC_T, D)] + \
        [(1, 1, min(w, PROMPT), 2, 4, E) for w in WIN] + [(1, 1, PROMPT, 2, 4, E)] + \
        [(1, DEC_B, b, 2, 4, E) for b in BUF] + [(1, DEC_B, DEC_T, 2, 4, E)]


def kernel(**inputs):
    import numpy as np
    import concourse.bacc as bacc
    from concourse.bass_utils import run_bass_kernel_spmd

    nc = bacc.Bacc("TRN2", target_bir_lowering=False, num_devices=1)
    arrays, a = {}, {}
    for name in _INS:
        v = np.ascontiguousarray(inputs[name])
        arrays[f"in_{name}"] = v
        a[name] = nc.dram_tensor(f"in_{name}", v.shape, mybir.dt.from_np(v.dtype), kind="ExternalInput").ap()
    arrays["in_const"] = constants()
    const = nc.dram_tensor("in_const", (128, C_END), F32, kind="ExternalInput").ap()
    outs = [nc.dram_tensor(f"out_{i}", shape, F32, kind="ExternalOutput").ap() for i, shape in enumerate(_OUTS)]
    caches = [a[f"cache_kv_a{g}"] for g in range(3)]
    build(nc, a["x_prompt"], a["x_sample"],
          [c.rearrange("a b l k h e -> (a b) l k (h e)") for c in caches],
          [c.rearrange("a b l k h e -> (a b) l (k h e)") for c in caches],
          a["cache_kv_b"].rearrange("a n p k h e -> (a n) p k (h e)"),
          a["page_table"], a["c_prompt"], a["c_sample"], a["w_ada"][0], a["b_ada"], a["w_in"][0], a["w_pa"][0],
          a["w_pb"][0], a["w_o"][0], a["ln1_g"], a["ln1_b"], a["w_up"][0], a["w_down"][0], a["ln2_g"], a["ln2_b"], const,
          outs[0], outs[1],
          [o.rearrange("a b l k h e -> (a b l) k (h e)") for o in outs[2:6]],
          [o.rearrange("a b l k h e -> (a b) l (k h e)") for o in outs[6:10]])
    r = run_bass_kernel_spmd(nc, [arrays], core_ids=[0])
    return tuple(r.results[0][f"out_{i}"] for i in range(len(_OUTS)))
```

```python
import math
from contextlib import ExitStack

import concourse.bass as bass
from concourse import mybir
from concourse.alu_op_type import AluOpType as ALU

F32 = mybir.dt.float32
F32R = mybir.dt.float32r
ACT = mybir.ActivationFunctionType

D = 1024
KT = D // 128
PROMPT = 256
DEC_B, DEC_T = 8, 4
SAMPLE = DEC_B * DEC_T
TOK = PROMPT + SAMPLE
PAST = 256
PAGE = 128
N_PAGES = PAST // PAGE
E = 64
ROT = E // 4
THETA = 500000.0
D_FF = -(-8 * D // (3 * 256)) * 256
FT = D_FF // 128
WIN = (128, 512, 2048)
DIL = (1, 4, 16)
BUF = tuple(min(w, PAST) for w in WIN)
ALPHA = 2.0 ** 0.25
EPS = 1e-5
SCALE = E ** -0.5
NEG = -1.0e30

RAW = 3
SPLIT = 4
N_ADA0 = 8
MIX0 = N_ADA0
GATE0 = MIX0 + 24
PAB0 = GATE0 + 8
WO0 = PAB0 + 2
ADA2 = WO0 + 4
UP0 = ADA2 + 4
DOWN0 = UP0 + 22
PAIRS = D_FF // 256


def ropetables():
    import numpy as np
    inv = np.exp(np.float32(-math.log(THETA)) * np.arange(0, ROT, 2, dtype=np.float32) / np.float32(ROT)).astype(np.float32)
    pos = np.concatenate([np.arange(PROMPT), np.tile(PAST + np.arange(DEC_T), DEC_B)]).astype(np.float32)
    ang = (pos[:, None] * inv[None, :]).astype(np.float32)
    cos, sin = np.cos(ang).astype(np.float32), np.sin(ang).astype(np.float32)
    c, s = np.ones((128, TOK), np.float32), np.zeros((128, TOK), np.float32)
    for base in (0, E):
        for j in range(ROT // 2):
            c[base + j] = c[base + j + ROT // 2] = cos[:, j]
            s[base + j] = -sin[:, j]
            s[base + j + ROT // 2] = sin[:, j]
    return c, s


def prompt_mask(tile, group):
    import numpy as np
    q = tile * 128 + np.arange(128)[:, None]
    k = np.arange((tile + 1) * 128)[None, :]
    off = q - k
    ok = off >= 0
    if group < 3:
        ok = ok & (off <= WIN[group]) & (off % DIL[group] == 0)
    return np.where(ok, 0.0, NEG).astype(np.float32)


def row_of(r):
    return r // 32 + 4 * (r % 32 // 16), r % 16 // 4, r % 4


def sample_mask():
    import numpy as np
    b, _, t = row_of(np.arange(128))
    m = np.full((128, 832), NEG, np.float32)
    new_b, new_t = np.arange(SAMPLE) // DEC_T, np.arange(SAMPLE) % DEC_T

    def put(at, ok):
        m[:, at:at + ok.shape[1]] = np.where(ok, 0.0, NEG)
    put(0, np.arange(128)[None, :] >= t[:, None])
    put(160, np.arange(256)[None, :] % 4 == t[:, None])
    put(448, np.arange(64)[None, :] % 4 == t[:, None])
    put(544, np.ones((128, 256), bool))
    own = new_b[None, :] == b[:, None]
    put(128, own & (new_t[None, :] <= t[:, None]))
    put(416, own & (new_t[None, :] == t[:, None]))
    put(512, own & (new_t[None, :] == t[:, None]))
    put(800, own & (new_t[None, :] <= t[:, None]))
    return m


C_ID, C_ONE, C_COS, C_SIN = 0, 128, 256, 256 + TOK
C_MS = 256 + 2 * TOK
C_MA1 = C_MS + 832
C_MA0 = C_MA1 + 768
C_MB1 = C_MA0 + 384
C_MB0 = C_MB1 + 256
C_EPS = C_MB0 + 128
C_SELM = C_EPS + 1
C_SEL = C_SELM + 8
C_END = C_SEL + SAMPLE


def constants():
    import numpy as np
    c = np.zeros((128, C_END), np.float32)
    c[:, C_ID:C_ID + 128] = np.eye(128)
    c[:, C_ONE:C_ONE + 128] = 1.0 / D
    c[:, C_COS:C_COS + TOK], c[:, C_SIN:C_SIN + TOK] = ropetables()
    c[:, C_MS:C_MS + 832] = sample_mask()
    for g in range(3):
        c[:, C_MA1 + 256 * g:C_MA1 + 256 * (g + 1)] = prompt_mask(1, g)
        c[:, C_MA0 + 128 * g:C_MA0 + 128 * (g + 1)] = prompt_mask(0, g)
    c[:, C_MB1:C_MB1 + 256] = prompt_mask(1, 3)
    c[:, C_MB0:C_MB0 + 128] = prompt_mask(0, 3)
    c[:, C_EPS] = EPS
    b, h, t = row_of(np.arange(128))
    c[:, C_SELM:C_SELM + 8] = (b // 4 * 4 + h)[:, None] == np.arange(8)[None, :]
    c[:, C_SEL:C_SEL + SAMPLE] = (b * DEC_T + t)[:, None] == np.arange(SAMPLE)[None, :]
    return c


S_PIECES = [(0, 128), (160, 128), (288, 128), (448, 64), (544, 128), (672, 128), (128, 32), (416, 32), (512, 32), (800, 32)]
NEW_COL = [128, 416, 512, 800]
SWAP = [(i + ROT // 2) % ROT if i < ROT else i for i in range(32)]
KV_LOADS = 3 + N_PAGES
KV_RING = 4
N_POOL_STORES = 16


def block_at(t, blk):
    if isinstance(blk, int):
        return t[:, blk, :]
    return t[:, bass.ds(blk, 1), :].rearrange("p a t -> p (a t)")


class Count:

    def __init__(self, sem):
        self.sem, self.n = sem, 0

    def up(self, ins):
        ins.then_inc(self.sem, 1)
        self.n = self.n + 1


def q_blk(g, hp):
    return 2 * g + hp if g < 3 else 18 + hp


def k_blk(g, hp):
    return 6 + 2 * g + hp if g < 3 else 20 + hp


def v_blk(g, hp):
    return 12 + 2 * g + hp if g < 3 else 22 + hp


def gate_slot(g):
    return 24 + g if g < 8 else ([12, 13, 14, 15, 16, 17, 22, 23])[g - 8]


UNITS = [(0, 1, h) for h in range(4)] + [(0, 0, h) for h in range(4)] + \
        [(1, 1, h) for h in range(4)] + [(1, 0, h) for h in range(4)]


def build(nc, x_prompt, x_sample, cache_a, cache_rows, cache_b, page_table, c_prompt, c_sample, w_ada, b_ada, w_in,
          w_pa, w_pb, w_o, ln1_g, ln1_b, w_up, w_down, ln2_g, ln2_b, const,
          y_prompt, y_sample, kv_prompt, kv_sample):
    ctx = ExitStack()
    base = nc.sbuf_base if isinstance(nc.sbuf_base, int) else 0
    at = [(base + 63) // 64 * 64]

    def sb(name, shape, dt=F32, offset=None):
        size = 4
        for n in shape[1:]:
            size *= n
        if offset is None:
            offset = at[0]
            at[0] += (size + 31) // 32 * 32
        return nc.alloc_sbuf_tensor_at(name, list(shape), dt, offset=offset), offset

    xT, _ = sb("xT", [128, KT, TOK])
    act_hi, _ = sb("act_hi", [128, KT, TOK], F32R)
    act_lo, _ = sb("act_lo", [128, KT, TOK], F32R)
    raw, _ = sb("raw", [128, RAW, 2048])
    w_hi, _ = sb("w_hi", [128, SPLIT, 1024], F32R)
    w_lo, _ = sb("w_lo", [128, SPLIT, 1024], F32R)
    cst, _ = sb("cst", [128, C_END])
    qkvg, o_qkvg = sb("qkvg", [128, 32, TOK])
    kvin, _ = sb("kvin", [128, 2, 6, 256])
    kT, o_kT = sb("kT", [128, 2, 832])
    qz, o_qz = sb("qz", [128, 4, 2, 4, 48])
    tok, o_tok = sb("tok", [128, 3, 2, 1024])
    tmp, o_tmp = sb("tmp", [128, 3840])
    o_tokens, _ = sb("o_tokens", [128, 2, 2, 256])
    mod, _ = sb("mod", [128, 48, 9])
    rowbuf, _ = sb("rowbuf", [18, 3, 256])
    mod_t, _ = sb("mod_t", [128, 8, 9])
    c_hl, _ = sb("c_hl", [128, KT, 18], F32R)
    small, _ = sb("small", [128, 128])
    rows, _ = sb("rows", [64, 128])
    pages, _ = sb("pages", [1, DEC_B * N_PAGES], mybir.dt.int32)

    x_tok, _ = sb("x_tok", [128, 3, D], F32, o_tok)
    s_msk, _ = sb("s_msk", [128, 832], F32, o_tmp)
    s_prb, _ = sb("s_prb", [128, 832], F32, o_tmp + 832 * 4)
    s_prbT, _ = sb("s_prbT", [128, 10, 128], F32, o_qz)
    msk, _ = sb("msk", [128, 768], F32, o_tmp)
    prb, _ = sb("prb", [128, 2, 768], F32, o_tmp + 768 * 4)
    prbT, _ = sb("prbT", [128, 2, 768], F32, o_tmp + 3 * 768 * 4)
    oT_hi, _ = sb("oT_hi", [128, 4, TOK], F32R, o_kT)
    oT_lo, _ = sb("oT_lo", [128, 4, TOK], F32R, o_tmp + 3 * 768 * 4)
    assert 4 * TOK <= 2 * 832 and 4 * TOK <= 2 * 768
    f_hi, _ = sb("f_hi", [128, FT, TOK], F32R, o_qkvg)
    f_lo, _ = sb("f_lo", [128, FT, TOK], F32R, o_qkvg + FT * TOK * 4)
    assert o_qkvg + 2 * FT * TOK * 4 <= o_tok
    ln_rows, _ = sb("ln_rows", [128, 2, D], F32, o_tok)
    y_tok, _ = sb("y_tok", [128, 3, D], F32, o_tok + 2 * D * 4)
    silu_t, _ = sb("silu_t", [128, 2, TOK], F32, o_tmp)
    f_t, _ = sb("f_t", [128, 2, TOK], F32, o_tmp + 2 * TOK * 4)
    rstd, _ = sb("rstd", [128, TOK], F32, o_tmp + 4 * TOK * 4)
    h_t, _ = sb("h_t", [128, 2, TOK], F32, o_tmp + 5 * TOK * 4)
    k_more, _ = sb("k_more", [128, 2, 6, 256], F32, o_tmp)
    v_more, _ = sb("v_more", [128, 2, 6, 256], F32, o_qkvg)
    assert 2 * 6 * 256 * 4 <= 12 * TOK * 4
    o_masked, _ = sb("o_masked", [128, 2, 512], F32, o_tmp)
    h2_t, _ = sb("h2_t", [128, KT, TOK], F32, o_qkvg + 16 * TOK * 4)
    rope_t, _ = sb("rope_t", [128, 2, TOK], F32, o_tmp)
    ctok, _ = sb("ctok", [9, D], F32, o_tmp)
    c_t, _ = sb("c_t", [128, KT, 9], F32, o_tmp + 8 * TOK * 4)

    lnp, _ = sb("lnp", [128, 80])
    st6, _ = sb("st6", [128, 3, 2, 6])
    ident = cst[:, C_ID:C_ID + 128]
    ones = cst[:, C_ONE:C_ONE + 128]

    assert at[0] <= nc.sbuf_usable_end
    psum = nc.alloc_psum_tensor("psum", [128, 8, 512], F32)

    def sem(name):
        return nc.alloc_semaphore(name)

    const_in, x_in, c_in, rows_in, pages_in = sem("const_in"), sem("x_in"), sem("c_in"), sem("rows_in"), sem("pages_in")
    ln_rows_in = sem("ln_rows_in")
    raw_in = [sem(f"raw_in{i}") for i in range(RAW)]
    kv_in = [sem(f"kv_in{i}") for i in range(KV_RING)]
    tables_in, moved, masked_s, sel_done, ln1_ready = (sem(n) for n in ("tables_in", "moved", "masked_s", "sel_done", "ln1_ready"))
    stored, y_stored = sem("stored"), sem("y_stored")
    hi_ready, lo_ready, half_used = sem("hi_ready"), sem("lo_ready"), sem("half_used")
    acc_free = [sem("acc_free0"), sem("acc_free1")]
    turned_c, turned_rows, turned_x = sem("turned_c"), sem("turned_rows"), sem("turned_x")
    c_silu, c_hi, c_ready = sem("c_silu"), sem("c_hi"), sem("c_ready")
    x_ready_act, x_ready_dve = sem("x_ready_act"), sem("x_ready_dve")
    rows_ready = sem("rows_ready")
    ada_done, ada_row, ada_turned, ada_mod = sem("ada_done"), sem("ada_row"), sem("ada_turned"), sem("ada_mod")
    h_ready, h_hi, h_lo = sem("h_ready"), sem("h_hi"), sem("h_lo")
    evicted, sin_done, cos_done, roped = sem("evicted"), sem("sin_done"), sem("cos_done"), sem("roped")
    x_scaled = sem("x_scaled")
    qz_zero, qz_ready = sem("qz_zero"), sem("qz_ready")
    tok_turned, v_tok, k_tok = sem("tok_turned"), sem("v_tok"), sem("k_tok")
    kt_turned, kt_x, kt_y, scored_s = sem("kt_turned"), sem("kt_x"), sem("kt_y"), sem("scored_s")
    max_s, exp_s, prob_s = sem("max_s"), sem("exp_s"), sem("prob_s")
    probT_turned, probT_s, pv_s = sem("probT_turned"), sem("probT_s"), sem("pv_s")
    scored, maxed, exped, turned, prbT_a, prbT_b, pv_done, o_ready = (sem(n) for n in (
        "scored", "maxed", "exped", "turned", "prbT_a", "prbT_b", "pv_done", "o_ready"))
    oT_turned, oT_h, oT_l = sem("oT_turned"), sem("oT_h"), sem("oT_l")
    gates_in, sig_ready = sem("gates_in"), sem("sig_ready")
    pab_done, merged, merged_hi, merged_lo = sem("pab_done"), sem("merged"), sem("merged_hi"), sem("merged_lo")
    z_ready, mean_done, centred, squared, var_done, std_ready = (sem(n) for n in (
        "z_ready", "mean_done", "centred", "squared", "var_done", "std_ready"))
    normed, x1_ready, h2_ready, h2_hi, h2_lo, x1_scaled = (sem(n) for n in (
        "normed", "x1_ready", "h2_ready", "h2_hi", "h2_lo", "x1_scaled"))
    silu_ready, f_ready, f_hi_ready, f_lo_ready = sem("silu_ready"), sem("f_ready"), sem("f_hi_ready"), sem("f_lo_ready")
    down_done, z2_ready, z2_turned = sem("down_done"), sem("z2_ready"), sem("z2_turned")
    var2, std2, rs2, y_norm, y_done = sem("var2"), sem("std2"), sem("rs2"), sem("y_norm"), sem("y_done")
    dve_link = Count(sem("dve_link"))
    sp_past, pe_past, dve_past = sem("sp_past"), sem("pe_past"), sem("dve_past")

    def halves_of(n):
        if isinstance(n, int) and n >= DOWN0:
            c = n - DOWN0
            return 2 * DOWN0 + 11 * (c // 6) + 2 * (c % 6)
        return 2 * n

    def raw_need(n, slot):
        extra = sum(1 for m in (PAB0, PAB0 + 1) if m % RAW == slot and n >= m)
        return 16 * (n // RAW + 1 + extra)

    MIX_TRIPS = 4
    UP_PAIRS = 3
    UP_TRIPS = PAIRS // UP_PAIRS

    w_in_v = w_in.rearrange("(k p) n -> p k n", p=128)
    w_ada_v = w_ada.rearrange("(k p) n -> p k n", p=128)
    w_o_v = w_o.rearrange("(k p) n -> p k n", p=128)
    w_up_v = w_up.rearrange("(k p) n -> p k n", p=128)
    w_pa_v = w_pa.rearrange("(k p) n -> p k n", p=128)
    w_pb_v = w_pb.rearrange("(k p) n -> p k n", p=128)
    w_down_v = w_down.rearrange("(k p) n -> p k n", p=128)

    def raw8(slot):
        return raw[:, slot, :].rearrange("p (k n) -> p k n", k=8)

    def raw_half(n_static_slot, hh, by_rows):
        if by_rows:
            return raw[:, n_static_slot, 1024 * hh:1024 * hh + 1024]
        return raw8(n_static_slot)[:, :, 128 * hh:128 * hh + 128]

    def kv_tile(b, kind):
        slot = b % KV_RING
        return kvin[:, slot, :, :] if slot < 2 else (v_more if kind else k_more)[:, slot - 2, :, :]

    def part(t, slot, by_rows):
        if by_rows:
            return t[:, slot, :]
        return t[:, slot, :].rearrange("p (k n) -> p k n", k=8)

    def split_hi(act, nb, slot4, rslot, hh, need, by_rows=False):
        act.wait_ge(raw_in[rslot], need)
        if not isinstance(nb, int) or nb >= SPLIT:
            act.wait_ge(half_used, nb - SPLIT + 1)
        nc.scalar.activation(part(w_hi, slot4, by_rows), raw_half(rslot, hh, by_rows), ACT.Copy).then_inc(hi_ready, 1)

    def split_lo(dve, nb, slot4, rslot, hh, by_rows=False):
        dve.wait_ge(hi_ready, nb + 1)
        nc.vector.tensor_tensor(part(w_lo, slot4, by_rows), raw_half(rslot, hh, by_rows),
                                part(w_hi, slot4, by_rows).bitcast(F32), ALU.subtract).then_inc(lo_ready, 1)

    def halves(first, last):
        out = []
        for n in range(first, last):
            by_rows = PAB0 <= n < WO0 or n >= DOWN0
            for hh in range(1 if n >= DOWN0 and (n - DOWN0) % 6 == 5 else 2):
                nb = halves_of(n) + hh
                out.append((nb, nb % SPLIT, n % RAW, hh, by_rows, raw_need(n, n % RAW)))
        return out

    ALL = {h[0]: h for h in halves(0, DOWN0 + 12)}
    LAST = max(ALL)

    def hi_static(act, nb):
        if nb in ALL:
            _, s, r, hh, by, need = ALL[nb]
            split_hi(act, nb, s, r, hh, need, by)

    def lo_static(dve, nb):
        if nb in ALL:
            _, s, r, hh, by, need = ALL[nb]
            split_lo(dve, nb, s, r, hh, by)

    AHEAD = SPLIT

    block = ctx.enter_context(nc.Block())

    @block.sync
    def _(sp):
        sp.dma_start(cst[:, 0:C_COS], const[:, 0:C_COS]).then_inc(const_in, 16)
        sp.dma_start(ctok[0:1, :], c_prompt).then_inc(c_in, 16)
        sp.dma_start(ctok[1:9, :], c_sample).then_inc(c_in, 16)
        sp.dma_start(rows[0:48, :], b_ada.rearrange("a (j p) -> (a j) p", p=128)).then_inc(rows_in, 16)
        sp.dma_start(rows[48:56, :], ln1_g.rearrange("a (j p) -> (a j) p", p=128)).then_inc(rows_in, 16)
        sp.dma_start(rows[56:64, :], ln1_b.rearrange("a (j p) -> (a j) p", p=128)).then_inc(rows_in, 16)
        sp.dma_start(pages[:], page_table.rearrange("b n -> (b n)").unsqueeze(0)).then_inc(pages_in, 16)

        def load(n, slot, src, dst, first_use):
            if not first_use:
                sp.wait_ge(lo_ready, halves_of(n - RAW + 1))
            sp.dma_start(dst, src).then_inc(raw_in[slot], 16)

        for n in range(MIX0):
            load(n, n % RAW, w_ada_v[:, :, 256 * n:256 * n + 256], raw8(n % RAW), n < RAW)
            if n == 3:
                sp.dma_start(x_tok[:, 0:2, :], x_prompt.rearrange("a (t p) d -> p (a t) d", p=128)).then_inc(x_in, 16)
                sp.dma_start(x_tok[0:SAMPLE, 2, :], x_sample.rearrange("b t d -> (b t) d")).then_inc(x_in, 16)

        sp.dma_start(cst[:, C_COS:C_END], const[:, C_COS:C_END]).then_inc(tables_in, 16)

        with sp.Fori(0, MIX_TRIPS) as i:
            for k in range(6):
                col = sp.snap((i * 3 + (k // 2 if k % 2 == 0 else N_ADA0 + k // 2)) * 256)
                sp.wait_ge(lo_ready, i * 12 + 2 * (MIX0 + k - RAW + 1))
                sp.sem_inc(sp_past, 1)
                src = (w_in_v if k % 2 == 0 else w_ada_v)[:, :, bass.ds(col, 256)]
                sp.dma_start(raw8((MIX0 + k) % RAW), src).then_inc(raw_in[(MIX0 + k) % RAW], 16)
        def load_kv(b, kind):
            dst, s = kv_tile(b, kind), kv_in[b % KV_RING]
            sp.dma_start(dst[:, 0, :], cache_a[0][b, :, kind, :]).then_inc(s, 16)
            sp.dma_start(dst[:, 1:3, :], cache_a[1][b, :, kind, :].rearrange("(n p) c -> p n c", p=128)).then_inc(s, 16)
            src = cache_a[2][b, :, kind, :].rearrange("(g r) c -> g r c", r=16)[:, 0:4, :]
            sp.dma_start(dst[0:64, 5, :], src).then_inc(s, 16)
            for j in range(N_PAGES):
                page = sp.value_load(pages[0:1, N_PAGES * b + j:N_PAGES * b + j + 1], min_val=0, max_val=cache_b.shape[0] - 1)
                sp.dma_start(dst[:, 3 + j, :], cache_b[bass.ds(page, 1), :, kind, :].rearrange("a p c -> (a p) c")).then_inc(s, 16)

        def load_static(n):
            if n < PAB0:
                col = 3072 + 256 * (n - GATE0)
                load(n, n % RAW, w_in_v[:, :, col:col + 256], raw8(n % RAW), False)
            elif n < WO0:
                j = n - PAB0
                dst = raw[:, n % RAW, :].rearrange("p (k n) -> p k n", k=4)
                load(n, n % RAW, w_pa_v[:, :, 512 * j:512 * j + 512], dst[:, 0:2, :], False)
                sp.dma_start(dst[:, 2:4, :], w_pb_v[:, :, 512 * j:512 * j + 512]).then_inc(raw_in[n % RAW], 16)
            elif n < ADA2:
                j = n - WO0
                load(n, n % RAW, w_o_v[:, :, 256 * j:256 * j + 256], raw8(n % RAW), False)
            else:
                j = 20 + n - ADA2
                load(n, n % RAW, w_ada_v[:, :, 256 * j:256 * j + 256], raw8(n % RAW), False)

        sp.wait_ge(pages_in, 16)
        for b in range(2):
            load_kv(b, 0)
        for n in range(GATE0, GATE0 + 5):
            load_static(n)
        sp.wait_ge(roped, 16)
        for b in range(2, DEC_B):
            if b >= KV_RING:
                sp.wait_ge(kt_turned, 2 * (b - KV_RING) + 2)
            load_kv(b, 0)
        for b in range(2):
            sp.wait_ge(kt_turned, 2 * (KV_RING + b) + 2)
            load_kv(b, 1)
        for n in range(GATE0 + 5, WO0):
            load_static(n)
            if n == PAB0 - 1:
                sp.wait_ge(scored, 8)
                load_kv(2, 1)
                load_kv(3, 1)
        for n in range(WO0, WO0 + 3):
            load_static(n)
        for b in range(KV_RING, DEC_B):
            sp.wait_ge(pv_s, b - KV_RING + 1)
            load_kv(b, 1)
        for n in range(WO0 + 3, UP0):
            load_static(n)
        with sp.Fori(0, UP_TRIPS) as i:
            for k in range(6):
                n = UP0 + k
                col = sp.snap((i * 3 + k // 2) * 256 + (D_FF if k % 2 == 0 else 0))
                sp.wait_ge(lo_ready, i * 12 + 2 * (n - RAW + 1))
                sp.sem_inc(sp_past, 1)
                sp.dma_start(raw8(n % RAW), w_up_v[:, :, bass.ds(col, 256)]).then_inc(raw_in[n % RAW], 16)
        for n in range(UP0 + 6 * UP_TRIPS, DOWN0):
            k = n - UP0
            col = (k // 2) * 256 + (D_FF if k % 2 == 0 else 0)
            load(n, n % RAW, w_up_v[:, :, col:col + 256], raw8(n % RAW), False)
        for n in range(DOWN0, DOWN0 + 12):
            c, hcol = (n - DOWN0) % 6, (n - DOWN0) // 6
            nk = min(4, FT - 4 * c)
            dst = raw[:, n % RAW, 0:512 * nk].rearrange("p (k n) -> p k n", k=nk)
            load(n, n % RAW, w_down_v[:, 4 * c:4 * c + nk, 512 * hcol:512 * hcol + 512], dst, False)
        for t in range(3):
            rows_n = 128 if t < 2 else SAMPLE
            sp.wait_ge(y_done, t + 1)
            dst = y_prompt[0, 128 * t:128 * t + 128, :] if t < 2 else y_sample.rearrange("b t d -> (b t) d")
            sp.dma_start(dst, y_tok[0:rows_n, t, :]).then_inc(y_stored, 16)
        sp.wait_ge(y_stored, 16 * 3)
        sp.wait_ge(stored, 16 * N_POOL_STORES)
        sp.wait_ge(moved, 16 * 3 * DEC_B)

    def mm3(out, hi_l, lo_l, hi_r, lo_r, start, stop):
        nc.tensor.matmul(out, hi_l, hi_r, start=start, stop=False, skip_group_check=True)
        nc.tensor.matmul(out, hi_l, lo_r, start=False, stop=False, skip_group_check=True)
        return nc.tensor.matmul(out, lo_l, hi_r, start=False, stop=stop, skip_group_check=True)

    def unit_mm(pe, nb, slot, bank, rhs_ready=None):
        pe.wait_ge(lo_ready, nb + 1)
        wh, wl = part(w_hi, slot, False), part(w_lo, slot, False)
        for k in range(KT):
            if rhs_ready is not None:
                pe.wait_ge(rhs_ready, k + 1)
            mm = mm3(psum[:, bank, 0:TOK], wh[:, k, :], wl[:, k, :], act_hi[:, k, :], act_lo[:, k, :], k == 0, k == KT - 1)
        mm.then_inc(half_used, 1)

    def ada_mm(pe, nb, slot, bank, hh):
        pe.wait_ge(lo_ready, nb + 1)
        wh, wl = part(w_hi, slot, False), part(w_lo, slot, False)
        out = psum[0:18, bank, 128 * hh:128 * hh + 128]
        for k in range(KT):
            nc.tensor.matmul(out, c_hl[:, k, :], wh[:, k, :], start=(k == 0), stop=False, skip_group_check=True)
            mm = nc.tensor.matmul(out, c_hl[:, k, :], wl[:, k, :], start=False, stop=(k == KT - 1), skip_group_check=True)
        mm.then_inc(half_used, 1)

    def ada_turn(pe, a, bank, slot):
        pe.wait_ge(ada_row, a + 1)
        pe.sem_inc(pe_past, 1)
        for hh in range(2):
            mm = nc.tensor.transpose(psum[:, bank, 256 + 18 * hh:256 + 18 * hh + 18],
                                     rowbuf[:, slot, 128 * hh:128 * hh + 128], cst[0:18, 0:18])
        mm.then_inc(ada_turned, 1)

    def kv_pieces():
        return [(0, 128, 0), (1, 128, 160), (2, 128, 288), (5, 64, 448), (3, 128, 544), (4, 128, 672)]

    @block.tensor
    def _(pe):
        pe.wait_ge(const_in, 16)
        pe.wait_ge(c_in, 32)
        for k in range(KT):
            mm = nc.tensor.transpose(psum[:, 0, 9 * k:9 * k + 9], ctok[:, 128 * k:128 * k + 128], cst[0:9, 0:9])
        mm.then_inc(turned_c, 1)
        pe.wait_ge(rows_in, 48)
        nc.tensor.transpose(psum[:, 1, 0:64], rows[:, :], cst[0:64, 0:64]).then_inc(turned_rows, 1)
        def turn_x():
            pe.wait_ge(x_in, 32)
            for t in range(2):
                for k in range(KT):
                    mm = nc.tensor.transpose(psum[:, 1 + 2 * t + k // 4, 128 * (k % 4):128 * (k % 4) + 128],
                                             x_tok[:, t, 128 * k:128 * k + 128], ident)
                    if k % 4 == 3:
                        mm.then_inc(turned_x, 1)
            for k in range(KT):
                mm = nc.tensor.transpose(psum[:, 0, SAMPLE * k:SAMPLE * k + SAMPLE],
                                         x_tok[0:SAMPLE, 2, 128 * k:128 * k + 128], cst[0:SAMPLE, 0:SAMPLE])
            mm.then_inc(turned_x, 1)

        pe.wait_ge(c_ready, 1)
        for a in range(N_ADA0):
            if a >= 3:
                pe.wait_ge(ada_mod, a - 2)
            for hh in range(2):
                ada_mm(pe, 2 * a + hh, (2 * a + hh) % SPLIT, 5 + a % 3, hh)
            if a >= 1:
                ada_turn(pe, a - 1, 5 + (a - 1) % 3, (a - 1) % 3)
            if a == 4:
                pe.wait_ge(rows_ready, 1)
                turn_x()
        ada_turn(pe, N_ADA0 - 1, 5 + (N_ADA0 - 1) % 3, (N_ADA0 - 1) % 3)

        def mix(i, first=False):
            for k in range(6):
                nb0 = i * 12 + 2 * (MIX0 + k)
                for hh in range(2):
                    slot = (2 * k + hh) % SPLIT
                    if k % 2 == 0:
                        u = i * 6 + (k + hh)
                        if not (first and k == 0):
                            pe.wait_ge(acc_free[hh], i * 3 + k // 2)
                        unit_mm(pe, nb0 + hh, slot, hh, h_lo if first and k == 0 and hh == 0 else None)
                    else:
                        a = i * 3 + (N_ADA0 + k // 2)
                        bank = (N_ADA0 + k // 2) % 3
                        if hh == 0:
                            pe.wait_ge(ada_mod, a - 2)
                        ada_mm(pe, nb0 + hh, slot, 5 + bank, hh)
                if k % 2 == 0 and k >= 2:
                    ada_turn(pe, i * 3 + (N_ADA0 + k // 2 - 1), 5 + (N_ADA0 + k // 2 - 1) % 3, (N_ADA0 + k // 2 - 1) % 3)
            ada_turn(pe, i * 3 + (N_ADA0 + 2), 5 + (N_ADA0 + 2) % 3, (N_ADA0 + 2) % 3)

        mix(0, True)
        with pe.Fori(1, MIX_TRIPS) as i:
            mix(i)

        pe.wait_ge(ada_mod, N_ADA0 + 12)
        for j in range(8):
            g, hp = j // 2, j % 2
            for kind in range(2):
                bank = 2 + (j % 2) * 2 + kind
                if kind == 0:
                    pe.wait_ge(acc_free[hp], v_blk(g, hp) // 2 + 1)
                    if j >= 2:
                        pe.wait_ge(v_tok, j - 1)
                else:
                    pe.wait_ge(roped, k_blk(g, hp) + 1 if g < 3 else 15 + hp)
                    if j >= 2:
                        pe.wait_ge(k_tok, j - 1)
                blk = (v_blk if kind == 0 else k_blk)(g, hp)
                for t in range(2):
                    nc.tensor.transpose(psum[:, bank, 128 * t:128 * t + 128], qkvg[:, blk, 128 * t:128 * t + 128], ident)
                nc.tensor.transpose(psum[0:SAMPLE, bank, 256:384], qkvg[:, blk, PROMPT:TOK], ident).then_inc(tok_turned, 1)

        pe.wait_ge(v_tok, 8)
        pe.wait_ge(k_tok, 8)
        pe.wait_ge(qz_ready, 1)

        def keys_turn(idx):
            b, hp = idx // 2, idx % 2
            if hp == 0:
                pe.wait_ge(kv_in[b % KV_RING], 16 * KV_LOADS * (b // KV_RING + 1))
            if idx >= 2:
                pe.wait_ge(kt_x, idx - 1)
                pe.wait_ge(kt_y, idx - 1)
            for n, (tile, nr, _) in enumerate(kv_pieces()):
                bank = 4 + 2 * hp + (n >= 3)
                col = 128 * n if n < 3 else (0, 64, 192)[n - 3]
                mm = nc.tensor.transpose(psum[:, bank, col:col + nr], kv_tile(b, 0)[0:nr, tile, 128 * hp:128 * hp + 128],
                                         cst[0:nr, 0:nr])
            mm.then_inc(kt_turned, 1)

        def sample_scores(idx):
            b, hp = idx // 2, idx % 2
            pe.wait_ge(kt_x, idx + 1)
            pe.wait_ge(kt_y, idx + 1)
            r0, half = 32 * (b % 4), b // 4
            for g, (c0, n, bank, o0) in enumerate(((0, 160, 2, 0), (160, 288, 2, 160), (448, 96, 3, 0), (544, 288, 3, 96))):
                w = qz[:, g, hp, b % 4, 16 * half:16 * half + 32]
                mm = nc.tensor.matmul(psum[r0:r0 + 32, bank, o0:o0 + n], w, kT[:, hp, c0:c0 + n],
                                      start=(half == 0 and hp == 0 and g in (0, 2)), stop=(half == 1 and hp == 1),
                                      skip_group_check=True)
            mm.then_inc(scored_s, 1)

        for idx in range(2 * DEC_B + 1):
            if idx < 2 * DEC_B:
                keys_turn(idx)
            if idx >= 1:
                sample_scores(idx - 1)

        def sample_probs_turn():
            pe.wait_ge(prob_s, 2)
            for n, (c0, nc_) in enumerate(S_PIECES):
                mm = nc.tensor.transpose(psum[0:nc_, 4 + n // 4, 128 * (n % 4):128 * (n % 4) + 128],
                                         s_prb[:, c0:c0 + nc_], ident)
                if n in (3, 7, 9):
                    mm.then_inc(probT_turned, 1)

        def sample_values(b):
            if b == 0:
                for g in range(4):
                    for half in range(2):
                        nc.tensor.matmul(psum[:, g // 3, 256 * half:256 * half + 256], s_prbT[0:SAMPLE, 6 + g, :],
                                         tok[0:SAMPLE, 2, 1, 256 * g:256 * g + 256], start=(g in (0, 3) and half == 0),
                                         stop=False, skip_group_check=True)
            q, half = b % 4, b // 4
            pe.wait_ge(kv_in[b % KV_RING], 16 * KV_LOADS * ((DEC_B + b) // KV_RING + 1))
            for n, (tile, nr, br) in enumerate(((0, 128, 0), (1, 128, 0), (2, 128, 0), (5, 64, 0), (3, 128, 1), (4, 128, 1))):
                mm = nc.tensor.matmul(psum[32 * q:32 * q + 32, br, 256 * half:256 * half + 256],
                                      s_prbT[0:nr, n, 32 * q:32 * q + 32], kv_tile(b, 1)[0:nr, tile, :],
                                      start=False, stop=(half == 1), skip_group_check=True)
            mm.then_inc(pv_s, 1)

        def prompt_scores(u):
            br, t, h = UNITS[u]
            if u >= 1:
                pe.wait_ge(maxed, u)
            nk = 128 * (t + 1)
            p0 = E * (h % 2)
            for j, g in enumerate((0, 1, 2) if br == 0 else (3,)):
                c0 = j * nk
                mm = nc.tensor.matmul(psum[:, 2 + c0 // 512, c0 % 512:c0 % 512 + nk],
                                      qkvg[p0:p0 + E, q_blk(g, h // 2), 128 * t:128 * t + 128],
                                      qkvg[p0:p0 + E, k_blk(g, h // 2), 0:nk], start=True, stop=True,
                                      skip_group_check=True)
            mm.then_inc(scored, 1)

        def prompt_turn(u):
            br, t, h = UNITS[u]
            pe.wait_ge(exped, u + 1)
            if u == 0:
                pe.wait_ge(probT_s, 2)
            else:
                pe.wait_ge(prbT_a, u)
                pe.wait_ge(prbT_b, min(u, 4))
            nb_ = (3 if br == 0 else 1) * (t + 1)
            for n in range(nb_):
                mm = nc.tensor.transpose(psum[:, 4 + n // 4, 128 * (n % 4):128 * (n % 4) + 128],
                                         prb[:, u % 2, 128 * n:128 * n + 128], ident)
            mm.then_inc(turned, 1)

        def prompt_values(u):
            br, t, h = UNITS[u]
            pe.wait_ge(prbT_a, u + 1)
            pe.wait_ge(prbT_b, min(u + 1, 4))
            if u >= 1:
                pe.wait_ge(o_ready, u)
            nkb = t + 1
            steps = [(j, g, kb) for j, g in enumerate((0, 1, 2) if br == 0 else (3,)) for kb in range(nkb)]
            for n, (j, g, kb) in enumerate(steps):
                mm = nc.tensor.matmul(psum[:, 6, 0:E], prbT[:, u % 2, 128 * (j * nkb + kb):128 * (j * nkb + kb) + 128],
                                      tok[:, kb, 1, 256 * g + E * h:256 * g + E * h + E],
                                      start=(n == 0), stop=(n == len(steps) - 1))
            mm.then_inc(pv_done, 1)

        for s in range(20):
            if s < 16:
                u = 24 + s
                pe.wait_ge(acc_free[s % 2], u // 2)
                unit_mm(pe, 2 * GATE0 + s, s % SPLIT, s % 2)
            if s == 2:
                sample_probs_turn()
            if 2 <= s < 18:
                prompt_scores(s - 2)
            if 3 <= s < 19:
                prompt_turn(s - 3)
            if s >= 4:
                prompt_values(s - 4)
            if s == 16:
                pe.wait_ge(acc_free[0], 20)
                pe.wait_ge(acc_free[1], 20)
            if s >= 16:
                sample_values(s - 16)

        pe.wait_ge(o_ready, 16)
        for t in range(2):
            for f in range(4):
                mm = nc.tensor.transpose(psum[:, 2 + t, 128 * f:128 * f + 128],
                                         o_tokens[:, t, f // 2, 128 * (f % 2):128 * (f % 2) + 128], ident)
            mm.then_inc(oT_turned, 1)
        for b in range(4, DEC_B):
            sample_values(b)
        pe.wait_ge(masked_s, 2)
        for f in range(4):
            for half in range(2):
                mm = nc.tensor.matmul(psum[:, 4, SAMPLE * f:SAMPLE * f + SAMPLE],
                                      o_masked[:, f // 2, 256 * half + 128 * (f % 2):256 * half + 128 * (f % 2) + 128],
                                      cst[:, C_SEL:C_SEL + SAMPLE], start=(f == 0 and half == 0), stop=(half == 1),
                                      skip_group_check=True)
        mm.then_inc(sel_done, 1)
        pe.wait_ge(oT_l, 3)

        for h in range(4):
            nb = 2 * PAB0 + h
            pe.wait_ge(lo_ready, nb + 1)
            wh, wl = w_hi[:, nb % SPLIT, :], w_lo[:, nb % SPLIT, :]
            for m in range(4):
                u = 40 + 4 * h + m
                pe.wait_ge(acc_free[u % 2], u // 2)
                for k in range(2):
                    c = 512 * k + 128 * m
                    mm = mm3(psum[:, u % 2, 0:TOK], wh[:, c:c + 128], wl[:, c:c + 128],
                             oT_hi[:, 2 * (h % 2) + k, :], oT_lo[:, 2 * (h % 2) + k, :], k == 0, k == 1)
                mm.then_inc(half_used if m == 3 else pab_done, 1)

        def mean(m):
            pe.wait_ge(z_ready, m + 1)
            mm = nc.tensor.matmul(psum[:, 2, 0:TOK], ones, xT[:, m, :], start=(m == 0), stop=(m == KT - 1))
            mm.then_inc(mean_done, 1)

        for m in range(KT):
            u = 56 + m
            if m < 2:
                pe.wait_ge(acc_free[u % 2], u // 2)
            else:
                pe.wait_ge(z_ready, m - 1)
            unit_mm(pe, 2 * WO0 + m, (2 * WO0 + m) % SPLIT, u % 2, merged_lo if m == 0 else None)
            if m >= 1:
                mean(m - 1)
        mean(KT - 1)
        for j in range(4):
            a = 20 + j
            for hh in range(2):
                nb = 2 * (ADA2 + j) + hh
                if hh == 0 and j == 3:
                    pe.wait_ge(ada_mod, a - 2)
                ada_mm(pe, nb, nb % SPLIT, 5 + a % 3, hh)
            if j >= 1:
                ada_turn(pe, a - 1, 5 + (a - 1) % 3, (a - 1) % 3)
            if j == 1:
                for m in range(KT):
                    if m % 4 == 0:
                        pe.wait_ge(squared, m // 4 + 1)
                    mm = nc.tensor.matmul(psum[:, 3, 0:TOK], ones, qkvg[:, 8 + m, :], start=(m == 0), stop=(m == KT - 1))
                mm.then_inc(var_done, 1)
        ada_turn(pe, 23, 5 + 23 % 3, 23 % 3)

        def up_pair(j, first=False):
            for q in range(4):
                nb = j * 4 + (2 * UP0 + q)
                if q < 2 and first:
                    pe.wait_ge(z_ready, KT)
                elif q < 2:
                    pe.wait_ge(f_ready, j * 2 + (q - 1))
                else:
                    pe.wait_ge(silu_ready, j * 2 + (q - 1))
                unit_mm(pe, nb, q, q % 2, h2_lo if first and q == 0 else None)

        up_pair(0, True)
        up_pair(1)
        up_pair(2)
        with pe.Fori(1, UP_TRIPS) as i:
            for k in range(UP_PAIRS):
                up_pair(i * 3 + k)
        for j in range(UP_PAIRS * UP_TRIPS, PAIRS):
            up_pair(j)

        def z2_turn(m):
            pe.wait_ge(z2_ready, 4 * (m // 4 + 1))
            for t in range(3):
                nt = 128 if t < 2 else SAMPLE
                mm = nc.tensor.transpose(psum[0:nt, t + 3 * (m // 4), 128 * (m % 4):128 * (m % 4) + 128],
                                         xT[:, m, 128 * t:128 * t + nt], ident)
            mm.then_inc(z2_turned, 1)

        for hcol in range(2):
            for kk in range(0, FT, 2):
                nb = 2 * DOWN0 + 11 * hcol + kk // 2
                pe.wait_ge(lo_ready, nb + 1)
                wh, wl = w_hi[:, nb % SPLIT, :], w_lo[:, nb % SPLIT, :]
                if hcol == 0:
                    pe.wait_ge(f_lo_ready, kk // 2 + 1)
                if hcol == 0 and kk == 0:
                    pe.wait_ge(f_ready, 2 * PAIRS)
                if hcol == 1 and kk == 0:
                    pe.wait_ge(ada_mod, 24)
                for m in range(4):
                    for k in range(2):
                        c = 512 * k + 128 * m
                        mm = mm3(psum[:, 4 * hcol + m, 0:TOK], wh[:, c:c + 128], wl[:, c:c + 128],
                                 f_hi[:, kk + k, :], f_lo[:, kk + k, :], kk + k == 0, kk + k == FT - 1)
                    if m == 3:
                        mm.then_inc(half_used, 1)
                    elif kk == FT - 2:
                        mm.then_inc(down_done, 1)
                if hcol == 1 and kk == 4:
                    for m in range(4):
                        z2_turn(m)
        for m in range(4, 8):
            z2_turn(m)

    @block.scalar
    def _(act):
        act.wait_ge(turned_c, 1)
        nc.scalar.activation(c_t[:], psum[:, 0, 0:72].rearrange("p (k c) -> p k c", c=9), ACT.Silu).then_inc(c_silu, 1)
        act.wait_ge(c_silu, 1)
        nc.scalar.activation(c_hl[:, :, 0:9], c_t[:], ACT.Copy).then_inc(c_hi, 1)
        for nb in range(AHEAD):
            hi_static(act, nb)

        def ada_rows(a, bank, slot, used):
            act.wait_ge(half_used, used)
            nc.scalar.activation(rowbuf[:, slot, :], psum[0:18, bank, 0:256], ACT.Copy).then_inc(ada_row, 1)

        for a in range(N_ADA0):
            hi_static(act, 2 * a + AHEAD)
            ada_rows(a, 5 + a % 3, a % 3, 2 * a + 2)
            hi_static(act, 2 * a + 1 + AHEAD)
            if a == 5:
                for j in range(2):
                    act.wait_ge(turned_x, j + 1)
                    nc.scalar.activation(xT[:, 4 * j:4 * j + 4, 0:128], psum[:, 1 + j, :].rearrange("p (k c) -> p k c", c=128),
                                         ACT.Copy).then_inc(x_ready_act, 1)
        for k in range(KT):
            act.wait_ge(h_ready, k + 1)
            nc.scalar.activation(act_hi[:, k, :], qkvg[:, k, :], ACT.Copy).then_inc(h_hi, 1)

        def mix(i, kinds):
            for k in range(6):
                nb0 = i * 12 + 2 * (MIX0 + k)
                for hh in range(2):
                    nb = nb0 + hh
                    if k % 2 == 0 and kinds[k // 2]:
                        act.wait_ge(half_used, nb + 1)
                        blk = i * 6 + (k + hh)
                        nc.scalar.activation(block_at(qkvg, blk), psum[:, hh, 0:TOK], ACT.Copy).then_inc(evicted, 1)
                    elif k % 2 == 1 and hh == 1:
                        a8 = N_ADA0 + k // 2
                        ada_rows(None, 5 + a8 % 3, a8 % 3, nb + 1)
                    kk = k + 2
                    rslot = (MIX0 + kk) % RAW
                    split_hi(act, nb + AHEAD, (2 * k + hh) % SPLIT, rslot, hh, (i * 2 + ((MIX0 + kk) // RAW + 1)) * 16)

        with act.Fori(0, 2) as i:
            mix(i, (True, True, True))
        mix(2, (False, False, False))
        mix(3, (True, True, False))

        for j in range(8):
            act.wait_ge(tok_turned, 2 * j + 1)
            bank = 2 + (j % 2) * 2
            nc.scalar.activation(tok[:, 0:2, 1, 128 * j:128 * j + 128],
                                 psum[:, bank, 0:256].rearrange("p (t c) -> p t c", t=2), ACT.Copy)
            nc.scalar.activation(tok[0:SAMPLE, 2, 1, 128 * j:128 * j + 128], psum[0:SAMPLE, bank, 256:384],
                                 ACT.Copy).then_inc(v_tok, 1)
        for idx in range(2 * DEC_B):
            b, hp = idx // 2, idx % 2
            act.wait_ge(kt_turned, idx + 1)
            if idx >= 2:
                act.wait_ge(scored_s, idx - 1)
            nc.scalar.activation(kT[:, hp, 0:128], psum[:, 4 + 2 * hp, 0:128], ACT.Copy)
            nc.scalar.activation(kT[:, hp, 160:416], psum[:, 4 + 2 * hp, 128:384], ACT.Copy).then_inc(kt_x, 1)
        for br, (c0, c1) in enumerate(((0, 544), (544, 832))):
            act.wait_ge(max_s, br + 1)
            nc.scalar.activation(s_prb[:, c0:c1], s_msk[:, c0:c1], ACT.Exp, bias=small[:, 4 + br:5 + br], scale=SCALE,
                                 accum_out=small[:, 6 + br:7 + br]).then_inc(exp_s, 1)

        def softmax_exp(u):
            br, t, h = UNITS[u]
            act.wait_ge(maxed, u + 1)
            if u >= 2:
                act.wait_ge(turned, u - 1)
            if u == 0:
                act.wait_ge(probT_turned, 3)
            n = (3 if br == 0 else 1) * 128 * (t + 1)
            nc.scalar.activation(prb[:, u % 2, 0:n], msk[:, 0:n], ACT.Exp, bias=small[:, 16 + u:17 + u], scale=SCALE,
                                 accum_out=small[:, 32 + u:33 + u]).then_inc(exped, 1)

        def prbT_copy(u):
            br, t, h = UNITS[u]
            act.wait_ge(turned, u + 1)
            if u >= 2:
                act.wait_ge(pv_done, u - 1)
            n = min(4, (3 if br == 0 else 1) * (t + 1)) * 128
            nc.scalar.activation(prbT[:, u % 2, 0:n], psum[:, 4, 0:n], ACT.Copy).then_inc(prbT_a, 1)

        for s in range(20):
            if s < 16:
                act.wait_ge(half_used, 2 * GATE0 + s + 1)
                if s == 8:
                    act.wait_ge(tok_turned, 16)
                nc.scalar.activation(qkvg[:, gate_slot(s), :], psum[:, s % 2, 0:TOK], ACT.Copy).then_inc(acc_free[s % 2], 1)
                hi_static(act, 2 * GATE0 + s + AHEAD)
            if s == 2:
                for n0, n1, rows_n, turned_n in ((0, 3, 128, 1), (3, 4, 64, 1), (4, 6, 128, 2), (6, 8, SAMPLE, 2), (8, 10, SAMPLE, 3)):
                    act.wait_ge(probT_turned, turned_n)
                    c0 = 128 * (n0 % 4)
                    src = psum[0:rows_n, 4 + n0 // 4, c0:c0 + 128 * (n1 - n0)].rearrange("p (k c) -> p k c", c=128)
                    ins = nc.scalar.activation(s_prbT[0:rows_n, n0:n1, :], src, ACT.Copy)
                    if n1 in (8, 10):
                        ins.then_inc(probT_s, 1)
            if 2 <= s < 18:
                softmax_exp(s - 2)
            if 3 <= s < 19:
                prbT_copy(s - 3)
        act.wait_ge(acc_free[1], 20)
        act.wait_ge(acc_free[0], 20)
        for c0, c1 in ((24, 32), (12, 18), (22, 24)):
            nc.scalar.activation(qkvg[:, c0:c1, :], qkvg[:, c0:c1, :], ACT.Sigmoid).then_inc(sig_ready, 1)
        for t in range(2):
            act.wait_ge(oT_turned, t + 1)
            nc.scalar.activation(oT_hi[:, :, 128 * t:128 * t + 128], psum[:, 2 + t, :].rearrange("p (k c) -> p k c", c=128),
                                 ACT.Copy).then_inc(oT_h, 1)
        act.wait_ge(sel_done, 1)
        nc.scalar.activation(oT_hi[:, :, PROMPT:TOK], psum[:, 4, 0:4 * SAMPLE].rearrange("p (k c) -> p k c", c=SAMPLE),
                             ACT.Copy).then_inc(oT_h, 1)
        for h in range(4):
            hi_static(act, 2 * PAB0 + h + AHEAD)
            if h % 2 == 0:
                for m in range(2 * h, 2 * h + 4):
                    act.wait_ge(merged, m + 1)
                    nc.scalar.activation(act_hi[:, m, :], qkvg[:, m, :], ACT.Copy).then_inc(merged_hi, 1)
        for m in range(KT):
            hi_static(act, 2 * WO0 + m + AHEAD)
        for j in range(2):
            act.wait_ge(centred, j + 1)
            nc.scalar.activation(qkvg[:, 8 + 4 * j:12 + 4 * j, :], xT[:, 4 * j:4 * j + 4, :], ACT.Square).then_inc(squared, 1)
        ada_rows(20, 5 + 20 % 3, 20 % 3, 2 * ADA2 + 2)
        hi_static(act, 2 * ADA2 + AHEAD)
        hi_static(act, 2 * ADA2 + 1 + AHEAD)
        nc.scalar.activation(small[:, 70:71], cst[:, C_EPS:C_EPS + 1], ACT.Sqrt)
        act.wait_ge(var_done, 1)
        nc.scalar.activation(rstd[:], psum[:, 3, 0:TOK], ACT.Sqrt, bias=cst[:, C_EPS:C_EPS + 1]).then_inc(std_ready, 1)
        for j in range(1, 3):
            ada_rows(20 + j, 5 + (20 + j) % 3, (20 + j) % 3, 2 * (ADA2 + j) + 2)
        for m in range(KT):
            act.wait_ge(h2_ready, m + 1)
            nc.scalar.activation(act_hi[:, m, :], h2_t[:, m, :], ACT.Copy).then_inc(h2_hi, 1)
            if m < 6:
                hi_static(act, 2 * ADA2 + 2 + AHEAD + m)
            if m == 3:
                ada_rows(23, 5 + 23 % 3, 23 % 3, 2 * (ADA2 + 3) + 2)
        for m in range(KT):
            nc.scalar.activation(xT[:, m, :], xT[:, m, :], ACT.Identity, bias=lnp[:, 72 + m:73 + m],
                                 scale=lnp[:, 64 + m:65 + m]).then_inc(x1_ready, 1)

        def up_pair(j, k, i):
            for q in range(4):
                nb = j * 4 + (2 * UP0 + q)
                if q < 2:
                    act.wait_ge(half_used, nb + 1)
                    if not isinstance(j, int) or j >= 1:
                        act.wait_ge(f_ready, j * 2 + (q - 1))
                    nc.scalar.activation(silu_t[:, q, :], psum[:, q, 0:TOK], ACT.Silu).then_inc(silu_ready, 1)
                if isinstance(j, int):
                    hi_static(act, nb + AHEAD)
                else:
                    n2 = UP0 + 2 * k + 2 + q // 2
                    split_hi(act, nb + AHEAD, q, n2 % RAW, q % 2, (i * 2 + raw_need(n2, n2 % RAW) // 16) * 16)
                if q >= 2:
                    fi = j * 2 + (q - 2)
                    act.wait_ge(f_ready, fi + 1)
                    nc.scalar.activation(block_at(f_hi, fi), f_t[:, q - 2, :], ACT.Copy).then_inc(f_hi_ready, 1)

        for j in range(3):
            up_pair(j, j, 0)
        with act.Fori(1, UP_TRIPS) as i:
            for k in range(UP_PAIRS):
                up_pair(i * 3 + k, k, i)
        for j in range(UP_PAIRS * UP_TRIPS, PAIRS):
            up_pair(j, 0, 0)
        for nb in range(2 * DOWN0, LAST + 1):
            hi_static(act, nb + AHEAD)
        for t in range(3):
            nt = 128 if t < 2 else SAMPLE
            act.wait_ge(var2, t + 1)
            nc.scalar.activation(small[0:nt, 60 + t:61 + t], small[0:nt, 51 + 2 * t:52 + 2 * t], ACT.Sqrt,
                                 bias=cst[0:nt, C_EPS:C_EPS + 1]).then_inc(std2, 1)
        act.wait_ge(ln_rows_in, 32)
        for t in range(3):
            nt = 128 if t < 2 else SAMPLE
            act.wait_ge(rs2, t + 1)
            for hcol in range(2):
                nc.scalar.activation(y_tok[0:nt, t, 512 * hcol:512 * hcol + 512], psum[0:nt, t + 3 * hcol, :], ACT.Identity,
                                     bias=small[0:nt, 66 + t:67 + t], scale=small[0:nt, 63 + t:64 + t]).then_inc(y_norm, 1)

    @block.vector
    def _(dve):
        V = nc.vector

        def link(ins):
            dve_link.up(ins)
            dve.wait_ge(dve_link.sem, dve_link.n)

        dve.wait_ge(c_hi, 1)
        V.tensor_tensor(c_hl[:, :, 9:18], c_t[:], c_hl[:, :, 0:9].bitcast(F32), ALU.subtract).then_inc(c_ready, 1)
        dve.wait_ge(turned_rows, 1)
        V.tensor_copy(lnp[:, 0:64], psum[:, 1, 0:64]).then_inc(rows_ready, 1)
        for nb in range(AHEAD):
            lo_static(dve, nb)
        dve.wait_ge(rows_ready, 1)
        V.tensor_scalar(lnp[:, 64:80], lnp[:, 48:64], ALPHA, None, ALU.mult).then_inc(ln1_ready, 1)

        def ada_add(a, bank):
            dve.wait_ge(ada_turned, a + 1)
            dst = mod[:, 2 * a:2 * a + 2, :] if isinstance(a, int) else mod[:, bass.ds(a * 2, 2), :]
            src = psum[:, bank, 256:292].rearrange("p (k h c) -> p k c h", k=2, h=2)
            V.tensor_reduce(dst, src, mybir.AxisListType.X, ALU.add).then_inc(ada_mod, 1)

        def add_bias(b0, b1, a_done):
            dve.wait_ge(ada_mod, a_done)
            link(V.tensor_tensor(mod[:, b0:b1, :], mod[:, b0:b1, :],
                                 lnp[:, b0:b1].unsqueeze(2).broadcast_to([128, b1 - b0, 9]), ALU.add))

        def modulate_samples(dst, src, sh, sc):
            by_b = lambda i: mod[:, 8 * i:8 * i + 8, 1:9].unsqueeze(3).broadcast_to([128, KT, DEC_B, DEC_T])
            d4 = dst[:, :, PROMPT:TOK].rearrange("p k (b t) -> p k b t", t=DEC_T)
            s4 = src[:, :, PROMPT:TOK].rearrange("p k (b t) -> p k b t", t=DEC_T)
            link(V.tensor_tensor(d4, s4, by_b(sc), ALU.mult))
            link(V.tensor_tensor(d4, d4, by_b(sh), ALU.add))

        def modulate_prompt(dst, src, m, sh, sc, done):
            V.tensor_scalar(dst[:, m, 0:PROMPT], src[:, m, 0:PROMPT], mod[:, 8 * sc + m, 0:1], mod[:, 8 * sh + m, 0:1],
                            ALU.mult, ALU.add).then_inc(done, 1)

        def rest_of(src, m, leading, done):
            dve.wait_ge(leading, m + 1)
            V.tensor_tensor(act_lo[:, m, :], src[:, m, :], act_hi[:, m, :].bitcast(F32), ALU.subtract).then_inc(done, 1)

        for a in range(N_ADA0):
            lo_static(dve, 2 * a + AHEAD)
            lo_static(dve, 2 * a + 1 + AHEAD)
            if a >= 1:
                ada_add(a - 1, 5 + (a - 1) % 3)
            if a == 5:
                for j in range(2):
                    dve.wait_ge(turned_x, j + 3)
                    V.tensor_copy(xT[:, 4 * j:4 * j + 4, 128:256],
                                  psum[:, 3 + j, :].rearrange("p (k c) -> p k c", c=128)).then_inc(x_ready_dve, 1)
                dve.wait_ge(turned_x, 5)
                V.tensor_copy(xT[:, :, PROMPT:TOK], psum[:, 0, 0:256].rearrange("p (k c) -> p k c", c=SAMPLE)).then_inc(x_ready_dve, 1)
        ada_add(N_ADA0 - 1, 5 + (N_ADA0 - 1) % 3)
        add_bias(0, 16, 8)
        link(V.tensor_scalar_add(mod[:, 8:16, :], mod[:, 8:16, :], 1.0))
        dve.wait_ge(x_ready_act, 2)
        dve.wait_ge(x_ready_dve, 3)
        modulate_samples(qkvg[:, 0:KT, :], xT[:, :, :], 0, 1)
        for k in range(KT + 1):
            if k < KT:
                modulate_prompt(qkvg, xT, k, 0, 1, h_ready)
            if k >= 1:
                rest_of(qkvg, k - 1, h_hi, h_lo)

        def rope_first(ru, hh, turn):
            dve.wait_ge(evicted, ru + 1)
            dve.sem_inc(dve_past, 1)
            V.stream_shuffle(rope_t[:, hh, :], psum[:, hh, 0:TOK], SWAP).then_inc(acc_free[hh], 1)
            dve.wait_ge(acc_free[hh], turn + 1)
            V.tensor_tensor(rope_t[:, hh, :], rope_t[:, hh, :], cst[:, C_SIN:C_SIN + TOK], ALU.mult).then_inc(sin_done, 1)

        def rope_last(blk, ru, hh):
            dve.wait_ge(sin_done, ru + 1)
            dve.wait_ge(cos_done, ru + 1)
            V.tensor_tensor(block_at(qkvg, blk), block_at(qkvg, blk), rope_t[:, hh, :], ALU.add).then_inc(roped, 1)

        def mix(i, rope_base, kinds):
            for k in range(6):
                nb0 = i * 12 + 2 * (MIX0 + k)
                for hh in range(2):
                    if k % 2 == 0 and kinds[k // 2]:
                        rope_first(rope_base + k + hh, hh, i * 3 + k // 2)
                    elif k % 2 == 0:
                        dve.wait_ge(half_used, nb0 + hh + 1)
                        V.tensor_copy(block_at(qkvg, i * 6 + (k + hh)), psum[:, hh, 0:TOK]).then_inc(acc_free[hh], 1)
                    split_lo(dve, nb0 + hh + AHEAD, (2 * k + hh) % SPLIT, (MIX0 + k + 2) % RAW, hh)
                if k % 2 == 1:
                    if kinds[k // 2]:
                        for hh in range(2):
                            rope_last(i * 6 + (k - 1 + hh), rope_base + k - 1 + hh, hh)
                    if k >= 3:
                        ada_add(i * 3 + (N_ADA0 + k // 2 - 1), 5 + (N_ADA0 + k // 2 - 1) % 3)
                    if k == 5:
                        ada_add(i * 3 + (N_ADA0 + 2), 5 + (N_ADA0 + 2) % 3)
                    if kinds[k // 2]:
                        dve.wait_ge(roped, rope_base + k + 1)

        dve.wait_ge(tables_in, 16)
        with dve.Fori(0, 2) as i:
            mix(i, i * 6, (True, True, True))
        mix(2, 0, (False, False, False))
        mix(3, 12, (True, True, False))
        add_bias(16, 40, N_ADA0 + 12)
        link(V.tensor_scalar_add(mod[:, 32:40, :], mod[:, 32:40, :], 1.0))
        gain, bias = (lnp[:, c:c + 8].unsqueeze(2).broadcast_to([128, 8, 9]) for c in (48, 56))
        link(V.tensor_tensor(mod_t[:, :, :], mod[:, 32:40, :], bias, ALU.mult))
        link(V.tensor_tensor(mod[:, 24:32, :], mod[:, 24:32, :], mod_t[:, :, :], ALU.add))
        link(V.tensor_tensor(mod[:, 32:40, :], mod[:, 32:40, :], gain, ALU.mult))

        dve.wait_ge(roped, 16)
        dve.wait_ge(qz_zero, 1)
        for g in range(4):
            for hp in range(2):
                for h2 in range(2):
                    dst = qz[E * h2:E * h2 + E, g, hp, :, :].rearrange("p q (s c) -> p q s c", c=16)
                    dst = dst[:, :, 0:3:2, 8 * hp + 4 * h2:8 * hp + 4 * h2 + 4]
                    src = qkvg[E * h2:E * h2 + E, q_blk(g, hp), PROMPT:TOK].rearrange("p (s q t) -> p q s t", s=2, t=4)
                    V.tensor_copy(dst, src)
                last = V.tensor_copy(kT[:, hp, NEW_COL[g]:NEW_COL[g] + SAMPLE], qkvg[:, k_blk(g, hp), PROMPT:TOK])
        last.then_inc(qz_ready, 1)
        for j in range(8):
            dve.wait_ge(tok_turned, 2 * j + 2)
            bank = 3 + (j % 2) * 2
            V.tensor_copy(tok[:, 0:2, 0, 128 * j:128 * j + 128], psum[:, bank, 0:256].rearrange("p (t c) -> p t c", t=2))
            V.tensor_copy(tok[0:SAMPLE, 2, 0, 128 * j:128 * j + 128], psum[0:SAMPLE, bank, 256:384]).then_inc(k_tok, 1)
        for idx in range(2 * DEC_B):
            b, hp = idx // 2, idx % 2
            dve.wait_ge(kt_turned, idx + 1)
            if idx >= 2:
                dve.wait_ge(scored_s, idx - 1)
            V.tensor_copy(kT[:, hp, 448:512], psum[:, 5 + 2 * hp, 0:64])
            V.tensor_copy(kT[:, hp, 544:800], psum[:, 5 + 2 * hp, 64:320]).then_inc(kt_y, 1)
        dve.wait_ge(scored_s, 2 * DEC_B)
        for j, (c0, c1, bank, o0) in enumerate(((0, 448, 2, 0), (448, 544, 3, 0), (544, 832, 3, 96))):
            ins = V.tensor_tensor_reduce(s_msk[:, c0:c1], psum[:, bank, o0:o0 + c1 - c0], cst[:, C_MS + c0:C_MS + c1],
                                         1.0, -3.0e38, ALU.add, ALU.max, small[:, j:j + 1])
            link(ins)
        link(V.tensor_tensor(small[:, 1:2], small[:, 0:1], small[:, 1:2], ALU.max))
        V.tensor_scalar(small[:, 4:5], small[:, 1:2], -SCALE, None, ALU.mult).then_inc(max_s, 1)
        V.tensor_scalar(small[:, 5:6], small[:, 2:3], -SCALE, None, ALU.mult).then_inc(max_s, 1)

        def softmax_max(u):
            br, t, h = UNITS[u]
            dve.wait_ge(scored, u + 1)
            if u == 0:
                dve.wait_ge(probT_turned, 3)
            else:
                dve.wait_ge(exped, u)
            n = (3 if br == 0 else 1) * 128 * (t + 1)
            m0 = ((C_MA0, C_MA1), (C_MB0, C_MB1))[br][t]
            src = psum[:, 2:4, :].rearrange("p b c -> p (b c)")[:, 0:n]
            link(V.tensor_tensor_reduce(msk[:, 0:n], src, cst[:, m0:m0 + n], 1.0, -3.0e38, ALU.add, ALU.max, small[:, 112 + u:113 + u]))
            V.tensor_scalar(small[:, 16 + u:17 + u], small[:, 112 + u:113 + u], -SCALE, None, ALU.mult).then_inc(maxed, 1)

        def prbT_copy(u):
            br, t, h = UNITS[u]
            dve.wait_ge(turned, u + 1)
            if u >= 2:
                dve.wait_ge(pv_done, u - 1)
            n = (3 if br == 0 else 1) * (t + 1) * 128
            if n > 512:
                V.tensor_copy(prbT[:, u % 2, 512:n], psum[:, 5, 0:n - 512]).then_inc(prbT_b, 1)

        def out_copy(u):
            br, t, h = UNITS[u]
            dve.wait_ge(exped, u + 1)
            link(V.reciprocal(small[:, 96 + u:97 + u], small[:, 32 + u:33 + u]))
            dve.wait_ge(pv_done, u + 1)
            V.tensor_scalar(o_tokens[:, t, br, E * h:E * h + E], psum[:, 6, 0:E], small[:, 96 + u:97 + u], None, ALU.mult).then_inc(o_ready, 1)

        for s in range(20):
            if s < 16:
                lo_static(dve, 2 * GATE0 + s + AHEAD)
            if s == 1:
                dve.wait_ge(exp_s, 2)
                link(V.reciprocal(small[:, 10:12], small[:, 6:8]))
                for br, (c0, c1) in enumerate(((0, 544), (544, 832))):
                    V.tensor_scalar(s_prb[:, c0:c1], s_prb[:, c0:c1], small[:, 10 + br:11 + br], None, ALU.mult).then_inc(prob_s, 1)
            if 2 <= s < 18:
                softmax_max(s - 2)
            if 3 <= s < 19:
                prbT_copy(s - 3)
            if s >= 4:
                out_copy(s - 4)
        for t in range(2):
            dve.wait_ge(oT_h, t + 1)
            V.tensor_tensor(oT_lo[:, :, 128 * t:128 * t + 128], psum[:, 2 + t, :].rearrange("p (k c) -> p k c", c=128),
                            oT_hi[:, :, 128 * t:128 * t + 128].bitcast(F32), ALU.subtract).then_inc(oT_l, 1)
        for br in range(2):
            if br == 0:
                dve.wait_ge(pv_s, DEC_B)
            V.tensor_tensor(o_masked[:, br, :].rearrange("p (j e) -> p j e", e=E), psum[:, br, :].rearrange("p (j e) -> p j e", e=E),
                            cst[:, C_SELM:C_SELM + 8].unsqueeze(2).broadcast_to([128, 8, E]), ALU.mult).then_inc(masked_s, 1)
        dve.wait_ge(oT_h, 3)
        V.tensor_tensor(oT_lo[:, :, PROMPT:TOK], psum[:, 4, 0:4 * SAMPLE].rearrange("p (k c) -> p k c", c=SAMPLE),
                        oT_hi[:, :, PROMPT:TOK].bitcast(F32), ALU.subtract).then_inc(oT_l, 1)
        dve.wait_ge(sig_ready, 3)

        def merged_rest(m):
            dve.wait_ge(merged_hi, m + 1)
            V.tensor_tensor(act_lo[:, m, :], qkvg[:, m, :], act_hi[:, m, :].bitcast(F32), ALU.subtract).then_inc(merged_lo, 1)

        for h in range(4):
            for m in range(4):
                u = 40 + 4 * h + m
                blk = 4 * (h // 2) + m
                if m < 3:
                    dve.wait_ge(pab_done, 3 * h + m + 1)
                else:
                    dve.wait_ge(half_used, 2 * PAB0 + h + 1)
                gate = qkvg[:, gate_slot(blk + 8 * (h % 2)), :]
                dst = h_t[:, m % 2, :] if h % 2 else qkvg[:, blk, :]
                V.tensor_tensor(dst, psum[:, u % 2, 0:TOK], gate, ALU.mult).then_inc(acc_free[u % 2], 1)
                if h % 2 == 1:
                    dve.wait_ge(acc_free[u % 2], u // 2 + 1)
                    V.tensor_tensor(qkvg[:, blk, :], qkvg[:, blk, :], h_t[:, m % 2, :], ALU.add).then_inc(merged, 1)
                    if m >= 1:
                        merged_rest(blk - 1)
            if h % 2 == 1:
                merged_rest(4 * (h // 2) + 3)
            lo_static(dve, 2 * PAB0 + h + AHEAD)

        def residual(m, bank, gi, done, free=None):
            g3 = mod[:, 8 * gi + m, 1:9].unsqueeze(2).broadcast_to([128, DEC_B, DEC_T])
            t3 = h_t[:, m % 2, 0:SAMPLE].rearrange("p (b t) -> p b t", t=DEC_T)
            p3 = psum[:, bank, PROMPT:TOK].rearrange("p (b t) -> p b t", t=DEC_T)
            link(V.tensor_tensor(t3, p3, g3, ALU.mult))
            link(V.tensor_tensor(xT[:, m, PROMPT:TOK], xT[:, m, PROMPT:TOK], h_t[:, m % 2, 0:SAMPLE], ALU.add))
            V.scalar_tensor_tensor(xT[:, m, 0:PROMPT], psum[:, bank, 0:PROMPT], mod[:, 8 * gi + m, 0:1], xT[:, m, 0:PROMPT],
                                   ALU.mult, ALU.add).then_inc(done, 1)

        dve.wait_ge(x_scaled, 1)
        for m in range(KT):
            dve.wait_ge(half_used, 2 * WO0 + m + 1)
            residual(m, m % 2, 2, z_ready)
            lo_static(dve, 2 * WO0 + m + AHEAD)
        dve.wait_ge(mean_done, KT)
        for j in range(2):
            V.tensor_tensor(xT[:, 4 * j:4 * j + 4, :], xT[:, 4 * j:4 * j + 4, :],
                            psum[:, 2, 0:TOK].unsqueeze(1).broadcast_to([128, 4, TOK]), ALU.subtract).then_inc(centred, 1)
        ada_add(20, 5 + 20 % 3)
        lo_static(dve, 2 * ADA2 + AHEAD)
        lo_static(dve, 2 * ADA2 + 1 + AHEAD)
        dve.wait_ge(std_ready, 1)
        link(V.reciprocal(rstd[:], rstd[:]))
        link(V.tensor_tensor(xT[:, :, PROMPT:TOK], xT[:, :, PROMPT:TOK],
                             rstd[:, PROMPT:TOK].unsqueeze(1).broadcast_to([128, KT, SAMPLE]), ALU.mult))
        modulate_samples(h2_t, xT, 3, 4)
        for m in range(KT + 1):
            if m < KT:
                link(V.tensor_tensor(xT[:, m, 0:PROMPT], xT[:, m, 0:PROMPT], rstd[:, 0:PROMPT], ALU.mult))
                modulate_prompt(h2_t, xT, m, 3, 4, h2_ready)
            if m < 6:
                lo_static(dve, 2 * ADA2 + 2 + AHEAD + m)
            if m >= 1:
                rest_of(h2_t, m - 1, h2_hi, h2_lo)
        for a in range(21, 24):
            ada_add(a, 5 + a % 3)
        add_bias(40, 48, 24)

        def up_pair(j, k):
            for q in range(4):
                nb = j * 4 + (2 * UP0 + q)
                fi = j * 2 + (q - 2)
                if q >= 2:
                    dve.wait_ge(half_used, nb + 1)
                    dve.wait_ge(silu_ready, fi + 1)
                    if not isinstance(j, int) or j >= 1:
                        dve.wait_ge(f_lo_ready, fi - 1)
                    V.tensor_tensor(f_t[:, q - 2, :], psum[:, q % 2, 0:TOK], silu_t[:, q - 2, :], ALU.mult).then_inc(f_ready, 1)
                if isinstance(j, int):
                    lo_static(dve, nb + AHEAD)
                else:
                    split_lo(dve, nb + AHEAD, q, (UP0 + 2 * k + 2 + q // 2) % RAW, q % 2)
                if q >= 2:
                    dve.wait_ge(f_hi_ready, fi + 1)
                    V.tensor_tensor(block_at(f_lo, fi), f_t[:, q - 2, :], block_at(f_hi, fi).bitcast(F32), ALU.subtract).then_inc(f_lo_ready, 1)

        for j in range(3):
            up_pair(j, j)
        with dve.Fori(1, UP_TRIPS) as i:
            for k in range(UP_PAIRS):
                up_pair(i * 3 + k, k)
        for j in range(UP_PAIRS * UP_TRIPS, PAIRS):
            up_pair(j, 0)

        dve.wait_ge(x1_ready, KT)

        def second(hcol):
            for m in range(4):
                if m < 3:
                    dve.wait_ge(down_done, 3 * hcol + m + 1)
                else:
                    dve.wait_ge(half_used, 2 * DOWN0 + 11 * hcol + 11)
                residual(4 * hcol + m, 4 * hcol + m, 5, z2_ready)
        for nb in range(2 * DOWN0, 2 * DOWN0 + 11):
            lo_static(dve, nb + AHEAD)
        second(0)
        for nb in range(2 * DOWN0 + 11, LAST + 1):
            lo_static(dve, nb + AHEAD)
        second(1)
        dve.wait_ge(z2_turned, 8)
        for t in range(3):
            nt = 128 if t < 2 else SAMPLE
            for hcol in range(2):
                link(V.bn_stats(st6[0:nt, t, hcol, :], psum[0:nt, t + 3 * hcol, :]))
            V.bn_aggr(small[0:nt, 50 + 2 * t:52 + 2 * t], st6[0:nt, t, :, :].rearrange("p a b -> p (a b)")).then_inc(var2, 1)
        for t in range(3):
            nt = 128 if t < 2 else SAMPLE
            dve.wait_ge(std2, t + 1)
            link(V.reciprocal(small[0:nt, 63 + t:64 + t], small[0:nt, 60 + t:61 + t]))
            V.scalar_tensor_tensor(small[0:nt, 66 + t:67 + t], small[0:nt, 50 + 2 * t:51 + 2 * t], -1.0, small[0:nt, 63 + t:64 + t],
                                   ALU.mult, ALU.mult).then_inc(rs2, 1)
        dve.wait_ge(ln_rows_in, 32)
        for t in range(3):
            nt = 128 if t < 2 else SAMPLE
            dve.wait_ge(y_norm, 2 * t + 2)
            link(V.tensor_tensor(y_tok[0:nt, t, :], y_tok[0:nt, t, :], ln_rows[0:nt, 0, :], ALU.mult))
            V.tensor_tensor(y_tok[0:nt, t, :], y_tok[0:nt, t, :], ln_rows[0:nt, 1, :], ALU.add).then_inc(y_done, 1)

    @block.gpsimd
    def _(pool):
        nc.gpsimd.memset(qz[:], 0.0).then_inc(qz_zero, 1)

        def cos_mult(blk, ru):
            pool.wait_ge(evicted, ru + 1)
            nc.gpsimd.tensor_tensor(block_at(qkvg, blk), block_at(qkvg, blk), cst[:, C_COS:C_COS + TOK], ALU.mult).then_inc(cos_done, 1)

        pool.wait_ge(tables_in, 16)
        with pool.Fori(0, 12) as i:
            cos_mult(i, i)
        for blk in range(18, 22):
            cos_mult(blk, blk - 6)
        nc.gpsimd.tensor_scalar(xT[:], xT[:], ALPHA, None, ALU.mult).then_inc(x_scaled, 1)
        pool.wait_ge(k_tok, 8)
        pool.wait_ge(v_tok, 8)
        for kind in range(2):
            for g in range(4):
                lo = PROMPT - (min(WIN[g], PROMPT) if g < 3 else PROMPT)
                cols = slice(256 * g, 256 * g + 256)
                dst = kv_prompt[g].rearrange("(t p) s c -> p t s c", p=128)
                pool.dma_start(dst[:, :, kind, :], tok[:, lo // 128:2, kind, cols]).then_inc(stored, 16)
        for kind in range(2):
            for g in range(4):
                dst = kv_sample[g][:, (BUF[g] - DEC_T if g < 3 else 0):, 256 * kind:256 * kind + 256]
                src = tok[0:SAMPLE, 2, kind, 256 * g:256 * g + 256]
                pool.dma_start(dst, src).then_inc(stored, 16)
        pool.wait_ge(half_used, 2 * WO0)
        pool.wait_ge(stored, 16 * N_POOL_STORES)
        pool.dma_start(ln_rows[:, 0, :], ln2_g.broadcast_to([128, D])).then_inc(ln_rows_in, 16)
        pool.dma_start(ln_rows[:, 1, :], ln2_b.broadcast_to([128, D])).then_inc(ln_rows_in, 16)
        with pool.Fori(0, DEC_B) as b:
            pool.wait_ge(half_used, b * 5 + 2 * UP0)
            for g in range(3):
                pool.dma_start(kv_sample[g][bass.ds(b, 1), 0:BUF[g] - DEC_T, :],
                               cache_rows[g][bass.ds(b, 1), DEC_T:BUF[g], :]).then_inc(moved, 16)

    ctx.close()


_INS = ["x_prompt", "x_sample", "cache_kv_a0", "cache_kv_a1", "cache_kv_a2", "cache_kv_b", "page_table", "c_prompt", "c_sample",
        "w_ada", "b_ada", "w_in", "w_pa", "w_pb", "w_o", "ln1_g", "ln1_b", "w_up", "w_down", "ln2_g", "ln2_b"]
_OUTS = [(1, PROMPT, D), (DEC_B, DEC_T, D)] + \
        [(1, 1, min(w, PROMPT), 2, 4, E) for w in WIN] + [(1, 1, PROMPT, 2, 4, E)] + \
        [(1, DEC_B, b, 2, 4, E) for b in BUF] + [(1, DEC_B, DEC_T, 2, 4, E)]


def kernel(**inputs):
    import numpy as np
    import concourse.bacc as bacc
    from concourse.bass_utils import run_bass_kernel_spmd

    nc = bacc.Bacc("TRN2", target_bir_lowering=False, num_devices=1)
    arrays, a = {}, {}
    for name in _INS:
        v = np.ascontiguousarray(inputs[name])
        arrays[f"in_{name}"] = v
        a[name] = nc.dram_tensor(f"in_{name}", v.shape, mybir.dt.from_np(v.dtype), kind="ExternalInput").ap()
    arrays["in_const"] = constants()
    const = nc.dram_tensor("in_const", (128, C_END), F32, kind="ExternalInput").ap()
    outs = [nc.dram_tensor(f"out_{i}", shape, F32, kind="ExternalOutput").ap() for i, shape in enumerate(_OUTS)]
    caches = [a[f"cache_kv_a{g}"] for g in range(3)]
    build(nc, a["x_prompt"], a["x_sample"],
          [c.rearrange("a b l k h e -> (a b) l k (h e)") for c in caches],
          [c.rearrange("a b l k h e -> (a b) l (k h e)") for c in caches],
          a["cache_kv_b"].rearrange("a n p k h e -> (a n) p k (h e)"),
          a["page_table"], a["c_prompt"], a["c_sample"], a["w_ada"][0], a["b_ada"], a["w_in"][0], a["w_pa"][0],
          a["w_pb"][0], a["w_o"][0], a["ln1_g"], a["ln1_b"], a["w_up"][0], a["w_down"][0], a["ln2_g"], a["ln2_b"], const,
          outs[0], outs[1],
          [o.rearrange("a b l k h e -> (a b l) k (h e)") for o in outs[2:6]],
          [o.rearrange("a b l k h e -> (a b) l (k h e)") for o in outs[6:10]])
    r = run_bass_kernel_spmd(nc, [arrays], core_ids=[0])
    return tuple(r.results[0][f"out_{i}"] for i in range(len(_OUTS)))
```

```python
import math
from contextlib import ExitStack

import concourse.bass as bass
from concourse import mybir
from concourse.alu_op_type import AluOpType as ALU

F32 = mybir.dt.float32
F32R = mybir.dt.float32r
ACT = mybir.ActivationFunctionType

D = 1024
KT = D // 128
PROMPT = 256
DEC_B, DEC_T = 8, 4
SAMPLE = DEC_B * DEC_T
TOK = PROMPT + SAMPLE
PAST = 256
PAGE = 128
N_PAGES = PAST // PAGE
E = 64
ROT = E // 4
THETA = 500000.0
D_FF = -(-8 * D // (3 * 256)) * 256
FT = D_FF // 128
WIN = (128, 512, 2048)
DIL = (1, 4, 16)
BUF = tuple(min(w, PAST) for w in WIN)
ALPHA = 2.0 ** 0.25
EPS = 1e-5
SCALE = E ** -0.5
NEG = -1.0e30

RAW = 3
SPLIT = 4
N_ADA0 = 8
MIX0 = N_ADA0
GATE0 = MIX0 + 24
ADA1 = GATE0 + 8
PAB0 = ADA1 + 2
WO0 = PAB0 + 2
ADA2 = WO0 + 4
UP0 = ADA2 + 2
DOWN0 = UP0 + 22
PAIRS = D_FF // 256


def ropetables():
    import numpy as np
    inv = np.exp(np.float32(-math.log(THETA)) * np.arange(0, ROT, 2, dtype=np.float32) / np.float32(ROT)).astype(np.float32)
    pos = np.concatenate([np.arange(PROMPT), np.tile(PAST + np.arange(DEC_T), DEC_B)]).astype(np.float32)
    ang = (pos[:, None] * inv[None, :]).astype(np.float32)
    cos, sin = np.cos(ang).astype(np.float32), np.sin(ang).astype(np.float32)
    c, s = np.ones((128, TOK), np.float32), np.zeros((128, TOK), np.float32)
    for base in (0, E):
        for j in range(ROT // 2):
            c[base + j] = c[base + j + ROT // 2] = cos[:, j]
            s[base + j] = -sin[:, j]
            s[base + j + ROT // 2] = sin[:, j]
    return c, s


def prompt_mask(tile, group):
    import numpy as np
    q = tile * 128 + np.arange(128)[:, None]
    k = np.arange((tile + 1) * 128)[None, :]
    off = q - k
    ok = off >= 0
    if group < 3:
        ok = ok & (off <= WIN[group]) & (off % DIL[group] == 0)
    return np.where(ok, 0.0, NEG).astype(np.float32)


def row_of(r):
    return r // 32 + 4 * (r % 32 // 16), r % 16 // 4, r % 4


def sample_mask():
    import numpy as np
    b, _, t = row_of(np.arange(128))
    m = np.full((128, 832), NEG, np.float32)
    new_b, new_t = np.arange(SAMPLE) // DEC_T, np.arange(SAMPLE) % DEC_T

    def put(at, ok):
        m[:, at:at + ok.shape[1]] = np.where(ok, 0.0, NEG)
    put(0, np.arange(128)[None, :] >= t[:, None])
    put(160, np.arange(256)[None, :] % 4 == t[:, None])
    put(448, np.arange(64)[None, :] % 4 == t[:, None])
    put(544, np.ones((128, 256), bool))
    own = new_b[None, :] == b[:, None]
    put(128, own & (new_t[None, :] <= t[:, None]))
    put(416, own & (new_t[None, :] == t[:, None]))
    put(512, own & (new_t[None, :] == t[:, None]))
    put(800, own & (new_t[None, :] <= t[:, None]))
    return m


C_ID, C_ONE, C_COS, C_SIN = 0, 128, 256, 256 + TOK
C_MS = 256 + 2 * TOK
C_MA1 = C_MS + 832
C_MA0 = C_MA1 + 768
C_MB1 = C_MA0 + 384
C_MB0 = C_MB1 + 256
C_EPS = C_MB0 + 128
C_SELM = C_EPS + 1
C_SEL = C_SELM + 8
C_END = C_SEL + SAMPLE


def constants():
    import numpy as np
    c = np.zeros((128, C_END), np.float32)
    c[:, C_ID:C_ID + 128] = np.eye(128)
    c[:, C_ONE:C_ONE + 128] = 1.0 / D
    c[:, C_COS:C_COS + TOK], c[:, C_SIN:C_SIN + TOK] = ropetables()
    c[:, C_MS:C_MS + 832] = sample_mask()
    for g in range(3):
        c[:, C_MA1 + 256 * g:C_MA1 + 256 * (g + 1)] = prompt_mask(1, g)
        c[:, C_MA0 + 128 * g:C_MA0 + 128 * (g + 1)] = prompt_mask(0, g)
    c[:, C_MB1:C_MB1 + 256] = prompt_mask(1, 3)
    c[:, C_MB0:C_MB0 + 128] = prompt_mask(0, 3)
    c[:, C_EPS] = EPS
    b, h, t = row_of(np.arange(128))
    c[:, C_SELM:C_SELM + 8] = (b // 4 * 4 + h)[:, None] == np.arange(8)[None, :]
    c[:, C_SEL:C_SEL + SAMPLE] = (b * DEC_T + t)[:, None] == np.arange(SAMPLE)[None, :]
    return c


S_PIECES = [(0, 128), (160, 128), (288, 128), (448, 64), (544, 128), (672, 128), (128, 32), (416, 32), (512, 32), (800, 32)]
NEW_COL = [128, 416, 512, 800]
SWAP = [(i + ROT // 2) % ROT if i < ROT else i for i in range(32)]
KV_LOADS = 3 + N_PAGES
KV_PLACES = 5
N_POOL_STORES = 16


def block_at(t, blk):
    if isinstance(blk, int):
        return t[:, blk, :]
    return t[:, bass.ds(blk, 1), :].rearrange("p a t -> p (a t)")


class Count:

    def __init__(self, sem):
        self.sem, self.n = sem, 0

    def up(self, ins):
        ins.then_inc(self.sem, 1)
        self.n = self.n + 1


def q_blk(g, hp):
    return 2 * g + hp if g < 3 else 18 + hp


def k_blk(g, hp):
    return 6 + 2 * g + hp if g < 3 else 20 + hp


def v_blk(g, hp):
    return 12 + 2 * g + hp if g < 3 else 22 + hp


def gate_slot(g):
    return 24 + g if g < 8 else ([12, 13, 14, 15, 16, 17, 22, 23])[g - 8]


UNITS = [(0, t, (h,)) for t in (1, 0) for h in range(4)] + [(1, t, (h, h + 1)) for t in (1, 0) for h in (0, 2)]
N_UNITS = len(UNITS)


def rows_before(u):
    return sum(len(heads) for _, _, heads in UNITS[:u])


def keys_of(u):
    br, t, _ = UNITS[u]
    return (3 if br == 0 else 1) * 128 * (t + 1)


def cols_of(u):
    return keys_of(u) * len(UNITS[u][2])


def build(nc, x_prompt, x_sample, cache_a, cache_rows, cache_b, page_table, c_prompt, c_sample, w_ada, b_ada, w_in,
          w_pa, w_pb, w_o, ln1_g, ln1_b, w_up, w_down, ln2_g, ln2_b, const,
          y_prompt, y_sample, kv_prompt, kv_sample):
    ctx = ExitStack()
    base = nc.sbuf_base if isinstance(nc.sbuf_base, int) else 0
    at = [(base + 63) // 64 * 64]

    def sb(name, shape, dt=F32, offset=None):
        size = 4
        for n in shape[1:]:
            size *= n
        if offset is None:
            offset = at[0]
            at[0] += (size + 31) // 32 * 32
        return nc.alloc_sbuf_tensor_at(name, list(shape), dt, offset=offset), offset

    xT, _ = sb("xT", [128, KT, TOK])
    act_hi, _ = sb("act_hi", [128, KT, TOK], F32R)
    act_lo, _ = sb("act_lo", [128, KT, TOK], F32R)
    raw, _ = sb("raw", [128, RAW, 2048])
    w_hi, _ = sb("w_hi", [128, SPLIT, 1024], F32R)
    w_lo, _ = sb("w_lo", [128, SPLIT, 1024], F32R)
    cst, _ = sb("cst", [128, C_END])
    qkvg, o_qkvg = sb("qkvg", [128, 32, TOK])
    kvin, _ = sb("kvin", [128, 2, 6, 256])
    kT, o_kT = sb("kT", [128, 2, 832])
    qz, o_qz = sb("qz", [128, 4, 2, 4, 48])
    tok, o_tok = sb("tok", [128, 3, 2, 1024])
    tmp, o_tmp = sb("tmp", [128, 3840])
    o_tokens, _ = sb("o_tokens", [128, 2, 2, 256])
    mod, _ = sb("mod", [128, 48, 9])
    rowbuf, _ = sb("rowbuf", [18, 3, 256])
    mod_t, _ = sb("mod_t", [128, 8, 9])
    c_hl, _ = sb("c_hl", [128, KT, 18], F32R)
    small, _ = sb("small", [128, 128])
    rows, _ = sb("rows", [64, 128])
    pages, _ = sb("pages", [1, DEC_B * N_PAGES], mybir.dt.int32)

    x_tok, _ = sb("x_tok", [128, 3, D], F32, o_tok)
    s_msk, _ = sb("s_msk", [128, 832], F32, o_tmp)
    s_prb, _ = sb("s_prb", [128, 832], F32, o_tmp + 832 * 4)
    s_prbT, _ = sb("s_prbT", [128, 10, 128], F32, o_qz)
    msk, _ = sb("msk", [128, 768], F32, o_tmp)
    prb, _ = sb("prb", [128, 2, 768], F32, o_tmp + 768 * 4)
    prbT, _ = sb("prbT", [128, 2, 768], F32, o_tmp + 3 * 768 * 4)
    oT_hi, _ = sb("oT_hi", [128, 4, TOK], F32R, o_kT)
    oT_lo, _ = sb("oT_lo", [128, 4, TOK], F32R, o_qz)
    assert 4 * TOK <= 2 * 832 and 4 * TOK <= 4 * 2 * 4 * 48
    f_hi, _ = sb("f_hi", [128, FT, TOK], F32R, o_qkvg)
    f_lo, _ = sb("f_lo", [128, FT, TOK], F32R, o_qkvg + FT * TOK * 4)
    assert o_qkvg + 2 * FT * TOK * 4 <= o_tok
    ln_rows, _ = sb("ln_rows", [128, 2, D], F32, o_tok)
    y_tok, _ = sb("y_tok", [128, 3, D], F32, o_tok + 2 * D * 4)
    silu_t, _ = sb("silu_t", [128, 2, TOK], F32, o_tmp)
    f_t, _ = sb("f_t", [128, 2, TOK], F32, o_tmp + 2 * TOK * 4)
    rstd, _ = sb("rstd", [128, TOK], F32, o_tmp + 4 * TOK * 4)
    h_t, _ = sb("h_t", [128, 2, TOK], F32, o_tmp + 5 * TOK * 4)
    k_early, _ = sb("k_early", [128, 6, 256], F32, o_qkvg + 24 * TOK * 4)
    k_late, _ = sb("k_late", [128, 6, 256], F32, o_tmp + 3 * 768 * 4)
    v_more, _ = sb("v_more", [128, 6, 256], F32, o_kT)
    o_masked, _ = sb("o_masked", [128, 2, 512], F32, o_qkvg + 8 * TOK * 4)
    gated, _ = sb("gated", [128, 4, TOK], F32, o_tmp)
    shift, _ = sb("shift", [128, TOK], F32, o_tmp)
    off_mean, _ = sb("off_mean", [128, TOK], F32, o_tmp + TOK * 4)
    off_sq, _ = sb("off_sq", [128, TOK], F32, o_tmp + 2 * TOK * 4)
    h2_t, _ = sb("h2_t", [128, KT, TOK], F32, o_qkvg + 16 * TOK * 4)
    rope_t, _ = sb("rope_t", [128, 2, TOK], F32, o_tmp)
    ctok, _ = sb("ctok", [9, D], F32, o_tmp)
    c_t, _ = sb("c_t", [128, KT, 9], F32, o_tmp + 8 * TOK * 4)

    lnp, _ = sb("lnp", [128, 80])
    st6, _ = sb("st6", [128, 3, 4, 6])
    ident = cst[:, C_ID:C_ID + 128]
    ones = cst[:, C_ONE:C_ONE + 128]

    assert at[0] <= nc.sbuf_usable_end
    psum = nc.alloc_psum_tensor("psum", [128, 8, 512], F32)

    def sem(name):
        return nc.alloc_semaphore(name)

    const_in, x_in, c_in, rows_in, pages_in = sem("const_in"), sem("x_in"), sem("c_in"), sem("rows_in"), sem("pages_in")
    ln_rows_in = sem("ln_rows_in")
    raw_in = [sem(f"raw_in{i}") for i in range(RAW)]
    kv_in = [sem(f"kv_in{i}") for i in range(KV_PLACES)]
    tables_in, moved, masked_s, sel_done = (sem(n) for n in ("tables_in", "moved", "masked_s", "sel_done"))
    stored, y_stored = sem("stored"), sem("y_stored")
    hi_ready, lo_ready, half_used = sem("hi_ready"), sem("lo_ready"), sem("half_used")
    acc_free = [sem("acc_free0"), sem("acc_free1")]
    turned_c, turned_rows, turned_x = sem("turned_c"), sem("turned_rows"), sem("turned_x")
    c_silu, c_hi, c_ready = sem("c_silu"), sem("c_hi"), sem("c_ready")
    x_ready_act, x_ready_dve = sem("x_ready_act"), sem("x_ready_dve")
    rows_ready = sem("rows_ready")
    ada_row, ada_turned, ada_mod = sem("ada_row"), sem("ada_turned"), sem("ada_mod")
    h_ready, h_hi, h_lo = sem("h_ready"), sem("h_hi"), sem("h_lo")
    evicted, sin_done, cos_done, roped = sem("evicted"), sem("sin_done"), sem("cos_done"), sem("roped")
    x_scaled = sem("x_scaled")
    qz_zero, qz_ready = sem("qz_zero"), sem("qz_ready")
    tok_turned, v_tok, k_tok = sem("tok_turned"), sem("v_tok"), sem("k_tok")
    kt_turned, kt_x, kt_y, scored_s = sem("kt_turned"), sem("kt_x"), sem("kt_y"), sem("scored_s")
    max_s, exp_s, prob_s = sem("max_s"), sem("exp_s"), sem("prob_s")
    probT_turned, probT_s, pv_s = sem("probT_turned"), sem("probT_s"), sem("pv_s")
    scored, maxed, exped, turned, prbT_a, prbT_b, pv_done, o_ready = (sem(n) for n in (
        "scored", "maxed", "exped", "turned", "prbT_a", "prbT_b", "pv_done", "o_ready"))
    oT_turned, oT_h, oT_l = sem("oT_turned"), sem("oT_h"), sem("oT_l")
    gate_ready = sem("gate_ready")
    pab_done, gated_ready, merged, merged_hi, merged_lo = (sem(n) for n in (
        "pab_done", "gated_ready", "merged", "merged_hi", "merged_lo"))
    z_ready, shift_done, shift_ready, shifted, squared = (sem(n) for n in (
        "z_ready", "shift_done", "shift_ready", "shifted", "squared"))
    sums_done, off_ready, var_ready, std_ready, rstd_ready = (sem(n) for n in (
        "sums_done", "off_ready", "var_ready", "std_ready", "rstd_ready"))
    centred = sem("centred")
    centred_s, h2s_ready, pool_step, x1_scaled = (sem(n) for n in ("centred_s", "h2s_ready", "pool_step", "x1_scaled"))
    x1_ready, h2_ready, h2_hi, h2_lo = (sem(n) for n in ("x1_ready", "h2_ready", "h2_hi", "h2_lo"))
    silu_ready, f_ready, f_hi_ready, f_lo_ready = sem("silu_ready"), sem("f_ready"), sem("f_hi_ready"), sem("f_lo_ready")
    down_done, z2_ready, z2_turned = sem("down_done"), sem("z2_ready"), sem("z2_turned")
    masks_in, new_keys = sem("masks_in"), sem("new_keys")
    z2_kept, y_scaled, y_gained, y_done_pool = sem("z2_kept"), sem("y_scaled"), sem("y_gained"), sem("y_done_pool")
    var2, std2, rs2, y_norm, y_done = sem("var2"), sem("std2"), sem("rs2"), sem("y_norm"), sem("y_done")
    dve_link = Count(sem("dve_link"))
    sp_past, pe_past, dve_past = sem("sp_past"), sem("pe_past"), sem("dve_past")

    def halves_of(n):
        if isinstance(n, int) and n >= DOWN0:
            c = n - DOWN0
            return 2 * DOWN0 + 11 * (c // 6) + 2 * (c % 6)
        return 2 * n

    def raw_need(n, slot):
        extra = sum(1 for m in (PAB0, PAB0 + 1) if m % RAW == slot and n >= m)
        return 16 * (n // RAW + 1 + extra)

    MIX_TRIPS = 4
    UP_PAIRS = 3
    UP_TRIPS = PAIRS // UP_PAIRS

    w_in_v = w_in.rearrange("(k p) n -> p k n", p=128)
    w_ada_v = w_ada.rearrange("(k p) n -> p k n", p=128)
    w_o_v = w_o.rearrange("(k p) n -> p k n", p=128)
    w_up_v = w_up.rearrange("(k p) n -> p k n", p=128)
    w_pa_v = w_pa.rearrange("(k p) n -> p k n", p=128)
    w_pb_v = w_pb.rearrange("(k p) n -> p k n", p=128)
    w_down_v = w_down.rearrange("(k p) n -> p k n", p=128)

    def raw8(slot):
        return raw[:, slot, :].rearrange("p (k n) -> p k n", k=8)

    def raw_half(n_static_slot, hh, by_rows):
        if by_rows:
            return raw[:, n_static_slot, 1024 * hh:1024 * hh + 1024]
        return raw8(n_static_slot)[:, :, 128 * hh:128 * hh + 128]

    def kv_place(b, kind):
        if kind == 0:
            return b % 4, b // 4
        place = (0, 1, 4)[b % 3]
        return place, b // 3 + (2 if place < 2 else 0)

    def kv_tile(b, kind):
        place, _ = kv_place(b, kind)
        return kvin[:, place, :, :] if place < 2 else (k_early, k_late, v_more)[place - 2]

    def part(t, slot, by_rows):
        if by_rows:
            return t[:, slot, :]
        return t[:, slot, :].rearrange("p (k n) -> p k n", k=8)

    def split_hi(act, nb, slot4, rslot, hh, need, by_rows=False):
        act.wait_ge(raw_in[rslot], need)
        if not isinstance(nb, int) or nb >= SPLIT:
            act.wait_ge(half_used, nb - SPLIT + 1)
        nc.scalar.activation(part(w_hi, slot4, by_rows), raw_half(rslot, hh, by_rows), ACT.Copy).then_inc(hi_ready, 1)

    def split_lo(dve, nb, slot4, rslot, hh, by_rows=False):
        dve.wait_ge(hi_ready, nb + 1)
        nc.vector.tensor_tensor(part(w_lo, slot4, by_rows), raw_half(rslot, hh, by_rows),
                                part(w_hi, slot4, by_rows).bitcast(F32), ALU.subtract).then_inc(lo_ready, 1)

    def halves(first, last):
        out = []
        for n in range(first, last):
            by_rows = PAB0 <= n < WO0 or n >= DOWN0
            for hh in range(1 if n >= DOWN0 and (n - DOWN0) % 6 == 5 else 2):
                nb = halves_of(n) + hh
                out.append((nb, nb % SPLIT, n % RAW, hh, by_rows, raw_need(n, n % RAW)))
        return out

    ALL = {h[0]: h for h in halves(0, DOWN0 + 12)}
    LAST = max(ALL)

    def hi_static(act, nb):
        if nb in ALL:
            _, s, r, hh, by, need = ALL[nb]
            split_hi(act, nb, s, r, hh, need, by)

    def lo_static(dve, nb):
        if nb in ALL:
            _, s, r, hh, by, need = ALL[nb]
            split_lo(dve, nb, s, r, hh, by)

    PAB_BANK = (0, 1, 6, 3)
    SHIFT_BLOCKS = 2
    SHIFT_ORDER = (4, 5, 6, 7, 0, 1, 2, 3)
    SUM_ORDER = (4, 0, 1, 2, 3, 5, 6, 7)
    SUMS_AFTER = {5: (0, 1), 6: (2, 3, 4), 7: (5,)}
    AHEAD = SPLIT

    block = ctx.enter_context(nc.Block())

    @block.sync
    def _(sp):
        sp.dma_start(cst[:, 0:C_COS], const[:, 0:C_COS]).then_inc(const_in, 16)
        sp.dma_start(ctok[0:1, :], c_prompt).then_inc(c_in, 16)
        sp.dma_start(ctok[1:9, :], c_sample).then_inc(c_in, 16)
        def load(n, slot, src, dst, first_use):
            if not first_use:
                sp.wait_ge(lo_ready, halves_of(n - RAW + 1))
            sp.dma_start(dst, src).then_inc(raw_in[slot], 16)

        for n in range(MIX0):
            load(n, n % RAW, w_ada_v[:, :, 256 * n:256 * n + 256], raw8(n % RAW), n < RAW)
            if n == 0:
                sp.dma_start(rows[0:48, :], b_ada.rearrange("a (j p) -> (a j) p", p=128)).then_inc(rows_in, 16)
                sp.dma_start(rows[48:56, :], ln1_g.rearrange("a (j p) -> (a j) p", p=128)).then_inc(rows_in, 16)
                sp.dma_start(rows[56:64, :], ln1_b.rearrange("a (j p) -> (a j) p", p=128)).then_inc(rows_in, 16)
            if n == 2:
                sp.dma_start(pages[:], page_table.rearrange("b n -> (b n)").unsqueeze(0)).then_inc(pages_in, 16)
            if n == 3:
                sp.dma_start(x_tok[:, 0:2, :], x_prompt.rearrange("a (t p) d -> p (a t) d", p=128)).then_inc(x_in, 16)
                sp.dma_start(x_tok[0:SAMPLE, 2, :], x_sample.rearrange("b t d -> (b t) d")).then_inc(x_in, 16)
        load(MIX0, MIX0 % RAW, w_in_v[:, :, 0:256], raw8(MIX0 % RAW), False)
        sp.dma_start(cst[:, C_COS:C_MS], const[:, C_COS:C_MS]).then_inc(tables_in, 16)

        def mix_loads(i):
            for k in range(6):
                col = sp.snap((i * 3 + (k // 2 if k % 2 == 0 else N_ADA0 + k // 2)) * 256)
                sp.wait_ge(lo_ready, i * 12 + 2 * (MIX0 + k - RAW + 1))
                sp.sem_inc(sp_past, 1)
                src = (w_in_v if k % 2 == 0 else w_ada_v)[:, :, bass.ds(col, 256)]
                sp.dma_start(raw8((MIX0 + k) % RAW), src).then_inc(raw_in[(MIX0 + k) % RAW], 16)

        def mix_load_first(k):
            n, col = MIX0 + k, 256 * (k // 2 if k % 2 == 0 else N_ADA0 + k // 2)
            load(n, n % RAW, (w_in_v if k % 2 == 0 else w_ada_v)[:, :, col:col + 256], raw8(n % RAW), False)

        for k in range(1, 6):
            mix_load_first(k)
        with sp.Fori(1, MIX_TRIPS) as i:
            mix_loads(i)
        sp.dma_start(cst[:, C_MS:C_END], const[:, C_MS:C_END]).then_inc(masks_in, 16)
        def load_kv(b, kind):
            dst, s = kv_tile(b, kind), kv_in[kv_place(b, kind)[0]]
            sp.dma_start(dst[:, 0, :], cache_a[0][b, :, kind, :]).then_inc(s, 16)
            sp.dma_start(dst[:, 1:3, :], cache_a[1][b, :, kind, :].rearrange("(n p) c -> p n c", p=128)).then_inc(s, 16)
            src = cache_a[2][b, :, kind, :].rearrange("(g r) c -> g r c", r=16)[:, 0:4, :]
            sp.dma_start(dst[0:64, 5, :], src).then_inc(s, 16)
            for j in range(N_PAGES):
                page = sp.value_load(pages[0:1, N_PAGES * b + j:N_PAGES * b + j + 1], min_val=0, max_val=cache_b.shape[0] - 1)
                sp.dma_start(dst[:, 3 + j, :], cache_b[bass.ds(page, 1), :, kind, :].rearrange("a p c -> (a p) c")).then_inc(s, 16)

        def load_static(n):
            if n < ADA1:
                col = 3072 + 256 * (n - GATE0)
                load(n, n % RAW, w_in_v[:, :, col:col + 256], raw8(n % RAW), False)
            elif n < PAB0:
                j = 20 + n - ADA1
                load(n, n % RAW, w_ada_v[:, :, 256 * j:256 * j + 256], raw8(n % RAW), False)
            elif n < WO0:
                j = n - PAB0
                dst = raw[:, n % RAW, :].rearrange("p (k n) -> p k n", k=4)
                load(n, n % RAW, w_pa_v[:, :, 512 * j:512 * j + 512], dst[:, 0:2, :], False)
                sp.dma_start(dst[:, 2:4, :], w_pb_v[:, :, 512 * j:512 * j + 512]).then_inc(raw_in[n % RAW], 16)
            elif n < ADA2:
                j = n - WO0
                load(n, n % RAW, w_o_v[:, :, 256 * j:256 * j + 256], raw8(n % RAW), False)
            else:
                j = 22 + n - ADA2
                load(n, n % RAW, w_ada_v[:, :, 256 * j:256 * j + 256], raw8(n % RAW), False)

        sp.wait_ge(pages_in, 16)
        load_static(GATE0)
        for b in range(3):
            load_kv(b, 0)
        load_static(GATE0 + 1)
        for b in range(3, DEC_B):
            if b >= 4:
                sp.wait_ge(kt_turned, 2 * (b - 4) + 2)
            load_kv(b, 0)
        load_static(GATE0 + 2)
        for b in range(2):
            sp.wait_ge(kt_turned, 2 * (4 + b) + 2)
            load_kv(b, 1)
        load_static(GATE0 + 3)
        load_static(GATE0 + 4)
        load_static(GATE0 + 5)
        sp.wait_ge(scored_s, 2 * DEC_B)
        load_kv(2, 1)
        load_static(GATE0 + 6)
        for b in range(3, DEC_B):
            sp.wait_ge(pv_s, b - 2)
            load_kv(b, 1)
            load_static(GATE0 + 4 + b)
        for n in range(GATE0 + 4 + DEC_B, UP0):
            load_static(n)
        with sp.Fori(0, UP_TRIPS) as i:
            for k in range(6):
                n = UP0 + k
                col = sp.snap((i * 3 + k // 2) * 256 + (D_FF if k % 2 == 0 else 0))
                sp.wait_ge(lo_ready, i * 12 + 2 * (n - RAW + 1))
                sp.sem_inc(sp_past, 1)
                sp.dma_start(raw8(n % RAW), w_up_v[:, :, bass.ds(col, 256)]).then_inc(raw_in[n % RAW], 16)
        for n in range(UP0 + 6 * UP_TRIPS, DOWN0):
            k = n - UP0
            col = (k // 2) * 256 + (D_FF if k % 2 == 0 else 0)
            load(n, n % RAW, w_up_v[:, :, col:col + 256], raw8(n % RAW), False)
        for n in range(DOWN0, DOWN0 + 12):
            c, hcol = (n - DOWN0) % 6, (n - DOWN0) // 6
            nk = min(4, FT - 4 * c)
            dst = raw[:, n % RAW, 0:512 * nk].rearrange("p (k n) -> p k n", k=nk)
            load(n, n % RAW, w_down_v[:, 4 * c:4 * c + nk, 512 * hcol:512 * hcol + 512], dst, False)
        def store_prompt(t, c0, done):
            sp.wait_ge(done, t + 1)
            sp.dma_start(y_prompt[0, 128 * t:128 * t + 128, c0:c0 + 512], y_tok[:, t, c0:c0 + 512]).then_inc(y_stored, 16)

        store_prompt(0, 512, y_done)
        store_prompt(0, 0, y_done_pool)
        store_prompt(1, 512, y_done)
        sp.wait_ge(y_done, 3)
        sp.dma_start(y_sample.rearrange("b t d -> (b t) d"), y_tok[0:SAMPLE, 2, :]).then_inc(y_stored, 16)
        store_prompt(1, 0, y_done_pool)
        sp.wait_ge(y_stored, 16 * 5)
        sp.wait_ge(stored, 16 * N_POOL_STORES)
        sp.wait_ge(moved, 16 * 3 * DEC_B)

    def mm3(out, hi_l, lo_l, hi_r, lo_r, start, stop):
        nc.tensor.matmul(out, hi_l, hi_r, start=start, stop=False, skip_group_check=True)
        nc.tensor.matmul(out, hi_l, lo_r, start=False, stop=False, skip_group_check=True)
        return nc.tensor.matmul(out, lo_l, hi_r, start=False, stop=stop, skip_group_check=True)

    def unit_mm(pe, nb, slot, bank, rhs_ready=None, before=0):
        pe.wait_ge(lo_ready, nb + 1)
        wh, wl = part(w_hi, slot, False), part(w_lo, slot, False)
        for k in range(KT):
            if rhs_ready is not None:
                pe.wait_ge(rhs_ready, before + k + 1)
            mm = mm3(psum[:, bank, 0:TOK], wh[:, k, :], wl[:, k, :], act_hi[:, k, :], act_lo[:, k, :], k == 0, k == KT - 1)
        mm.then_inc(half_used, 1)

    def ada_mm(pe, nb, slot, bank, hh):
        pe.wait_ge(lo_ready, nb + 1)
        wh, wl = part(w_hi, slot, False), part(w_lo, slot, False)
        out = psum[0:18, bank, 128 * hh:128 * hh + 128]
        for k in range(KT):
            nc.tensor.matmul(out, c_hl[:, k, :], wh[:, k, :], start=(k == 0), stop=False, skip_group_check=True)
            mm = nc.tensor.matmul(out, c_hl[:, k, :], wl[:, k, :], start=False, stop=(k == KT - 1), skip_group_check=True)
        mm.then_inc(half_used, 1)

    def ada_turn(pe, a, bank, slot):
        pe.wait_ge(ada_row, a + 1)
        pe.sem_inc(pe_past, 1)
        for hh in range(2):
            mm = nc.tensor.transpose(psum[:, bank, 256 + 18 * hh:256 + 18 * hh + 18],
                                     rowbuf[:, slot, 128 * hh:128 * hh + 128], cst[0:18, 0:18])
        mm.then_inc(ada_turned, 1)

    def kv_pieces():
        return [(0, 128, 0), (1, 128, 160), (2, 128, 288), (5, 64, 448), (3, 128, 544), (4, 128, 672)]

    @block.tensor
    def _(pe):
        pe.wait_ge(const_in, 16)
        pe.wait_ge(c_in, 32)
        for k in range(KT):
            mm = nc.tensor.transpose(psum[:, 0, 9 * k:9 * k + 9], ctok[:, 128 * k:128 * k + 128], cst[0:9, 0:9])
        mm.then_inc(turned_c, 1)
        pe.wait_ge(rows_in, 48)
        nc.tensor.transpose(psum[:, 1, 0:64], rows[:, :], cst[0:64, 0:64]).then_inc(turned_rows, 1)
        def turn_x():
            pe.wait_ge(x_in, 32)
            for t in range(2):
                for k in range(KT):
                    mm = nc.tensor.transpose(psum[:, 1 + 2 * t + k // 4, 128 * (k % 4):128 * (k % 4) + 128],
                                             x_tok[:, t, 128 * k:128 * k + 128], ident)
                    if k % 4 == 3:
                        mm.then_inc(turned_x, 1)
            for k in range(KT):
                mm = nc.tensor.transpose(psum[:, 0, SAMPLE * k:SAMPLE * k + SAMPLE],
                                         x_tok[0:SAMPLE, 2, 128 * k:128 * k + 128], cst[0:SAMPLE, 0:SAMPLE])
            mm.then_inc(turned_x, 1)

        pe.wait_ge(c_ready, 1)
        for a in range(N_ADA0):
            if a >= 3:
                pe.wait_ge(ada_mod, a - 2)
            for hh in range(2):
                ada_mm(pe, 2 * a + hh, (2 * a + hh) % SPLIT, 5 + a % 3, hh)
            if a >= 1:
                ada_turn(pe, a - 1, 5 + (a - 1) % 3, (a - 1) % 3)
            if a == 2:
                pe.wait_ge(rows_ready, 1)
                turn_x()
        ada_turn(pe, N_ADA0 - 1, 5 + (N_ADA0 - 1) % 3, (N_ADA0 - 1) % 3)

        def mix(i, first=False):
            for k in range(6):
                nb0 = i * 12 + 2 * (MIX0 + k)
                for hh in range(2):
                    slot = (2 * k + hh) % SPLIT
                    if k % 2 == 0:
                        u = i * 6 + (k + hh)
                        if not (first and k == 0):
                            pe.wait_ge(acc_free[hh], i * 3 + k // 2)
                        unit_mm(pe, nb0 + hh, slot, hh, h_lo if first and k == 0 and hh == 0 else None)
                    else:
                        a = i * 3 + (N_ADA0 + k // 2)
                        bank = (N_ADA0 + k // 2) % 3
                        if hh == 0:
                            pe.wait_ge(ada_mod, a - 2)
                        ada_mm(pe, nb0 + hh, slot, 5 + bank, hh)
                if k % 2 == 0 and not (first and k == 0):
                    ada_turn(pe, i * 3 + (N_ADA0 + k // 2 - 1), 5 + (N_ADA0 + k // 2 - 1) % 3, (N_ADA0 + k // 2 - 1) % 3)

        mix(0, True)
        with pe.Fori(1, MIX_TRIPS) as i:
            mix(i)

        for j in range(8):
            g, hp = j // 2, j % 2
            if j == 1:
                pe.wait_ge(acc_free[0], 12)
                pe.wait_ge(acc_free[1], 12)
            for kind in range(2):
                bank = 2 * (1 - j % 2) + kind
                if kind == 0:
                    pe.wait_ge(acc_free[hp], v_blk(g, hp) // 2 + 1)
                    if j >= 2:
                        pe.wait_ge(v_tok, j - 1)
                else:
                    pe.wait_ge(roped, k_blk(g, hp) + 1 if g < 3 else 15 + hp)
                    if j >= 2:
                        pe.wait_ge(k_tok, j - 1)
                blk = (v_blk if kind == 0 else k_blk)(g, hp)
                for t in range(2):
                    nc.tensor.transpose(psum[:, bank, 128 * t:128 * t + 128], qkvg[:, blk, 128 * t:128 * t + 128], ident)
                nc.tensor.transpose(psum[0:SAMPLE, bank, 256:384], qkvg[:, blk, PROMPT:TOK], ident).then_inc(tok_turned, 1)
            if j == 1:
                ada_turn(pe, N_ADA0 + 11, 5 + (N_ADA0 + 11) % 3, (N_ADA0 + 11) % 3)
        pe.wait_ge(ada_mod, N_ADA0 + 12)

        pe.wait_ge(v_tok, 8)
        pe.wait_ge(k_tok, 8)

        def keys_turn(idx):
            b, hp = idx // 2, idx % 2
            if hp == 0:
                place, before = kv_place(b, 0)
                pe.wait_ge(kv_in[place], 16 * KV_LOADS * (before + 1))
            if idx >= 2:
                pe.wait_ge(kt_x, idx - 1)
                pe.wait_ge(kt_y, idx - 1)
            for n, (tile, nr, _) in enumerate(kv_pieces()):
                bank = 4 + 2 * hp + (n >= 3)
                col = 128 * n if n < 3 else (0, 64, 192)[n - 3]
                mm = nc.tensor.transpose(psum[:, bank, col:col + nr], kv_tile(b, 0)[0:nr, tile, 128 * hp:128 * hp + 128],
                                         cst[0:nr, 0:nr])
            mm.then_inc(kt_turned, 1)

        def sample_scores(idx):
            b, hp = idx // 2, idx % 2
            pe.wait_ge(kt_x, idx + 1)
            pe.wait_ge(kt_y, idx + 1)
            r0, half = 32 * (b % 4), b // 4
            if idx == 0:
                pe.wait_ge(qz_ready, 1)
                pe.wait_ge(new_keys, 8)
            for g, (c0, n, bank, o0) in enumerate(((0, 160, 2, 0), (160, 288, 2, 160), (448, 96, 3, 0), (544, 288, 3, 96))):
                w = qz[:, g, hp, b % 4, 16 * half:16 * half + 32]
                mm = nc.tensor.matmul(psum[r0:r0 + 32, bank, o0:o0 + n], w, kT[:, hp, c0:c0 + n],
                                      start=(half == 0 and hp == 0 and g in (0, 2)), stop=(half == 1 and hp == 1),
                                      skip_group_check=True)
            mm.then_inc(scored_s, 1)

        for idx in range(2 * DEC_B + 1):
            if idx < 2 * DEC_B:
                keys_turn(idx)
            if idx >= 1:
                sample_scores(idx - 1)

        def sample_probs_turn():
            pe.wait_ge(prob_s, 2)
            for n, (c0, nc_) in enumerate(S_PIECES):
                mm = nc.tensor.transpose(psum[0:nc_, 4 + n // 4, 128 * (n % 4):128 * (n % 4) + 128],
                                         s_prb[:, c0:c0 + nc_], ident)
                if n in (3, 7, 9):
                    mm.then_inc(probT_turned, 1)

        def sample_values(b):
            q, half = b % 4, b // 4
            if q == 0:
                if half == 1:
                    pe.wait_ge(masked_s, 1)
                for g in range(4):
                    nc.tensor.matmul(psum[:, 7, 256 * (g // 3):256 * (g // 3) + 256], s_prbT[0:SAMPLE, 6 + g, :],
                                     tok[0:SAMPLE, 2, 1, 256 * g:256 * g + 256], start=(g == 0), stop=False,
                                     skip_group_check=True)
            place, before = kv_place(b, 1)
            pe.wait_ge(kv_in[place], 16 * KV_LOADS * (before + 1))
            for n, (tile, nr, br) in enumerate(((0, 128, 0), (1, 128, 0), (2, 128, 0), (5, 64, 0), (3, 128, 1), (4, 128, 1))):
                mm = nc.tensor.matmul(psum[32 * q:32 * q + 32, 7, 256 * br:256 * br + 256],
                                      s_prbT[0:nr, n, 32 * q:32 * q + 32], kv_tile(b, 1)[0:nr, tile, :],
                                      start=False, stop=(q == 3), skip_group_check=True)
            mm.then_inc(pv_s, 1)

        def prompt_scores(u):
            br, t, heads = UNITS[u]
            if u >= 1:
                pe.wait_ge(maxed, rows_before(u))
            nk = 128 * (t + 1)
            for i, h in enumerate(heads):
                p0, c0 = E * (h % 2), 512 * i
                for g in ((0, 1, 2) if br == 0 else (3,)):
                    mm = nc.tensor.matmul(psum[:, 2 + c0 // 512, c0 % 512:c0 % 512 + nk],
                                          qkvg[p0:p0 + E, q_blk(g, h // 2), 128 * t:128 * t + 128],
                                          qkvg[p0:p0 + E, k_blk(g, h // 2), 0:nk], start=True, stop=True,
                                          skip_group_check=True)
                    c0 += nk
            mm.then_inc(scored, 1)

        def prompt_turn(u):
            pe.wait_ge(exped, rows_before(u + 1))
            if u == 0:
                pe.wait_ge(probT_s, 2)
            else:
                pe.wait_ge(prbT_a, u)
                pe.wait_ge(prbT_b, min(u, 4))
            for n in range(cols_of(u) // 128):
                mm = nc.tensor.transpose(psum[:, 4 + n // 4, 128 * (n % 4):128 * (n % 4) + 128],
                                         prb[:, u % 2, 128 * n:128 * n + 128], ident)
            mm.then_inc(turned, 1)

        def prompt_values(u):
            br, t, heads = UNITS[u]
            pe.wait_ge(prbT_a, u + 1)
            pe.wait_ge(prbT_b, min(u + 1, 4))
            if u >= 1:
                pe.wait_ge(o_ready, u)
            groups, n = (0, 1, 2) if br == 0 else (3,), 0
            for i, h in enumerate(heads):
                for g in groups:
                    for kb in range(t + 1):
                        mm = nc.tensor.matmul(psum[:, 6, E * i:E * i + E], prbT[:, u % 2, 128 * n:128 * n + 128],
                                              tok[:, kb, 1, 256 * g + E * h:256 * g + E * h + E],
                                              start=(g == groups[0] and kb == 0), stop=(g == groups[-1] and kb == t),
                                              skip_group_check=True)
                        n += 1
            mm.then_inc(pv_done, 1)

        def outputs_turn(br):
            for f in range(2):
                for t in range(2):
                    mm = nc.tensor.transpose(psum[:, 3 - br, 256 * f + 128 * t:256 * f + 128 * t + 128],
                                             o_tokens[:, t, br, 128 * f:128 * f + 128], ident)
            mm.then_inc(oT_turned, 1)

        for s in range(16):
            u = 24 + s
            pe.wait_ge(acc_free[s % 2], u // 2)
            unit_mm(pe, 2 * GATE0 + s, s % SPLIT, s % 2)
            if s == 2:
                sample_probs_turn()
            if 2 <= s < N_UNITS + 2:
                prompt_scores(s - 2)
            if 3 <= s < N_UNITS + 3:
                prompt_turn(s - 3)
            if 4 <= s < N_UNITS + 4:
                prompt_values(s - 4)
            if 5 <= s < 9:
                sample_values(s - 5)
            if 10 <= s < 14:
                sample_values(s - 6)
            if s == 14:
                pe.wait_ge(o_ready, 8)
                pe.wait_ge(maxed, 16)
                outputs_turn(0)
        pe.wait_ge(masked_s, 2)
        for f in range(4):
            for half in range(2):
                mm = nc.tensor.matmul(psum[:, 7, SAMPLE * f:SAMPLE * f + SAMPLE], o_masked[:, half, 128 * f:128 * f + 128],
                                      cst[:, C_SEL:C_SEL + SAMPLE], start=(f == 0 and half == 0), stop=(half == 1),
                                      skip_group_check=True)
        mm.then_inc(sel_done, 1)

        def ada_static(a, chunk, bank):
            for hh in range(2):
                nb = 2 * chunk + hh
                ada_mm(pe, nb, nb % SPLIT, bank, hh)

        ada_static(20, ADA1, 5)
        pe.wait_ge(o_ready, N_UNITS)
        outputs_turn(1)
        ada_static(21, ADA1 + 1, 4)
        ada_turn(pe, 20, 5, 20 % 3)

        for h in range(4):
            nb = 2 * PAB0 + h
            pe.wait_ge(lo_ready, nb + 1)
            if h == 0:
                pe.wait_ge(oT_l, 2)
            if h == 1:
                pe.wait_ge(oT_l, 3)
            wh, wl = w_hi[:, nb % SPLIT, :], w_lo[:, nb % SPLIT, :]
            for m in range(4):
                n = 4 * h + m
                if n < 2:
                    pe.wait_ge(acc_free[n], 20)
                if n >= 4:
                    pe.wait_ge(gated_ready, n - 3)
                for k in range(2):
                    c = 512 * k + 128 * m
                    mm = mm3(psum[:, PAB_BANK[m], 0:TOK], wh[:, c:c + 128], wl[:, c:c + 128],
                             oT_hi[:, 2 * (h % 2) + k, :], oT_lo[:, 2 * (h % 2) + k, :], k == 0, k == 1)
                mm.then_inc(half_used if m == 3 else pab_done, 1)
            if h == 0:
                ada_turn(pe, 21, 4, 21 % 3)

        def ones_mm(bank, src, m, first, last):
            return nc.tensor.matmul(psum[:, bank, 0:TOK], ones, src[:, m, :], start=first, stop=last)

        def sums(n):
            m = SUM_ORDER[n]
            pe.wait_ge(squared, n + 1)
            ones_mm(3, xT, m, n == 0, n == KT - 1)
            mm = ones_mm(6, qkvg[:, 8:16, :], m, n == 0, n == KT - 1)
            if n == KT - 1:
                mm.then_inc(sums_done, 1)

        for m in range(KT):
            pe.wait_ge(*((gated_ready, 13 + m) if m < 2 else (z_ready, m - 1)))
            unit_mm(pe, 2 * WO0 + m, (2 * WO0 + m) % SPLIT, m % 2, merged_lo if m == 0 else None)
            if m == SHIFT_BLOCKS:
                for k in range(SHIFT_BLOCKS):
                    pe.wait_ge(z_ready, k + 1)
                    mm = ones_mm(2, xT, k, k == 0, k == SHIFT_BLOCKS - 1)
                mm.then_inc(shift_done, 1)
            for n in SUMS_AFTER.get(m, ()):
                sums(n)
        sums(6)
        ada_mm(pe, 2 * ADA2, (2 * ADA2) % SPLIT, 7, 0)
        sums(7)
        ada_mm(pe, 2 * ADA2 + 1, (2 * ADA2 + 1) % SPLIT, 7, 1)
        pe.wait_ge(ada_mod, 22)
        ada_static(23, ADA2 + 1, 5)
        ada_turn(pe, 22, 7, 22 % 3)
        ada_turn(pe, 23, 5, 23 % 3)

        def up_pair(j, first=False):
            for q in range(4):
                nb = j * 4 + (2 * UP0 + q)
                if q < 2 and first:
                    pe.wait_ge(z_ready, KT)
                elif q < 2:
                    pe.wait_ge(f_ready, j * 2 + (q - 1))
                else:
                    pe.wait_ge(silu_ready, j * 2 + (q - 1))
                if first and q == 0:
                    pe.wait_ge(h2_lo, 1)
                unit_mm(pe, nb, q, q % 2, h2_lo if first and q == 0 else None, 1)

        up_pair(0, True)
        up_pair(1)
        up_pair(2)
        with pe.Fori(1, UP_TRIPS) as i:
            for k in range(UP_PAIRS):
                up_pair(i * 3 + k)
        for j in range(UP_PAIRS * UP_TRIPS, PAIRS):
            up_pair(j)

        def z2_turn(m):
            if m == 4:
                pe.wait_ge(z2_kept, 3)
            pe.wait_ge(z2_ready, max(m + 1, 4))
            for t in range(3):
                nt = 128 if t < 2 else SAMPLE
                bank, c = (t, 128 * (m % 4)) if m < 6 else (3 + t, 128 * (m - 6))
                nc.tensor.transpose(psum[0:nt, bank, c:c + 128],
                                    xT[:, m, 128 * t:128 * t + nt], ident).then_inc(z2_turned, 1)

        def down_mm(hcol, kk, m):
            nb = 2 * DOWN0 + 11 * hcol + kk // 2
            wh, wl = w_hi[:, nb % SPLIT, :], w_lo[:, nb % SPLIT, :]
            for k in range(2):
                c = 512 * k + 128 * m
                mm = mm3(psum[:, 4 * hcol + m, 0:TOK], wh[:, c:c + 128], wl[:, c:c + 128],
                         f_hi[:, kk + k, :], f_lo[:, kk + k, :], kk + k == 0, kk + k == FT - 1)
            if m == 3:
                mm.then_inc(half_used, 1)
            elif kk == FT - 2:
                mm.then_inc(down_done, 1)

        for hcol in range(2):
            for kk in range(0, FT if hcol == 0 else FT - 6, 2):
                pe.wait_ge(lo_ready, 2 * DOWN0 + 11 * hcol + kk // 2 + 1)
                if hcol == 0:
                    pe.wait_ge(f_lo_ready, kk + 2)
                if hcol == 0 and kk == 0:
                    pe.wait_ge(f_ready, 2 * PAIRS)
                if hcol == 1 and kk == 0:
                    pe.wait_ge(ada_mod, 24)
                for m in range(4):
                    down_mm(hcol, kk, m)
                if hcol == 1 and kk == 4:
                    for m in range(4):
                        z2_turn(m)
        pe.wait_ge(lo_ready, 2 * DOWN0 + 22)
        for m in range(4):
            for kk in range(FT - 6, FT, 2):
                down_mm(1, kk, m)
            if m >= 1:
                z2_turn(4 + m - 1)
        z2_turn(7)

    @block.scalar
    def _(act):
        act.wait_ge(turned_c, 1)
        nc.scalar.activation(c_t[:], psum[:, 0, 0:72].rearrange("p (k c) -> p k c", c=9), ACT.Silu).then_inc(c_silu, 1)
        act.wait_ge(c_silu, 1)
        nc.scalar.activation(c_hl[:, :, 0:9], c_t[:], ACT.Copy).then_inc(c_hi, 1)
        for nb in range(AHEAD):
            hi_static(act, nb)

        def ada_rows(a, bank, slot, used):
            act.wait_ge(half_used, used)
            nc.scalar.activation(rowbuf[:, slot, :], psum[0:18, bank, 0:256], ACT.Copy).then_inc(ada_row, 1)

        for a in range(N_ADA0):
            if a < N_ADA0 - 2:
                hi_static(act, 2 * a + AHEAD)
            elif a == N_ADA0 - 1:
                hi_static(act, 2 * MIX0)
            ada_rows(a, 5 + a % 3, a % 3, 2 * a + 2)
            if a < N_ADA0 - 2:
                hi_static(act, 2 * a + 1 + AHEAD)
            if a == 3:
                for j in range(2):
                    act.wait_ge(turned_x, j + 1)
                    nc.scalar.activation(xT[:, 4 * j:4 * j + 4, 0:128], psum[:, 1 + j, :].rearrange("p (k c) -> p k c", c=128),
                                         ACT.Copy).then_inc(x_ready_act, 1)
        hi_static(act, 2 * MIX0 + 1)
        for k in range(KT):
            if k == 5:
                hi_static(act, 2 * MIX0 + 2)
            act.wait_ge(h_ready, k + 1)
            nc.scalar.activation(act_hi[:, k, :], qkvg[:, k, :], ACT.Copy).then_inc(h_hi, 1)
        hi_static(act, 2 * MIX0 + 3)

        def mix(i, kinds, last=False):
            for k in range(6):
                nb0 = i * 12 + 2 * (MIX0 + k)
                for hh in range(2):
                    nb = nb0 + hh
                    if k % 2 == 0 and kinds[k // 2]:
                        act.wait_ge(half_used, nb + 1)
                        blk = i * 6 + (k + hh)
                        nc.scalar.activation(block_at(qkvg, blk), psum[:, hh, 0:TOK], ACT.Copy).then_inc(evicted, 1)
                    elif k % 2 == 1 and hh == 1:
                        a8 = N_ADA0 + k // 2
                        ada_rows(None, 5 + a8 % 3, a8 % 3, nb + 1)
                    kk = k + 2
                    rslot = (MIX0 + kk) % RAW
                    if not (last and k == 5):
                        split_hi(act, nb + AHEAD, (2 * k + hh) % SPLIT, rslot, hh, (i * 2 + ((MIX0 + kk) // RAW + 1)) * 16)

        with act.Fori(0, 2) as i:
            mix(i, (True, True, True))
        mix(2, (False, False, False))
        mix(3, (True, True, False), True)

        for j in range(8):
            act.wait_ge(tok_turned, 2 * j + 1)
            bank = 2 * (1 - j % 2)
            nc.scalar.activation(tok[:, 0:2, 1, 128 * j:128 * j + 128],
                                 psum[:, bank, 0:256].rearrange("p (t c) -> p t c", t=2), ACT.Copy)
            nc.scalar.activation(tok[0:SAMPLE, 2, 1, 128 * j:128 * j + 128], psum[0:SAMPLE, bank, 256:384],
                                 ACT.Copy).then_inc(v_tok, 1)
        for idx in range(2 * DEC_B):
            b, hp = idx // 2, idx % 2
            act.wait_ge(kt_turned, idx + 1)
            if idx >= 2:
                act.wait_ge(scored_s, idx - 1)
            nc.scalar.activation(kT[:, hp, 0:128], psum[:, 4 + 2 * hp, 0:128], ACT.Copy)
            nc.scalar.activation(kT[:, hp, 160:416], psum[:, 4 + 2 * hp, 128:384], ACT.Copy).then_inc(kt_x, 1)
            if idx in (10, 12):
                hi_static(act, 2 * GATE0 + idx // 2 - 3)
        for br, (c0, c1) in enumerate(((0, 544), (544, 832))):
            act.wait_ge(max_s, br + 1)
            nc.scalar.activation(s_prb[:, c0:c1], s_msk[:, c0:c1], ACT.Exp, bias=small[:, 4 + br:5 + br], scale=SCALE,
                                 accum_out=small[:, 6 + br:7 + br]).then_inc(exp_s, 1)

        def softmax_exp(u):
            if u >= 2:
                act.wait_ge(turned, u - 1)
            if u == 0:
                act.wait_ge(probT_turned, 3)
            for i in range(len(UNITS[u][2])):
                r, n = rows_before(u) + i, keys_of(u)
                act.wait_ge(maxed, r + 1)
                nc.scalar.activation(prb[:, u % 2, i * n:i * n + n], msk[:, i * n:i * n + n], ACT.Exp,
                                     bias=small[:, 16 + r:17 + r], scale=SCALE, accum_out=small[:, 32 + r:33 + r]).then_inc(exped, 1)

        def prbT_copy(u):
            act.wait_ge(turned, u + 1)
            if u >= 2:
                act.wait_ge(pv_done, u - 1)
            n = min(512, cols_of(u))
            nc.scalar.activation(prbT[:, u % 2, 0:n], psum[:, 4, 0:n], ACT.Copy).then_inc(prbT_a, 1)

        def sigmoids(c0, c1):
            nc.scalar.activation(qkvg[:, c0:c1, :], qkvg[:, c0:c1, :], ACT.Sigmoid).then_inc(gate_ready, 1)

        for s in range(16):
            if s >= 14:
                act.wait_ge(acc_free[s % 2], (24 + s) // 2)
            act.wait_ge(half_used, 2 * GATE0 + s + 1)
            if s == 8:
                act.wait_ge(tok_turned, 16)
            nc.scalar.activation(qkvg[:, gate_slot(s), :], psum[:, s % 2, 0:TOK], ACT.Copy).then_inc(acc_free[s % 2], 1)
            hi_static(act, 2 * GATE0 + s + AHEAD)
            if s == 2:
                for n0, n1, rows_n, turned_n in ((0, 3, 128, 1), (3, 4, 64, 1), (4, 6, 128, 2), (6, 8, SAMPLE, 2), (8, 10, SAMPLE, 3)):
                    act.wait_ge(probT_turned, turned_n)
                    c0 = 128 * (n0 % 4)
                    src = psum[0:rows_n, 4 + n0 // 4, c0:c0 + 128 * (n1 - n0)].rearrange("p (k c) -> p k c", c=128)
                    ins = nc.scalar.activation(s_prbT[0:rows_n, n0:n1, :], src, ACT.Copy)
                    if n1 in (8, 10):
                        ins.then_inc(probT_s, 1)
            if 2 <= s < N_UNITS + 2:
                softmax_exp(s - 2)
            if 3 <= s < N_UNITS + 3:
                prbT_copy(s - 3)
            if s == 14:
                sigmoids(24, 28)
            if s == 15:
                sigmoids(28, 32)

        def oT_leading(br):
            act.wait_ge(oT_turned, br + 1)
            nc.scalar.activation(oT_hi[:, 2 * br:2 * br + 2, 0:PROMPT], psum[:, 3 - br, :].rearrange("p (k c) -> p k c", c=PROMPT),
                                 ACT.Copy).then_inc(oT_h, 1)

        oT_leading(0)
        act.wait_ge(sel_done, 1)
        nc.scalar.activation(oT_hi[:, :, PROMPT:TOK], psum[:, 7, 0:4 * SAMPLE].rearrange("p (k c) -> p k c", c=SAMPLE),
                             ACT.Copy).then_inc(oT_h, 1)
        hi_static(act, 2 * ADA1 + AHEAD)
        ada_rows(20, 5, 20 % 3, 2 * ADA1 + 2)
        oT_leading(1)
        act.wait_ge(acc_free[0], 20)
        act.wait_ge(acc_free[1], 20)
        hi_static(act, 2 * ADA1 + 1 + AHEAD)
        hi_static(act, 2 * ADA1 + 2 + AHEAD)
        hi_static(act, 2 * ADA1 + 3 + AHEAD)
        sigmoids(12, 16)
        sigmoids(16, 18)
        sigmoids(22, 24)
        ada_rows(21, 4, 21 % 3, 2 * ADA1 + 4)
        for h in range(4):
            hi_static(act, 2 * PAB0 + h + AHEAD)
            if h % 2 == 1:
                for m in range(2 * h - 2, 2 * h + 2):
                    act.wait_ge(merged, m + 1)
                    nc.scalar.activation(act_hi[:, m, :], qkvg[:, m, :], ACT.Copy).then_inc(merged_hi, 1)

        def square(m, ready, value):
            act.wait_ge(ready, value)
            nc.scalar.activation(qkvg[:, 8 + m, :], xT[:, m, :], ACT.Square).then_inc(squared, 1)

        for m in range(KT):
            hi_static(act, 2 * WO0 + m + AHEAD)
            if m == SHIFT_BLOCKS:
                act.wait_ge(shift_done, 1)
                nc.scalar.activation(shift[:], psum[:, 2, 0:TOK], ACT.Copy, scale=float(KT // SHIFT_BLOCKS)).then_inc(shift_ready, 1)
            if m == 4:
                square(4, z_ready, 5)
                square(0, shifted, 5)
            if m == 5:
                square(1, shifted, 6)
                square(2, shifted, 7)
                square(3, shifted, 8)
                square(5, z_ready, 6)
            if m >= 6:
                square(m, z_ready, m + 1)
        hi_static(act, 2 * ADA2 + AHEAD)
        nc.scalar.activation(small[:, 70:71], cst[:, C_EPS:C_EPS + 1], ACT.Sqrt)
        act.wait_ge(sums_done, 1)
        nc.scalar.activation(off_mean[:], psum[:, 3, 0:TOK], ACT.Copy).then_inc(off_ready, 1)
        nc.scalar.activation(off_sq[:], psum[:, 3, 0:TOK], ACT.Square).then_inc(off_ready, 1)
        act.wait_ge(var_ready, 1)
        nc.scalar.activation(rstd[:], off_sq[:], ACT.Sqrt, bias=cst[:, C_EPS:C_EPS + 1]).then_inc(std_ready, 1)
        hi_static(act, 2 * ADA2 + 1 + AHEAD)
        ada_rows(22, 7, 22 % 3, 2 * ADA2 + 2)
        ada_rows(23, 5, 23 % 3, 2 * ADA2 + 4)
        for m in range(KT):
            act.wait_ge(h2_ready, m + 1)
            nc.scalar.activation(act_hi[:, m, 0:PROMPT], h2_t[:, m, 0:PROMPT], ACT.Identity,
                                 bias=mod[:, 24 + m, 0:1]).then_inc(h2_hi, 1)
            if m == 2:
                act.wait_ge(h2s_ready, 1)
                nc.scalar.activation(act_hi[:, :, PROMPT:TOK], h2_t[:, :, PROMPT:TOK], ACT.Copy).then_inc(h2_hi, 1)
        hi_static(act, 2 * ADA2 + 2 + AHEAD)
        hi_static(act, 2 * ADA2 + 3 + AHEAD)

        def up_pair(j, k, i):
            for q in range(4):
                nb = j * 4 + (2 * UP0 + q)
                if q < 2:
                    act.wait_ge(half_used, nb + 1)
                    if not isinstance(j, int) or j >= 1:
                        act.wait_ge(f_ready, j * 2 + (q - 1))
                    nc.scalar.activation(silu_t[:, q, :], psum[:, q, 0:TOK], ACT.Silu).then_inc(silu_ready, 1)
                if isinstance(j, int):
                    hi_static(act, nb + AHEAD)
                else:
                    n2 = UP0 + 2 * k + 2 + q // 2
                    split_hi(act, nb + AHEAD, q, n2 % RAW, q % 2, (i * 2 + raw_need(n2, n2 % RAW) // 16) * 16)
                if q >= 2:
                    fi = j * 2 + (q - 2)
                    act.wait_ge(f_ready, fi + 1)
                    nc.scalar.activation(block_at(f_hi, fi), f_t[:, q - 2, :], ACT.Copy).then_inc(f_hi_ready, 1)

        for j in range(3):
            up_pair(j, j, 0)
            if j == 1:
                act.wait_ge(x1_scaled, 1)
                for m in range(KT):
                    nc.scalar.activation(xT[:, m, :], xT[:, m, :], ACT.Identity, bias=lnp[:, 72 + m:73 + m],
                                         scale=lnp[:, 64 + m:65 + m]).then_inc(x1_ready, 1)
        with act.Fori(1, UP_TRIPS) as i:
            for k in range(UP_PAIRS):
                up_pair(i * 3 + k, k, i)
        for j in range(UP_PAIRS * UP_TRIPS, PAIRS):
            up_pair(j, 0, 0)
        for nb in range(2 * DOWN0, LAST + 1):
            hi_static(act, nb + AHEAD)
        act.wait_ge(ln_rows_in, 32)
        for t in range(3):
            nt = 128 if t < 2 else SAMPLE
            act.wait_ge(z2_turned, 10 + t)
            nc.scalar.activation(y_tok[0:nt, t, 0:512], psum[0:nt, t, :], ACT.Copy).then_inc(z2_kept, 1)
        nc.scalar.activation(small[:, 70:71], cst[:, C_EPS:C_EPS + 1], ACT.Sqrt)
        for t in range(3):
            nt = 128 if t < 2 else SAMPLE
            act.wait_ge(var2, t + 1)
            nc.scalar.activation(small[0:nt, 60 + t:61 + t], small[0:nt, 51 + 2 * t:52 + 2 * t], ACT.Sqrt,
                                 bias=cst[0:nt, C_EPS:C_EPS + 1]).then_inc(std2, 1)
        for t in range(2):
            act.wait_ge(rs2, t + 1)
            nc.scalar.activation(y_tok[:, t, 0:512], y_tok[:, t, 0:512], ACT.Identity,
                                 bias=small[:, 66 + t:67 + t], scale=small[:, 63 + t:64 + t]).then_inc(y_norm, 1)

    @block.vector
    def _(dve):
        V = nc.vector

        def link(ins):
            dve_link.up(ins)
            dve.wait_ge(dve_link.sem, dve_link.n)

        dve.wait_ge(c_hi, 1)
        V.tensor_tensor(c_hl[:, :, 9:18], c_t[:], c_hl[:, :, 0:9].bitcast(F32), ALU.subtract).then_inc(c_ready, 1)
        dve.wait_ge(turned_rows, 1)
        V.tensor_copy(lnp[:, 0:64], psum[:, 1, 0:64]).then_inc(rows_ready, 1)
        for nb in range(AHEAD):
            lo_static(dve, nb)
        dve.wait_ge(rows_ready, 1)
        link(V.tensor_scalar(lnp[:, 64:80], lnp[:, 48:64], ALPHA, None, ALU.mult))
        for c in (8, 32):
            link(V.tensor_scalar_add(lnp[:, c:c + 8], lnp[:, c:c + 8], 1.0))

        def ada_add(a, bank):
            dve.wait_ge(ada_turned, a + 1)
            dst = mod[:, 2 * a:2 * a + 2, :] if isinstance(a, int) else mod[:, bass.ds(a * 2, 2), :]
            src = psum[:, bank, 256:292].rearrange("p (k h c) -> p k c h", k=2, h=2)
            V.tensor_reduce(dst, src, mybir.AxisListType.X, ALU.add).then_inc(ada_mod, 1)

        def add_bias(b0, b1, a_done):
            dve.wait_ge(ada_mod, a_done)
            link(V.tensor_tensor(mod[:, b0:b1, :], mod[:, b0:b1, :],
                                 lnp[:, b0:b1].unsqueeze(2).broadcast_to([128, b1 - b0, 9]), ALU.add))

        def modulate_samples(dst, src, sh, sc):
            by_b = lambda i: mod[:, 8 * i:8 * i + 8, 1:9].unsqueeze(3).broadcast_to([128, KT, DEC_B, DEC_T])
            d4 = dst[:, :, PROMPT:TOK].rearrange("p k (b t) -> p k b t", t=DEC_T)
            s4 = src[:, :, PROMPT:TOK].rearrange("p k (b t) -> p k b t", t=DEC_T)
            link(V.tensor_tensor(d4, s4, by_b(sc), ALU.mult))
            link(V.tensor_tensor(d4, d4, by_b(sh), ALU.add))

        def modulate_prompt(dst, src, m, sh, sc, done):
            V.tensor_scalar(dst[:, m, 0:PROMPT], src[:, m, 0:PROMPT], mod[:, 8 * sc + m, 0:1], mod[:, 8 * sh + m, 0:1],
                            ALU.mult, ALU.add).then_inc(done, 1)

        def rest_of(src, m, leading, done):
            dve.wait_ge(leading, m + 1)
            V.tensor_tensor(act_lo[:, m, :], src[:, m, :], act_hi[:, m, :].bitcast(F32), ALU.subtract).then_inc(done, 1)

        for a in range(N_ADA0):
            if a < N_ADA0 - 2:
                lo_static(dve, 2 * a + AHEAD)
                lo_static(dve, 2 * a + 1 + AHEAD)
            elif a == N_ADA0 - 1:
                lo_static(dve, 2 * MIX0)
            if a >= 1:
                ada_add(a - 1, 5 + (a - 1) % 3)
            if a == 5:
                add_bias(0, 8, 4)
            if a == 3:
                for j in range(2):
                    dve.wait_ge(turned_x, j + 3)
                    V.tensor_copy(xT[:, 4 * j:4 * j + 4, 128:256],
                                  psum[:, 3 + j, :].rearrange("p (k c) -> p k c", c=128)).then_inc(x_ready_dve, 1)
                dve.wait_ge(turned_x, 5)
                V.tensor_copy(xT[:, :, PROMPT:TOK], psum[:, 0, 0:256].rearrange("p (k c) -> p k c", c=SAMPLE)).then_inc(x_ready_dve, 1)
        ada_add(N_ADA0 - 1, 5 + (N_ADA0 - 1) % 3)
        add_bias(8, 16, 8)
        dve.wait_ge(x_ready_act, 2)
        dve.wait_ge(x_ready_dve, 3)
        modulate_samples(qkvg[:, 0:KT, :], xT[:, :, :], 0, 1)
        for k in range(KT + 1):
            if k < KT:
                modulate_prompt(qkvg, xT, k, 0, 1, h_ready)
            if k >= 1:
                rest_of(qkvg, k - 1, h_hi, h_lo)
            if k in (3, 7):
                lo_static(dve, 2 * MIX0 + 1 + k // 7)
        lo_static(dve, 2 * MIX0 + 3)

        def rope_first(ru, hh, turn):
            dve.wait_ge(evicted, ru + 1)
            dve.sem_inc(dve_past, 1)
            V.stream_shuffle(rope_t[:, hh, :], psum[:, hh, 0:TOK], SWAP).then_inc(acc_free[hh], 1)
            dve.wait_ge(acc_free[hh], turn + 1)
            V.tensor_tensor(rope_t[:, hh, :], rope_t[:, hh, :], cst[:, C_SIN:C_SIN + TOK], ALU.mult).then_inc(sin_done, 1)

        def rope_last(blk, ru, hh):
            dve.wait_ge(sin_done, ru + 1)
            dve.wait_ge(cos_done, ru + 1)
            V.tensor_tensor(block_at(qkvg, blk), block_at(qkvg, blk), rope_t[:, hh, :], ALU.add).then_inc(roped, 1)

        def mix(i, rope_base, kinds, first=False, last=False):
            for k in range(6):
                nb0 = i * 12 + 2 * (MIX0 + k)
                for hh in range(2):
                    if k % 2 == 0 and kinds[k // 2]:
                        rope_first(rope_base + k + hh, hh, i * 3 + k // 2)
                    elif k % 2 == 0:
                        dve.wait_ge(half_used, nb0 + hh + 1)
                        V.tensor_copy(block_at(qkvg, i * 6 + (k + hh)), psum[:, hh, 0:TOK]).then_inc(acc_free[hh], 1)
                    if not (last and k == 5):
                        split_lo(dve, nb0 + hh + AHEAD, (2 * k + hh) % SPLIT, (MIX0 + k + 2) % RAW, hh)
                if k % 2 == 1:
                    if kinds[k // 2]:
                        for hh in range(2):
                            rope_last(i * 6 + (k - 1 + hh), rope_base + k - 1 + hh, hh)
                    if not (first and k == 1):
                        ada_add(i * 3 + (N_ADA0 + k // 2 - 1), 5 + (N_ADA0 + k // 2 - 1) % 3)
                    if kinds[k // 2]:
                        dve.wait_ge(roped, rope_base + k + 1)

        dve.wait_ge(tables_in, 16)
        mix(0, 0, (True, True, True), first=True)
        mix(1, 6, (True, True, True))
        mix(2, 0, (False, False, False))
        mix(3, 12, (True, True, False), last=True)

        for j in range(8):
            dve.wait_ge(tok_turned, 2 * j + 2)
            bank = 3 - 2 * (j % 2)
            V.tensor_copy(tok[:, 0:2, 0, 128 * j:128 * j + 128], psum[:, bank, 0:256].rearrange("p (t c) -> p t c", t=2))
            V.tensor_copy(tok[0:SAMPLE, 2, 0, 128 * j:128 * j + 128], psum[0:SAMPLE, bank, 256:384]).then_inc(k_tok, 1)
            if j == 1:
                ada_add(N_ADA0 + 11, 5 + (N_ADA0 + 11) % 3)
        dve.wait_ge(roped, 16)
        dve.wait_ge(qz_zero, 1)
        for g in range(4):
            for hp in range(2):
                for h2 in range(2):
                    dst = qz[E * h2:E * h2 + E, g, hp, :, :].rearrange("p q (s c) -> p q s c", c=16)
                    dst = dst[:, :, 0:3:2, 8 * hp + 4 * h2:8 * hp + 4 * h2 + 4]
                    src = qkvg[E * h2:E * h2 + E, q_blk(g, hp), PROMPT:TOK].rearrange("p (s q t) -> p q s t", s=2, t=4)
                    ins = V.tensor_copy(dst, src)
        ins.then_inc(qz_ready, 1)
        dve.wait_ge(masks_in, 16)
        for idx in range(2 * DEC_B):
            b, hp = idx // 2, idx % 2
            dve.wait_ge(kt_turned, idx + 1)
            if idx >= 2:
                dve.wait_ge(scored_s, idx - 1)
            V.tensor_copy(kT[:, hp, 448:512], psum[:, 5 + 2 * hp, 0:64])
            V.tensor_copy(kT[:, hp, 544:800], psum[:, 5 + 2 * hp, 64:320]).then_inc(kt_y, 1)
            if idx in (10, 12):
                lo_static(dve, 2 * GATE0 + idx // 2 - 3)
            if idx == 6:
                add_bias(16, 40, N_ADA0 + 12)
                gain, bias = (lnp[:, c:c + 8].unsqueeze(2).broadcast_to([128, 8, 9]) for c in (48, 56))
                link(V.tensor_tensor(mod_t[:, :, :], mod[:, 32:40, :], bias, ALU.mult))
                link(V.tensor_tensor(mod[:, 24:32, :], mod[:, 24:32, :], mod_t[:, :, :], ALU.add))
                link(V.tensor_tensor(mod[:, 32:40, :], mod[:, 32:40, :], gain, ALU.mult))
        dve.wait_ge(scored_s, 2 * DEC_B)
        for j, (c0, c1, bank, o0) in enumerate(((0, 448, 2, 0), (448, 544, 3, 0), (544, 832, 3, 96))):
            ins = V.tensor_tensor_reduce(s_msk[:, c0:c1], psum[:, bank, o0:o0 + c1 - c0], cst[:, C_MS + c0:C_MS + c1],
                                         1.0, -3.0e38, ALU.add, ALU.max, small[:, j:j + 1])
            link(ins)
        link(V.tensor_tensor(small[:, 1:2], small[:, 0:1], small[:, 1:2], ALU.max))
        V.tensor_scalar(small[:, 4:5], small[:, 1:2], -SCALE, None, ALU.mult).then_inc(max_s, 1)
        V.tensor_scalar(small[:, 5:6], small[:, 2:3], -SCALE, None, ALU.mult).then_inc(max_s, 1)

        def softmax_max(u):
            br, t, heads = UNITS[u]
            dve.wait_ge(scored, u + 1)
            if u == 0:
                dve.wait_ge(probT_turned, 3)
            else:
                dve.wait_ge(exped, rows_before(u))
            n, m0 = keys_of(u), ((C_MA0, C_MA1), (C_MB0, C_MB1))[br][t]
            for i in range(len(heads)):
                r = rows_before(u) + i
                src = psum[:, 2:4, :].rearrange("p b c -> p (b c)")[:, 512 * i:512 * i + n]
                link(V.tensor_tensor_reduce(msk[:, i * n:i * n + n], src, cst[:, m0:m0 + n], 1.0, -3.0e38, ALU.add, ALU.max,
                                            small[:, 112 + r:113 + r]))
                V.tensor_scalar(small[:, 16 + r:17 + r], small[:, 112 + r:113 + r], -SCALE, None, ALU.mult).then_inc(maxed, 1)

        def prbT_copy(u):
            n = cols_of(u)
            if n > 512:
                dve.wait_ge(turned, u + 1)
                if u >= 2:
                    dve.wait_ge(pv_done, u - 1)
                V.tensor_copy(prbT[:, u % 2, 512:n], psum[:, 5, 0:n - 512]).then_inc(prbT_b, 1)

        def out_copy(u):
            br, t, heads = UNITS[u]
            r0, r1 = rows_before(u), rows_before(u + 1)
            dve.wait_ge(exped, r1)
            link(V.reciprocal(small[:, 96 + r0:96 + r1], small[:, 32 + r0:32 + r1]))
            dve.wait_ge(pv_done, u + 1)
            for i, h in enumerate(heads):
                ins = V.tensor_scalar(o_tokens[:, t, br, E * h:E * h + E], psum[:, 6, E * i:E * i + E],
                                      small[:, 96 + r0 + i:97 + r0 + i], None, ALU.mult)
            ins.then_inc(o_ready, 1)

        def own_rows(half):
            dve.wait_ge(pv_s, 4 * half + 4)
            if half == 0:
                dve.wait_ge(scored, 8)
            pick = cst[:, C_SELM + 4 * half:C_SELM + 4 * half + 4].unsqueeze(2).broadcast_to([128, 4, E])
            for br in range(2):
                ins = V.tensor_tensor(o_masked[:, half, 256 * br:256 * br + 256].rearrange("p (j e) -> p j e", e=E),
                                      psum[:, 7, 256 * br:256 * br + 256].rearrange("p (j e) -> p j e", e=E), pick, ALU.mult)
            ins.then_inc(masked_s, 1)

        def oT_rest(br):
            dve.wait_ge(oT_h, 1 if br == 0 else 3)
            V.tensor_tensor(oT_lo[:, 2 * br:2 * br + 2, 0:PROMPT], psum[:, 3 - br, :].rearrange("p (k c) -> p k c", c=PROMPT),
                            oT_hi[:, 2 * br:2 * br + 2, 0:PROMPT].bitcast(F32), ALU.subtract).then_inc(oT_l, 1)

        for s in range(16):
            lo_static(dve, 2 * GATE0 + s + AHEAD)
            if s == 1:
                dve.wait_ge(exp_s, 2)
                link(V.reciprocal(small[:, 10:12], small[:, 6:8]))
                for br, (c0, c1) in enumerate(((0, 544), (544, 832))):
                    V.tensor_scalar(s_prb[:, c0:c1], s_prb[:, c0:c1], small[:, 10 + br:11 + br], None, ALU.mult).then_inc(prob_s, 1)
            if 2 <= s < N_UNITS + 2:
                softmax_max(s - 2)
            if 3 <= s < N_UNITS + 3:
                prbT_copy(s - 3)
            if s >= 4:
                out_copy(s - 4)
            if s == 9:
                own_rows(0)
            if s == 14:
                own_rows(1)
        oT_rest(0)
        dve.wait_ge(oT_h, 2)
        V.tensor_tensor(oT_lo[:, :, PROMPT:TOK], psum[:, 7, 0:4 * SAMPLE].rearrange("p (k c) -> p k c", c=SAMPLE),
                        oT_hi[:, :, PROMPT:TOK].bitcast(F32), ALU.subtract).then_inc(oT_l, 1)
        oT_rest(1)
        ada_add(20, 5)
        for nb in range(2 * ADA1, 2 * ADA1 + 4):
            lo_static(dve, nb + AHEAD)

        def merged_rest(m):
            dve.wait_ge(merged_hi, m + 1)
            V.tensor_tensor(act_lo[:, m, :], qkvg[:, m, :], act_hi[:, m, :].bitcast(F32), ALU.subtract).then_inc(merged_lo, 1)

        for h in range(4):
            dve.wait_ge(gate_ready, (1, 3, 3, 5)[h])
            for m in range(4):
                blk = 4 * (h // 2) + m
                if m < 3:
                    dve.wait_ge(pab_done, 3 * h + m + 1)
                else:
                    dve.wait_ge(half_used, 2 * PAB0 + h + 1)
                if h == 3:
                    dve.wait_ge(merged, m + 1)
                gate = qkvg[:, gate_slot(blk + 8 * (h % 2)), :]
                dst = gated[:, m, :] if h % 2 else qkvg[:, blk, :]
                V.tensor_tensor(dst, psum[:, PAB_BANK[m], 0:TOK], gate, ALU.mult).then_inc(gated_ready, 1)
            lo_static(dve, 2 * PAB0 + h + AHEAD)
            if h == 1:
                ada_add(21, 4)
            if h >= 2:
                for m in range(4 * h - 8, 4 * h - 4):
                    merged_rest(m)

        def residual(m, bank, gi, done):
            g3 = mod[:, 8 * gi + m, 1:9].unsqueeze(2).broadcast_to([128, DEC_B, DEC_T])
            t3 = h_t[:, m % 2, 0:SAMPLE].rearrange("p (b t) -> p b t", t=DEC_T)
            p3 = psum[:, bank, PROMPT:TOK].rearrange("p (b t) -> p b t", t=DEC_T)
            link(V.tensor_tensor(t3, p3, g3, ALU.mult))
            link(V.tensor_tensor(xT[:, m, PROMPT:TOK], xT[:, m, PROMPT:TOK], h_t[:, m % 2, 0:SAMPLE], ALU.add))
            V.scalar_tensor_tensor(xT[:, m, 0:PROMPT], psum[:, bank, 0:PROMPT], mod[:, 8 * gi + m, 0:1], xT[:, m, 0:PROMPT],
                                   ALU.mult, ALU.add).then_inc(done, 1)

        dve.wait_ge(x_scaled, 1)
        for m in range(KT):
            dve.wait_ge(half_used, 2 * WO0 + m + 1)
            if m >= 4:
                dve.wait_ge(shifted, m - 3)
            residual(m, m % 2, 2, z_ready)
            lo_static(dve, 2 * WO0 + m + AHEAD)
        lo_static(dve, 2 * ADA2 + AHEAD)
        dve.wait_ge(off_ready, 2)
        V.tensor_tensor(off_sq[:], psum[:, 6, 0:TOK], off_sq[:], ALU.subtract).then_inc(var_ready, 1)
        x4 = xT[:, 0:4, 0:PROMPT]
        dve_link.up(V.tensor_tensor(x4, x4, off_mean[:, 0:PROMPT].unsqueeze(1).broadcast_to([128, 4, PROMPT]), ALU.subtract))
        dve.wait_ge(std_ready, 1)
        V.reciprocal(rstd[:], rstd[:]).then_inc(rstd_ready, 1)
        dve.wait_ge(rstd_ready, 1)
        dve.wait_ge(dve_link.sem, dve_link.n)

        def h2_rest(m):
            dve.wait_ge(h2_hi, m + 1 if m < 3 else m + 2)
            V.scalar_tensor_tensor(act_lo[:, m, 0:PROMPT], h2_t[:, m, 0:PROMPT], mod[:, 24 + m, 0:1], act_hi[:, m, 0:PROMPT].bitcast(F32),
                                   ALU.add, ALU.subtract).then_inc(h2_lo, 1)

        for m in range(KT + 1):
            if m in (4, 6):
                dve.wait_ge(centred, m // 2 - 1)
            if m < KT:
                V.scalar_tensor_tensor(h2_t[:, m, 0:PROMPT], xT[:, m, 0:PROMPT], mod[:, 32 + m, 0:1], rstd[:, 0:PROMPT],
                                       ALU.mult, ALU.mult).then_inc(h2_ready, 1)
            if m == 3:
                dve.wait_ge(h2_hi, 4)
                V.tensor_tensor(act_lo[:, :, PROMPT:TOK], h2_t[:, :, PROMPT:TOK], act_hi[:, :, PROMPT:TOK].bitcast(F32),
                                ALU.subtract).then_inc(h2_lo, 1)
                h2_rest(0)
                h2_rest(1)
            if m >= 3:
                h2_rest(m - 1)
            if m == 4:
                lo_static(dve, 2 * ADA2 + 1 + AHEAD)
        ada_add(22, 7)
        ada_add(23, 5)
        lo_static(dve, 2 * ADA2 + 2 + AHEAD)
        lo_static(dve, 2 * ADA2 + 3 + AHEAD)
        add_bias(40, 48, 24)

        def up_pair(j, k):
            for q in range(4):
                nb = j * 4 + (2 * UP0 + q)
                fi = j * 2 + (q - 2)
                if q >= 2:
                    dve.wait_ge(half_used, nb + 1)
                    dve.wait_ge(silu_ready, fi + 1)
                    if not isinstance(j, int) or j >= 1:
                        dve.wait_ge(f_lo_ready, fi - 1)
                    V.tensor_tensor(f_t[:, q - 2, :], psum[:, q % 2, 0:TOK], silu_t[:, q - 2, :], ALU.mult).then_inc(f_ready, 1)
                if isinstance(j, int):
                    lo_static(dve, nb + AHEAD)
                else:
                    split_lo(dve, nb + AHEAD, q, (UP0 + 2 * k + 2 + q // 2) % RAW, q % 2)
                if q >= 2:
                    dve.wait_ge(f_hi_ready, fi + 1)
                    V.tensor_tensor(block_at(f_lo, fi), f_t[:, q - 2, :], block_at(f_hi, fi).bitcast(F32), ALU.subtract).then_inc(f_lo_ready, 1)

        for j in range(3):
            up_pair(j, j)
        with dve.Fori(1, UP_TRIPS) as i:
            for k in range(UP_PAIRS):
                up_pair(i * 3 + k, k)
        for j in range(UP_PAIRS * UP_TRIPS, PAIRS):
            up_pair(j, 0)

        dve.wait_ge(x1_ready, KT)

        def second(hcol, first=0, last=4):
            for m in range(first, last):
                if m < 3:
                    dve.wait_ge(down_done, 3 * hcol + m + 1)
                else:
                    dve.wait_ge(half_used, 2 * DOWN0 + 11 * hcol + 11)
                residual(4 * hcol + m, 4 * hcol + m, 5, z2_ready)
        for nb in range(2 * DOWN0, 2 * DOWN0 + 11):
            lo_static(dve, nb + AHEAD)
        second(0)
        for nb in range(2 * DOWN0 + 11, LAST + 1):
            lo_static(dve, nb + AHEAD)
        def piece(t, q):
            nt = 128 if t < 2 else SAMPLE
            src = y_tok[0:nt, t, 256 * q:256 * q + 256] if q < 2 else psum[0:nt, t + 3 * (q - 2), 0:256]
            dve_link.up(V.bn_stats(st6[0:nt, t, q, :], src))

        for t in range(3):
            dve.wait_ge(z2_kept, t + 1)
            piece(t, 0)
            piece(t, 1)
        second(1, 0, 3)
        for t in range(3):
            dve.wait_ge(z2_turned, 3 * 5 + t + 1)
            piece(t, 2)
        second(1, 3, 4)

        def inverse_std(t):
            nt = 128 if t < 2 else SAMPLE
            dve.wait_ge(std2, t + 1)
            link(V.reciprocal(small[0:nt, 63 + t:64 + t], small[0:nt, 60 + t:61 + t]))
            if t < 2:
                V.scalar_tensor_tensor(small[:, 66 + t:67 + t], small[:, 50 + 2 * t:51 + 2 * t], -1.0, small[:, 63 + t:64 + t],
                                       ALU.mult, ALU.mult).then_inc(rs2, 1)

        for t in range(3):
            nt = 128 if t < 2 else SAMPLE
            dve.wait_ge(z2_turned, 3 * 7 + t + 1)
            piece(t, 3)
            dve.wait_ge(dve_link.sem, dve_link.n)
            V.bn_aggr(small[0:nt, 50 + 2 * t:52 + 2 * t], st6[0:nt, t, :, :].rearrange("p a b -> p (a b)")).then_inc(var2, 1)
            if t >= 1:
                inverse_std(t - 1)
        dve.wait_ge(ln_rows_in, 32)
        dve.wait_ge(var2, 3)

        def gained(t, own):
            nt = 128 if t < 2 else SAMPLE
            mean = small[0:nt, 50 + 2 * t:51 + 2 * t]
            halves_of_row = lambda v: v[:, 512:D].rearrange("p (a c) -> p a c", a=2)
            V.scalar_tensor_tensor(halves_of_row(y_tok[0:nt, t, :]), psum[0:nt, t:t + 4:3, 0:256], mean,
                                   halves_of_row(ln_rows[0:nt, 0, :]), ALU.subtract, ALU.mult).then_inc(y_scaled, 1)
            if own:
                V.scalar_tensor_tensor(y_tok[0:nt, t, 0:512], y_tok[0:nt, t, 0:512], mean, ln_rows[0:nt, 0, 0:512],
                                       ALU.subtract, ALU.mult).then_inc(y_scaled, 1)

        def biased(t, c0, scaled):
            nt = 128 if t < 2 else SAMPLE
            dve.wait_ge(y_scaled, scaled)
            V.scalar_tensor_tensor(y_tok[0:nt, t, c0:D], y_tok[0:nt, t, c0:D], small[0:nt, 63 + t:64 + t],
                                   ln_rows[0:nt, 1, c0:D], ALU.mult, ALU.add).then_inc(y_done, 1)

        gained(0, False)
        inverse_std(2)
        biased(0, 512, 1)
        gained(1, False)
        gained(2, True)
        biased(1, 512, 2)
        biased(2, 0, 4)

    @block.gpsimd
    def _(pool):
        nc.gpsimd.memset(qz[:], 0.0).then_inc(qz_zero, 1)

        def cos_mult(blk, ru):
            pool.wait_ge(evicted, ru + 1)
            nc.gpsimd.tensor_tensor(block_at(qkvg, blk), block_at(qkvg, blk), cst[:, C_COS:C_COS + TOK], ALU.mult).then_inc(cos_done, 1)

        pool.wait_ge(tables_in, 16)
        with pool.Fori(0, 12) as i:
            cos_mult(i, i)
        for blk in range(18, 22):
            cos_mult(blk, blk - 6)
        pool.wait_ge(roped, 16)
        for g in range(4):
            for hp in range(2):
                nc.gpsimd.tensor_copy(kT[:, hp, NEW_COL[g]:NEW_COL[g] + SAMPLE], qkvg[:, k_blk(g, hp), PROMPT:TOK]).then_inc(new_keys, 1)
        nc.gpsimd.tensor_scalar(xT[:], xT[:], ALPHA, None, ALU.mult).then_inc(x_scaled, 1)
        pool.wait_ge(scored_s, 2 * DEC_B)
        pool.wait_ge(k_tok, 8)
        pool.wait_ge(v_tok, 8)
        for kind in range(2):
            for g in range(4):
                lo = PROMPT - (min(WIN[g], PROMPT) if g < 3 else PROMPT)
                cols = slice(256 * g, 256 * g + 256)
                dst = kv_prompt[g].rearrange("(t p) s c -> p t s c", p=128)
                pool.dma_start(dst[:, :, kind, :], tok[:, lo // 128:2, kind, cols]).then_inc(stored, 16)
        for kind in range(2):
            for g in range(4):
                dst = kv_sample[g][:, (BUF[g] - DEC_T if g < 3 else 0):, 256 * kind:256 * kind + 256]
                src = tok[0:SAMPLE, 2, kind, 256 * g:256 * g + 256]
                pool.dma_start(dst, src).then_inc(stored, 16)
        for m in range(KT):
            pool.wait_ge(gated_ready, 8 * (m // 4) + 4 + m % 4 + 1)
            nc.gpsimd.tensor_tensor(qkvg[:, m, :], qkvg[:, m, :], gated[:, m % 4, :], ALU.add).then_inc(merged, 1)
        pool.wait_ge(shift_ready, 1)
        for m in SHIFT_ORDER:
            if m < 4:
                pool.wait_ge(z_ready, m + 1)
            nc.gpsimd.tensor_tensor(xT[:, m, :], xT[:, m, :], shift[:], ALU.subtract).then_inc(shifted, 1)
        steps = Count(pool_step)

        def step(ins):
            steps.up(ins)
            pool.wait_ge(pool_step, steps.n)

        xs, hs = xT[:, :, PROMPT:TOK], h2_t[:, :, PROMPT:TOK]
        xs4, hs4 = (v.rearrange("p k (b t) -> p k b t", t=DEC_T) for v in (xs, hs))
        by_token = lambda v: v[:, PROMPT:TOK].unsqueeze(1).broadcast_to([128, KT, SAMPLE])
        by_batch = lambda i: mod[:, 8 * i:8 * i + 8, 1:9].unsqueeze(3).broadcast_to([128, KT, DEC_B, DEC_T])
        pool.wait_ge(off_ready, 1)
        nc.gpsimd.tensor_tensor(xs, xs, by_token(off_mean), ALU.subtract).then_inc(centred_s, 1)

        def centre(m):
            x2 = xT[:, m:m + 2, 0:PROMPT]
            nc.gpsimd.tensor_tensor(x2, x2, off_mean[:, 0:PROMPT].unsqueeze(1).broadcast_to([128, 2, PROMPT]),
                                    ALU.subtract).then_inc(centred, 1)

        centre(4)
        pool.wait_ge(centred_s, 1)
        pool.wait_ge(rstd_ready, 1)
        step(nc.gpsimd.tensor_tensor(hs, xs, by_token(rstd), ALU.mult))
        step(nc.gpsimd.tensor_tensor(hs4, hs4, by_batch(4), ALU.mult))
        nc.gpsimd.tensor_tensor(hs4, hs4, by_batch(3), ALU.add).then_inc(h2s_ready, 1)
        centre(6)
        pool.wait_ge(centred, 2)
        pool.wait_ge(h2_ready, KT)
        nc.gpsimd.tensor_tensor(xT[:], xT[:], rstd[:].unsqueeze(1).broadcast_to([128, KT, TOK]), ALU.mult).then_inc(x1_scaled, 1)
        pool.wait_ge(stored, 16 * N_POOL_STORES)
        pool.dma_start(ln_rows[:, 0, :], ln2_g.broadcast_to([128, D])).then_inc(ln_rows_in, 16)
        pool.dma_start(ln_rows[:, 1, :], ln2_b.broadcast_to([128, D])).then_inc(ln_rows_in, 16)
        with pool.Fori(0, DEC_B) as b:
            pool.wait_ge(half_used, b * 5 + 2 * UP0)
            for g in range(3):
                pool.dma_start(kv_sample[g][bass.ds(b, 1), 0:BUF[g] - DEC_T, :],
                               cache_rows[g][bass.ds(b, 1), DEC_T:BUF[g], :]).then_inc(moved, 16)
        pool.wait_ge(ln_rows_in, 32)
        for t in range(2):
            y = y_tok[:, t, 0:512]
            pool.wait_ge(y_norm, t + 1)
            nc.gpsimd.tensor_tensor(y, y, ln_rows[:, 0, 0:512], ALU.mult).then_inc(y_gained, 1)
            pool.wait_ge(y_gained, t + 1)
            nc.gpsimd.tensor_tensor(y, y, ln_rows[:, 1, 0:512], ALU.add).then_inc(y_done_pool, 1)

    ctx.close()


_INS = ["x_prompt", "x_sample", "cache_kv_a0", "cache_kv_a1", "cache_kv_a2", "cache_kv_b", "page_table", "c_prompt", "c_sample",
        "w_ada", "b_ada", "w_in", "w_pa", "w_pb", "w_o", "ln1_g", "ln1_b", "w_up", "w_down", "ln2_g", "ln2_b"]
_OUTS = [(1, PROMPT, D), (DEC_B, DEC_T, D)] + \
        [(1, 1, min(w, PROMPT), 2, 4, E) for w in WIN] + [(1, 1, PROMPT, 2, 4, E)] + \
        [(1, DEC_B, b, 2, 4, E) for b in BUF] + [(1, DEC_B, DEC_T, 2, 4, E)]


def kernel(**inputs):
    import numpy as np
    import concourse.bacc as bacc
    from concourse.bass_utils import run_bass_kernel_spmd

    nc = bacc.Bacc("TRN2", target_bir_lowering=False, num_devices=1)
    arrays, a = {}, {}
    for name in _INS:
        v = np.ascontiguousarray(inputs[name])
        arrays[f"in_{name}"] = v
        a[name] = nc.dram_tensor(f"in_{name}", v.shape, mybir.dt.from_np(v.dtype), kind="ExternalInput").ap()
    arrays["in_const"] = constants()
    const = nc.dram_tensor("in_const", (128, C_END), F32, kind="ExternalInput").ap()
    outs = [nc.dram_tensor(f"out_{i}", shape, F32, kind="ExternalOutput").ap() for i, shape in enumerate(_OUTS)]
    caches = [a[f"cache_kv_a{g}"] for g in range(3)]
    build(nc, a["x_prompt"], a["x_sample"],
          [c.rearrange("a b l k h e -> (a b) l k (h e)") for c in caches],
          [c.rearrange("a b l k h e -> (a b) l (k h e)") for c in caches],
          a["cache_kv_b"].rearrange("a n p k h e -> (a n) p k (h e)"),
          a["page_table"], a["c_prompt"], a["c_sample"], a["w_ada"][0], a["b_ada"], a["w_in"][0], a["w_pa"][0],
          a["w_pb"][0], a["w_o"][0], a["ln1_g"], a["ln1_b"], a["w_up"][0], a["w_down"][0], a["ln2_g"], a["ln2_b"], const,
          outs[0], outs[1],
          [o.rearrange("a b l k h e -> (a b l) k (h e)") for o in outs[2:6]],
          [o.rearrange("a b l k h e -> (a b) l (k h e)") for o in outs[6:10]])
    r = run_bass_kernel_spmd(nc, [arrays], core_ids=[0])
    return tuple(r.results[0][f"out_{i}"] for i in range(len(_OUTS)))
```
